# Optimizing a Trainium2 kernel written in Bass

```python
import jax, jax.numpy as jnp
from jax import lax
import numpy as np

D_MODEL = 2048
BATCH = 1
SEQ = 256
DEPTH = 1

MEM_LEN = 256
MLA_HEADS = 8
MLA_NOPE_DIM = 128
MLA_ROPE_DIM = 64
MLA_QK_DIM = MLA_NOPE_DIM + MLA_ROPE_DIM
MLA_V_DIM = 128
MLA_Q_RANK = 512
MLA_KV_RANK = 256
SB_HEADS = 8
SB_HEAD_DIM = 128
MLA_OUT = MLA_HEADS * MLA_V_DIM
SB_OUT = SB_HEADS * SB_HEAD_DIM
D_MIX = MLA_OUT + SB_OUT
IN_SPLITS = (MLA_Q_RANK,
             MLA_Q_RANK + MLA_KV_RANK,
             MLA_Q_RANK + MLA_KV_RANK + MLA_ROPE_DIM,
             MLA_Q_RANK + MLA_KV_RANK + MLA_ROPE_DIM + SB_OUT,
             MLA_Q_RANK + MLA_KV_RANK + MLA_ROPE_DIM + 2 * SB_OUT)
IN_COLS = MLA_Q_RANK + MLA_KV_RANK + MLA_ROPE_DIM + 3 * SB_OUT
MEM_HEADS = 4
MEM_HEAD_DIM = 128
N_GROUPS = 4
EXPERTS_PER_GROUP = 8
N_EXPERTS = N_GROUPS * EXPERTS_PER_GROUP
TOP_K = 2
D_EXPERT = 512

Q_BLOCK = 128
ROPE_THETA = 10000.0
EPS = 1e-6

kernel_name = "hymba_mla_stickbreaking_hiermoe_block"

def rms_norm(x, g):
    xf = x.astype(jnp.float32)
    y = xf * lax.rsqrt(jnp.mean(xf * xf, axis=-1, keepdims=True) + EPS)
    return (y * g.astype(jnp.float32)).astype(x.dtype)

def rotary_tables(positions):
    inv_freq = ROPE_THETA ** (-jnp.arange(0, MLA_ROPE_DIM, 2, dtype=jnp.float32) / MLA_ROPE_DIM)
    ang = positions.astype(jnp.float32)[..., None] * inv_freq
    return jnp.cos(ang), jnp.sin(ang)

def apply_rope(x, cos, sin):
    x1, x2 = jnp.split(x.astype(jnp.float32), 2, axis=-1)
    return jnp.concatenate([x1 * cos - x2 * sin, x2 * cos + x1 * sin], axis=-1).astype(x.dtype)

def to_blocks(t):
    b, s, h, d = t.shape
    return t.reshape(b, s // Q_BLOCK, Q_BLOCK, h, d).transpose(1, 0, 3, 2, 4)

def from_blocks(o):
    nb, b, h, blk, d = o.shape
    return o.transpose(1, 0, 3, 2, 4).reshape(b, nb * blk, h, d)

def mla_attention(q, k, v):
    s_len = q.shape[1]
    scale = MLA_QK_DIM ** -0.5
    k_pos = jnp.arange(s_len)

    def block(args):
        q_blk, bi = args
        s = jnp.einsum('bhqd,bkhd->bhqk', q_blk, k).astype(jnp.float32) * scale
        q_pos = bi * Q_BLOCK + jnp.arange(Q_BLOCK)
        mask = k_pos[None, :] <= q_pos[:, None]
        p = jax.nn.softmax(jnp.where(mask, s, -jnp.inf), axis=-1).astype(v.dtype)
        return jnp.einsum('bhqk,bkhd->bhqd', p, v)

    o = lax.map(block, (to_blocks(q), jnp.arange(s_len // Q_BLOCK)))
    return from_blocks(o)

def stick_breaking_attention(q, k, v):
    s_len = q.shape[1]
    scale = SB_HEAD_DIM ** -0.5
    k_pos = jnp.arange(s_len)

    def block(args):
        q_blk, bi = args
        z = jnp.einsum('bhqd,bkhd->bhqk', q_blk, k).astype(jnp.float32) * scale
        q_pos = bi * Q_BLOCK + jnp.arange(Q_BLOCK)
        mask = k_pos[None, :] < q_pos[:, None]
        log_beta = jax.nn.log_sigmoid(z)
        log_1m = jnp.where(mask, jax.nn.log_sigmoid(-z), 0.0)
        later = lax.cumsum(log_1m, axis=3, reverse=True) - log_1m
        a = jnp.where(mask, jnp.exp(log_beta + later), 0.0).astype(v.dtype)
        return jnp.einsum('bhqk,bkhd->bhqd', a, v)

    o = lax.map(block, (to_blocks(q), jnp.arange(s_len // Q_BLOCK)))
    return from_blocks(o)

def memory_cross_attention(h, mem_n, w_q, w_kv, w_o):
    b, s, _ = h.shape
    m = mem_n.shape[1]
    q = (h @ w_q).reshape(b, s, MEM_HEADS, MEM_HEAD_DIM)
    kv = (mem_n @ w_kv).reshape(b, m, 2, MEM_HEADS, MEM_HEAD_DIM)
    k, v = kv[:, :, 0], kv[:, :, 1]
    sc = jnp.einsum('bshd,bmhd->bhsm', q, k).astype(jnp.float32) * (MEM_HEAD_DIM ** -0.5)
    p = jax.nn.softmax(sc, axis=-1).astype(v.dtype)
    o = jnp.einsum('bhsm,bmhd->bshd', p, v).reshape(b, s, MEM_HEADS * MEM_HEAD_DIM)
    return o @ w_o

def hierarchical_moe(h, w_group, b_group, w_expert_router, b_expert, w_gate, w_up, w_down):
    b, s, d = h.shape
    t = h.reshape(b * s, d)
    group_prob = jax.nn.softmax((t @ w_group).astype(jnp.float32) + b_group.astype(jnp.float32), axis=-1)
    p_g, g_idx = lax.top_k(group_prob, 1)
    exp_logits = ((t @ w_expert_router).astype(jnp.float32) + b_expert.astype(jnp.float32)
                  ).reshape(-1, N_GROUPS, EXPERTS_PER_GROUP)
    sel_logits = jnp.einsum('tg,tge->te', jax.nn.one_hot(g_idx[:, 0], N_GROUPS, dtype=jnp.float32), exp_logits)
    p_e, e_idx = lax.top_k(jax.nn.softmax(sel_logits, axis=-1), TOP_K)
    p_e = p_e / jnp.sum(p_e, axis=-1, keepdims=True)
    gates = p_g * p_e
    expert_id = g_idx * EXPERTS_PER_GROUP + e_idx
    combine = jnp.einsum('tk,tke->te', gates,
                         jax.nn.one_hot(expert_id, N_EXPERTS, dtype=jnp.float32)).astype(h.dtype)
    a = jnp.einsum('td,edf->tef', t, w_gate)
    u = jnp.einsum('td,edf->tef', t, w_up)
    act = jax.nn.silu(a) * u * combine[:, :, None]
    y = jnp.einsum('tef,efd->td', act, w_down)
    return y.reshape(b, s, d)

def setup_inputs(seed: int = 0) -> dict:
    key = jax.random.key(seed)
    ks = jax.random.split(key, 26)
    f32 = jnp.float32
    L = DEPTH

    def w(k, shape, fan_in):
        return jax.random.normal(k, shape, f32) * (fan_in ** -0.5)

    def gain(k, shape):
        return 1.0 + 0.02 * jax.random.normal(k, shape, f32)

    return {
        "x": jax.random.normal(ks[0], (BATCH, SEQ, D_MODEL), f32),
        "mem": jax.random.normal(ks[1], (BATCH, MEM_LEN, D_MODEL), f32),
        "positions": jnp.broadcast_to(jnp.arange(SEQ, dtype=jnp.int32), (BATCH, SEQ)),
        "norm_mix": gain(ks[2], (L, D_MODEL)),
        "w_in": w(ks[3], (L, D_MODEL, IN_COLS), D_MODEL),
        "norm_q_lat": gain(ks[4], (L, MLA_Q_RANK)),
        "w_q_b": w(ks[5], (L, MLA_Q_RANK, MLA_HEADS * MLA_QK_DIM), MLA_Q_RANK),
        "norm_kv_lat": gain(ks[6], (L, MLA_KV_RANK)),
        "w_kv_b": w(ks[7], (L, MLA_KV_RANK, MLA_HEADS * (MLA_NOPE_DIM + MLA_V_DIM)), MLA_KV_RANK),
        "norm_mla_out": gain(ks[8], (L, MLA_OUT)),
        "norm_sb_out": gain(ks[9], (L, SB_OUT)),
        "w_out": w(ks[10], (L, D_MIX, D_MODEL), D_MIX),
        "norm_mem_x": gain(ks[11], (L, D_MODEL)),
        "norm_mem_src": gain(ks[12], (L, D_MODEL)),
        "w_mem_q": w(ks[13], (L, D_MODEL, MEM_HEADS * MEM_HEAD_DIM), D_MODEL),
        "w_mem_kv": w(ks[14], (L, D_MODEL, 2 * MEM_HEADS * MEM_HEAD_DIM), D_MODEL),
        "w_mem_o": w(ks[15], (L, MEM_HEADS * MEM_HEAD_DIM, D_MODEL), MEM_HEADS * MEM_HEAD_DIM),
        "norm_ffn": gain(ks[16], (L, D_MODEL)),
        "w_group": w(ks[17], (L, D_MODEL, N_GROUPS), D_MODEL),
        "b_group": 0.01 * jax.random.normal(ks[18], (L, N_GROUPS), f32),
        "w_expert_router": w(ks[19], (L, D_MODEL, N_EXPERTS), D_MODEL),
        "b_expert": 0.01 * jax.random.normal(ks[20], (L, N_EXPERTS), f32),
        "w_gate": w(ks[21], (L, N_EXPERTS, D_MODEL, D_EXPERT), D_MODEL),
        "w_up": w(ks[22], (L, N_EXPERTS, D_MODEL, D_EXPERT), D_MODEL),
        "w_down": w(ks[23], (L, N_EXPERTS, D_EXPERT, D_MODEL), D_EXPERT),
        "norm_final": gain(ks[24], (D_MODEL,)),
    }

def reference(x, mem, positions, norm_mix, w_in, norm_q_lat, w_q_b, norm_kv_lat, w_kv_b,
              norm_mla_out, norm_sb_out, w_out, norm_mem_x, norm_mem_src, w_mem_q, w_mem_kv,
              w_mem_o, norm_ffn, w_group, b_group, w_expert_router, b_expert, w_gate, w_up,
              w_down, norm_final):
    b, s, _ = x.shape
    cos, sin = rotary_tables(positions)
    for l in range(DEPTH):
        h = rms_norm(x, norm_mix[l])
        proj = h @ w_in[l]
        c_q, c_kv, k_pe, q_sb, k_sb, v_sb = jnp.split(proj, IN_SPLITS, axis=-1)

        q = (rms_norm(c_q, norm_q_lat[l]) @ w_q_b[l]).reshape(b, s, MLA_HEADS, MLA_QK_DIM)
        q_nope, q_pe = q[..., :MLA_NOPE_DIM], q[..., MLA_NOPE_DIM:]
        kv = (rms_norm(c_kv, norm_kv_lat[l]) @ w_kv_b[l]).reshape(b, s, MLA_HEADS, MLA_NOPE_DIM + MLA_V_DIM)
        k_nope, v_mla = kv[..., :MLA_NOPE_DIM], kv[..., MLA_NOPE_DIM:]
        q_pe = apply_rope(q_pe, cos[:, :, None, :], sin[:, :, None, :])
        k_pe = apply_rope(k_pe, cos, sin)
        q_mla = jnp.concatenate([q_nope, q_pe], axis=-1)
        k_mla = jnp.concatenate(
            [k_nope, jnp.broadcast_to(k_pe[:, :, None, :], (b, s, MLA_HEADS, MLA_ROPE_DIM))], axis=-1)
        o_mla = mla_attention(q_mla, k_mla, v_mla).reshape(b, s, MLA_OUT)

        o_sb = stick_breaking_attention(q_sb.reshape(b, s, SB_HEADS, SB_HEAD_DIM),
                                        k_sb.reshape(b, s, SB_HEADS, SB_HEAD_DIM),
                                        v_sb.reshape(b, s, SB_HEADS, SB_HEAD_DIM)).reshape(b, s, SB_OUT)

        mixed = jnp.concatenate([rms_norm(o_mla, norm_mla_out[l]), rms_norm(o_sb, norm_sb_out[l])], axis=-1)
        x = x + mixed @ w_out[l]

        mem_n = rms_norm(mem, norm_mem_src[l])
        x = x + memory_cross_attention(rms_norm(x, norm_mem_x[l]), mem_n, w_mem_q[l], w_mem_kv[l], w_mem_o[l])

        x = x + hierarchical_moe(rms_norm(x, norm_ffn[l]), w_group[l], b_group[l], w_expert_router[l],
                                 b_expert[l], w_gate[l], w_up[l], w_down[l])
    return rms_norm(x, norm_final)


_drawn_inputs = setup_inputs


def setup_inputs(seed=0):
    import zlib

    import numpy as np

    out = dict(_drawn_inputs(seed))
    spreads = {}
    factors = {'norm_q_lat': 3.866,
     'norm_kv_lat': 2.902,
     'norm_mla_out': 4.56,
     'norm_sb_out': 3.082,
     'norm_mem_x': 8.0,
     'norm_mem_src': 8.0,
     'norm_ffn': 2.733,
     'b_group': 4.755,
     'b_expert': 4.191,
     'norm_final': 2.841}
    for name, (base, spread) in spreads.items():
        noise = np.random.default_rng([zlib.crc32(name.encode()), seed]).standard_normal(out[name].shape)
        drawn = base * np.exp(spread * noise) if base else spread * noise
        out[name] = __import__('jax').numpy.asarray(drawn.astype(out[name].dtype))
    for name, factor in factors.items():
        out[name] = (out[name] * factor).astype(out[name].dtype)
    return out
```

```python
from contextlib import ExitStack

import concourse.bass as bass
from concourse import mybir

F32 = mybir.dt.float32
F32R = mybir.dt.float32r
I32 = mybir.dt.int32
U32 = mybir.dt.uint32
ALU = mybir.AluOpType
ACT = mybir.ActivationFunctionType
AX = mybir.AxisListType.X

P = 128
KB = 256
SEQ, D = 256, 2048
TT = SEQ // P
KD = D // P
Q_RANK, KV_RANK, ROPE = 512, 256, 64
HEADS, HD = 8, 128
MEM_HEADS = 4
GROUPS, PER_GROUP = 4, 8
EXPERTS = GROUPS * PER_GROUP
FE = 512
SLOTS = 32
NJ = P // SLOTS
MAX_PASSES = SEQ // SLOTS
PASS_ROWS = EXPERTS * SLOTS
EPS = 1e-6
SC_MLA = float(HD + ROPE) ** -0.5
SC_SB = float(HD) ** -0.5
BLK = 3 * P
RING = 4
UK = 2
UN = 512

MEM_K, MEM_V, Q_LAT, KV_LAT, SB_Q, SB_K, SB_V = 0, 1, 2, 3, 4, 6, 8
Q_NOPE, Q_PE, K_NOPE, V_MLA, W_OUT, MEM_Q, MEM_O, CHUNKS = 10, 12, 13, 15, 17, 21, 22, 26


def chunk_tiles(c):
    if Q_NOPE <= c <= Q_PE:
        return Q_RANK // P
    if K_NOPE <= c < W_OUT:
        return KV_RANK // P
    return MEM_HEADS if c >= MEM_O else KD


def chunk_cols(c):
    return KV_RANK + ROPE if c == KV_LAT else UN


UNIT0 = [0]
for _c in range(CHUNKS):
    UNIT0.append(UNIT0[-1] + chunk_tiles(_c) // UK)
UNITS = [(c, i) for c in range(CHUNKS) for i in range(chunk_tiles(c) // UK)]

TURNED = [MEM_K, SB_Q, SB_Q + 1, SB_K, SB_K + 1, KV_LAT, Q_NOPE, Q_NOPE + 1, Q_PE, K_NOPE, K_NOPE + 1, MEM_Q]
BY_VECTOR = list(range(W_OUT, MEM_Q)) + list(range(MEM_O, CHUNKS))
SPLITS = [("mem", KD), ("mix", KD), ("q", 4), ("kv", 2), ("out", KD), ("memx", KD), ("memo", MEM_HEADS)]
SPLIT0 = {}
_n = 0
for _name, _k in SPLITS:
    SPLIT0[_name] = _n
    _n += _k
SPLIT_K = dict(SPLITS)


def layer(nc, x, mem, positions, norm_mix, w_in, norm_q_lat, w_q_b, norm_kv_lat, w_kv_b,
          norm_mla_out, norm_sb_out, w_out, norm_mem_x, norm_mem_src, w_mem_q, w_mem_kv,
          w_mem_o, norm_ffn, w_group, b_group, w_expert_router, b_expert, w_gate, w_up,
          w_down, norm_final, out):
    ctx = ExitStack()
    sems = {}

    def S(name):
        if name not in sems:
            sems[name] = ctx.enter_context(nc.semaphore(name))
        return sems[name]

    with ctx:
        base = nc.sbuf_base + (-nc.sbuf_base) % 64
        at = [base]
        limit = nc.sbuf_usable_end

        def place(name, shape, dt=F32, offset=None):
            size = 4
            for s in shape[1:]:
                size *= s
            if offset is None:
                offset = at[0]
                at[0] += size + (-size) % 64
            assert offset + size <= limit, (name, offset + size, limit)
            return nc.alloc_sbuf_tensor_at(name, shape, dt, offset=offset)

        x_res = place("x_res", [P, TT, D])
        a_hi_at = at[0]
        a_hi = place("a_hi", [P, KD, SEQ], F32R)
        a_lo = place("a_lo", [P, KD, SEQ], F32R)
        w_at = at[0]
        w_raw = place("w_raw", [P, RING, UK, UN])
        w_hi = place("w_hi", [P, RING, UK, UN], F32R)
        w_lo = place("w_lo", [P, RING, UK, UN], F32R)
        nat = place("nat", [P, 2, TT, UN])
        km_t = place("km_t", [P, MEM_HEADS, SEQ])
        v_mem = place("v_mem", [P, TT, UN])
        ident = place("ident", [P, P])
        ones = place("ones", [P, P])
        above = place("above", [P, P])
        sb_mask = place("sb_mask", [P, BLK])
        mla_mask = place("mla_mask", [P, BLK])
        before = sb_mask[:, 0:P]
        g_nat = place("g_nat", [70, P])
        g_t = place("g_t", [P, 70])
        g_ffn = place("g_ffn", [P, KD])
        sums = place("sums", [P, 16])
        rstd = place("rstd", [P, 16])
        rope_cs = place("rope_cs", [P, 2, TT, ROPE // 2])
        small = place("small", [P, 64])
        minus_half = place("minus_half", [P, TT])
        iota32 = place("iota32", [P, SLOTS])
        gate_w = place("gate_w", [P, 2, TT])
        rel = place("rel", [P, 2, TT])
        y_idx = place("y_idx", [P, 2, TT, 1], U32)
        y_idx2 = place("y_idx2", [P, 2, TT, 1], U32)
        n_iter = place("n_iter", [P, 1], I32)
        pos_i = place("pos_i", [P, TT], I32)
        e_at = at[0]
        qsb_t = place("qsb_t", [P, HEADS, SEQ])
        ksb_t = place("ksb_t", [P, HEADS, SEQ])
        v_sb = place("v_sb", [P, TT, HEADS * HD])
        q_t = place("q_t", [P, HEADS, SEQ])
        qpe_t = place("qpe_t", [P, HEADS // 2, SEQ])
        k_t = place("k_t", [P, HEADS, SEQ])
        kpe_t = place("kpe_t", [P, SEQ])
        v_mla = place("v_mla", [P, TT, HEADS * HD])
        o_at = at[0]
        o_cat = place("o_cat", [P, TT, D])
        c_q = place("c_q", [P, TT, Q_RANK])
        c_kv = place("c_kv", [P, TT, KV_RANK + ROPE])
        mem_sb = place("mem_sb", [P, TT, D], offset=o_at)
        gu = place("gu", [P, 2, 2, KD // 2, FE], offset=e_at)
        down0 = place("down0", [P, 2, D], offset=e_at + 4 * 16 * 1024)
        down1 = place("down1", [P, 2, D], offset=w_at)
        tmp = at_tmp = a_hi_at
        def scratch(name, shape):
            nonlocal at_tmp
            size = 4
            for s in shape[1:]:
                size *= s
            t = place(name, shape, offset=at_tmp)
            at_tmp += size
            return t
        p_mla = scratch("p_mla", [P, 2, BLK])
        pt_mla = scratch("pt_mla", [P, 2, BLK])
        sb_e = scratch("sb_e", [P, 2, BLK])
        sb_l = scratch("sb_l", [P, 2, BLK])
        sb_b = scratch("sb_b", [P, 2, BLK])
        sb_m = scratch("sb_m", [P, 2, BLK])
        sb_a = scratch("sb_a", [P, 2, BLK])
        row_m = scratch("row_m", [P, HEADS, TT])
        row_n = scratch("row_n", [P, HEADS, TT])
        row_s = scratch("row_s", [P, HEADS, TT])
        row_r = scratch("row_r", [P, HEADS, TT])
        pm = place("pm", [P, 2, TT, SEQ], offset=a_hi_at)
        pmt = place("pmt", [P, 2, TT, SEQ], offset=a_hi_at + 4096)
        mrow = place("mrow", [P, 4, MEM_HEADS, TT], offset=a_hi_at + 8192)
        o_mem = place("o_mem", [P, TT, UN], offset=a_hi_at + 16 * 1024 + 8192)
        h_f = place("h_f", [P, TT, D], offset=w_at + 16 * 1024)
        h_t = place("h_t", [P, KD, SEQ], offset=w_at + 32 * 1024)
        late = w_at + 16 * 1024
        w_r = place("w_r", [P, KD, 36], offset=w_at + 48 * 1024)
        b_r = place("b_r", [P, 36], offset=w_at + 48 * 1024 + 2560)
        rt = place("rt", [P, 1024], offset=w_at + 48 * 1024 + 3072)
        xe = place("xe", [P, KD, SLOTS], offset=late)
        hot = place("hot", [P, TT, SLOTS], F32R, offset=late + 2048)
        hot_f = place("hot_f", [P, 2, TT, SLOTS], offset=late + 2304)
        sg = place("sg", [P, P], offset=late + 3072)
        act = place("act", [P, P], offset=late + 3584)
        act_t = place("act_t", [P, P], offset=late + 4096)
        y_sb = place("y_sb", [P, UN], offset=late + 4608)
        g_fin = place("g_fin", [P, D], offset=late + 8192)
        y_pick = place("y_pick", [P, 2, TT, D], offset=e_at)
        y_dram = nc.dram_tensor("y_slots", [MAX_PASSES * PASS_ROWS, D], F32).ap()

        ps = [ctx.enter_context(nc.psum_tensor(f"ps{i}", [P, 512], F32)) for i in range(8)]

        def unit_src(c, i):
            rows = slice(i * UK * P, (i + 1) * UK * P)
            def cols(w, n0, n=UN):
                return w[0, rows, n0:n0 + n].rearrange("(k p) n -> p k n", p=P)
            def headed(w, width, h0, nh, lo, hi):
                return w[0, rows, h0 * width:(h0 + nh) * width].rearrange(
                    "(k p) (h c) -> p k h c", p=P, c=width)[:, :, :, lo:hi]
            if c < Q_LAT:
                return [cols(w_mem_kv, c * UN)]
            if c < Q_NOPE:
                n0 = {Q_LAT: 0, KV_LAT: Q_RANK}.get(c, Q_RANK + KV_RANK + ROPE + (c - SB_Q) * UN)
                return [cols(w_in, n0, chunk_cols(c))]
            if c < Q_PE:
                return [headed(w_q_b, HD + ROPE, 4 * (c - Q_NOPE), 4, 0, HD)]
            if c == Q_PE:
                return [headed(w_q_b, HD + ROPE, 0, HEADS, HD, HD + ROPE)]
            if c < V_MLA:
                return [headed(w_kv_b, 2 * HD, 4 * (c - K_NOPE), 4, 0, HD)]
            if c < W_OUT:
                return [headed(w_kv_b, 2 * HD, 4 * (c - V_MLA), 4, HD, 2 * HD)]
            if c < MEM_Q:
                return [cols(w_out, (c - W_OUT) * UN)]
            if c == MEM_Q:
                return [cols(w_mem_q, 0)]
            return [cols(w_mem_o, (c - MEM_O) * UN)]

        def chunk_out(c):
            if c in BY_VECTOR:
                return S("chunk_added"), BY_VECTOR.index(c) + 1
            return S("chunk_copied"), sum(1 for d in range(c + 1) if d not in BY_VECTOR)

        def turned_dst(c):
            if c == MEM_K:
                return km_t[:, :, :]
            if c in (SB_Q, SB_Q + 1):
                return qsb_t[:, 4 * (c - SB_Q):4 * (c - SB_Q) + 4, :]
            if c in (SB_K, SB_K + 1):
                return ksb_t[:, 4 * (c - SB_K):4 * (c - SB_K) + 4, :]
            if c in (Q_NOPE, Q_NOPE + 1):
                return q_t[:, 4 * (c - Q_NOPE):4 * (c - Q_NOPE) + 4, :]
            if c == Q_PE:
                return qpe_t[:, :, :]
            if c in (K_NOPE, K_NOPE + 1):
                return k_t[:, 4 * (c - K_NOPE):4 * (c - K_NOPE) + 4, :]
            return qsb_t[:, 0:4, :]

        qm_t = qsb_t
        bank0 = {}
        n = 0
        for c in TURNED:
            bank0[c] = n
            n += 1 if c == KV_LAT else 2

        SS_MEM, SS_X, SS_Q, SS_KV, SS_A, SS_B, SS_X1, SS_X2, = range(0, 16, 2)

        block = ctx.enter_context(nc.Block())

        @block.sync
        def _(sp):
            for u, (c, i) in enumerate(UNITS):
                if u >= RING:
                    sp.wait_ge(S("w_split"), u - RING + 1)
                dst = w_raw[:, u % RING, :, 0:chunk_cols(c)]
                (src,) = unit_src(c, i)
                if len(src.shape) == 4:
                    for k in range(UK):
                        sp.dma_start(dst[:, k, :].rearrange("p (h c) -> p h c", h=src.shape[2]),
                                     src[:, k]).then_inc(S(f"w_loaded{u % RING}"), 16)
                else:
                    sp.dma_start(dst, src).then_inc(S(f"w_loaded{u % RING}"), 16)

            def load_expert(n, e, first=False):
                wg = w_gate[0, e].rearrange("(p k) f -> p (k f)", k=KD)
                wu = w_up[0, e].rearrange("(p k) f -> p (k f)", k=KD)
                wd = w_down[0, e].rearrange("(j p) d -> p j d", p=P)
                half = KD // 2 * FE
                for b in range(2):
                    if not first:
                        sp.wait_ge(S(f"gu_used{b}"), n)
                    sp.dma_start(gu[:, b, 0].rearrange("p k f -> p (k f)"),
                                 wg[:, b * half:(b + 1) * half]).then_inc(S(f"gate_loaded{b}"), 16)
                    sp.dma_start(gu[:, b, 1].rearrange("p k f -> p (k f)"),
                                 wu[:, b * half:(b + 1) * half]).then_inc(S(f"up_loaded{b}"), 16)
                for b, dst in enumerate((down0, down1)):
                    if not first:
                        sp.wait_ge(S(f"down_used{b}"), n)
                    elif b == 1:
                        sp.wait_ge(S("w_used"), len(UNITS))
                    sp.dma_start(dst[:, :, :], wd[:, 2 * b:2 * b + 2, :]).then_inc(
                        S(f"down_loaded{b}"), 16)

            sp.wait_ge(S("mem_turned_q"), 1)
            sp.wait_ge(S("mem_scores"), MEM_HEADS)
            load_expert(0, 0, first=True)
            with sp.Fori(1, EXPERTS) as e:
                load_expert(e, e)
            sp.wait_ge(S("routed"), 1)
            total = sp.value_load(n_iter[0:1, 0:1], min_val=EXPERTS, max_val=MAX_PASSES * EXPERTS)
            with sp.If(total > EXPERTS):
                with sp.Fori(EXPERTS, total, EXPERTS) as n0:
                    with sp.Fori(0, EXPERTS) as e:
                        load_expert(n0 + e, e)
            sp.nop()
            for t in range(TT):
                sp.wait_ge(S("final"), t + 1)
                sp.dma_start(out[0, t * P:(t + 1) * P, :], x_res[:, t, :]).then_inc(S("stored"), 16)
            sp.wait_ge(S("stored"), 16 * TT)

        @block.tensor
        def _(pe):
            def split_stage(name, src):
                k0, kn = SPLIT0[name], SPLIT_K[name]
                for kk in range(kn // 2):
                    b = (k0 // 2 + kk)
                    if b >= 4:
                        pe.wait_ge(S("split_lo"), 2 * (b - 4) + 2)
                        pe.wait_ge(S("split_hi"), 2 * (b - 4) + 2)
                    for i in range(2):
                        for t in range(TT):
                            k = 2 * kk + i
                            mm = pe.transpose(ps[4 + b % 4][:, i * SEQ + t * P:i * SEQ + (t + 1) * P],
                                              src[:, t, k * P:(k + 1) * P], ident[:, :])
                    mm.then_inc(S("split_turned"), 1)

            def project(c, a0=0):
                kn, n = chunk_tiles(c), chunk_cols(c)
                acc = [ps[2 * (c % 2) + t] for t in range(TT)]
                if c >= 2:
                    pe.wait_ge(*chunk_out(c - 2))
                for i in range(kn // UK):
                    u = UNIT0[c] + i
                    pe.wait_ge(S("w_rounded"), u + 1)
                    pe.wait_ge(S("w_split"), u + 1)
                    for j in range(UK):
                        k = i * UK + j
                        for t in range(TT):
                            xh = a_hi[:, a0 + k, t * P:(t + 1) * P]
                            xl = a_lo[:, a0 + k, t * P:(t + 1) * P]
                            wh, wl = w_hi[:, u % RING, j, 0:n], w_lo[:, u % RING, j, 0:n]
                            pe.matmul(acc[t][:, 0:n], xh, wh, start=(k == 0), stop=False)
                            pe.matmul(acc[t][:, 0:n], xh, wl, start=False, stop=False)
                            mm = pe.matmul(acc[t][:, 0:n], xl, wh, start=False, stop=(k == kn - 1))
                    mm.then_inc(S("w_used"), 1)

            def turn(c):
                j = TURNED.index(c)
                if c in (KV_LAT, Q_PE):
                    pe.wait_ge(S("roped"), 1 if c == KV_LAT else 2)
                else:
                    pe.wait_ge(*chunk_out(c))
                for b in range(1 if c == KV_LAT else 2):
                    m = bank0[c] + b
                    bank = ps[4 + m % 4]
                    if m >= 4:
                        pe.wait_ge(S("turn_copied"), m - 3)
                    for i in range(1 if c == KV_LAT else 2):
                        for t in range(TT):
                            f = 2 * b + i
                            mm = pe.transpose(bank[:, i * SEQ + t * P:i * SEQ + (t + 1) * P],
                                              nat[:, j % 2, t, f * P:(f + 1) * P], ident[:, :])
                    mm.then_inc(S("turned"), 1)

            pe.wait_ge(S("consts"), 1)
            pe.wait_ge(S("gains_loaded"), 7 * 16)
            pe.transpose(ps[0][:, 0:70], g_nat[:, :], ident[0:70, 0:70]).then_inc(S("gains_turned"), 1)
            pe.wait_ge(S("mem_loaded"), 16)
            split_stage("mem", mem_sb)
            pe.wait_ge(S("gains_copied"), 1)
            pe.wait_ge(S("split_lo"), SPLIT0["mem"] + KD)
            project(MEM_K)
            project(MEM_V)
            turn(MEM_K)
            pe.wait_ge(S("x_loaded"), 16)
            pe.wait_ge(S("turn_copied"), bank0[SB_Q])
            split_stage("mix", x_res)
            pe.wait_ge(S("split_lo"), SPLIT0["mix"] + KD)
            for c in range(Q_LAT, Q_NOPE):
                project(c)
                if SB_Q <= c - 1 < SB_V:
                    if c - 1 == SB_Q:
                        pe.wait_ge(S("split_lo"), SPLIT0["q"])
                    turn(c - 1)
            turn(KV_LAT)
            pe.wait_ge(S("turn_copied"), bank0[Q_NOPE])
            split_stage("q", c_q)
            split_stage("kv", c_kv)
            pe.wait_ge(S("split_lo"), SPLIT0["kv"] + 2)
            for c in range(Q_NOPE, W_OUT):
                project(c, a0=0 if c <= Q_PE else 4)
                if c - 1 in TURNED:
                    turn(c - 1)

            def scores(h):
                s, z = ps[h % 2], ps[2 + h % 2]
                if h < 2:
                    pe.wait_ge(*chunk_out(W_OUT - 1))
                else:
                    pe.wait_ge(S("mla_masked"), h - 1)
                    pe.wait_ge(S("sb_logs"), h - 1)
                    pe.wait_ge(S("sb_abs"), h - 1)
                po = ROPE * (h % 2)
                for t in range(TT):
                    n = (t + 1) * P
                    o = s[:, 0:P] if t == 0 else s[:, P:BLK]
                    q = slice(t * P, (t + 1) * P)
                    pe.matmul(o, q_t[:, h, q], k_t[:, h, 0:n], start=True, stop=False)
                    mm = pe.matmul(o, qpe_t[po:po + ROPE, h // 2, q], kpe_t[po:po + ROPE, 0:n],
                                   start=False, stop=True)
                mm.then_inc(S("mla_scored"), 1)
                pe.matmul(z[:, 0:SEQ], ksb_t[:, h, 0:P], qsb_t[:, h, :], start=True, stop=True)
                pe.matmul(z[:, SEQ:BLK], ksb_t[:, h, P:SEQ], qsb_t[:, h, P:SEQ], start=True,
                          stop=True).then_inc(S("sb_scored"), 1)

            def turn_probs(h):
                pe.wait_ge(S("mla_probs"), h + 1)
                if h >= 1:
                    pe.wait_ge(S("probs_copied"), h)
                for i in range(3):
                    mm = pe.transpose(ps[4][:, i * P:(i + 1) * P], p_mla[:, h % 2, i * P:(i + 1) * P],
                                      ident[:, :])
                mm.then_inc(S("probs_turned"), 1)

            def later(h):
                pe.wait_ge(S("sb_masked"), h + 1)
                if h >= 1:
                    pe.wait_ge(S("sb_summed"), h)
                m = sb_m[:, h % 2]
                pe.matmul(ps[5][:, 0:SEQ], above[:, :], m[:, 0:SEQ], start=True, stop=False)
                pe.matmul(ps[5][:, P:SEQ], ones[:, :], m[:, SEQ:BLK], start=False, stop=True)
                pe.matmul(ps[5][:, SEQ:BLK], above[:, :], m[:, SEQ:BLK], start=True,
                          stop=True).then_inc(S("sb_later"), 1)

            def values(h):
                o = ps[6 + h % 2]
                if h >= 2:
                    pe.wait_ge(S("o_copied"), h - 1)
                d = slice(h * HD, (h + 1) * HD)
                for m, (ready, w, v) in enumerate((("probs_copied", pt_mla, v_mla),
                                                   ("sb_weights", sb_a, v_sb))):
                    pe.wait_ge(S(ready), h + 1)
                    pe.matmul(o[:, 2 * m * P:(2 * m + 1) * P], w[:, h % 2, 0:P], v[:, 0, d],
                              start=True, stop=True)
                    pe.matmul(o[:, (2 * m + 1) * P:(2 * m + 2) * P], w[:, h % 2, P:SEQ], v[:, 0, d],
                              start=True, stop=False)
                    mm = pe.matmul(o[:, (2 * m + 1) * P:(2 * m + 2) * P], w[:, h % 2, SEQ:BLK],
                                   v[:, 1, d], start=False, stop=True)
                mm.then_inc(S("o_made"), 1)

            pe.wait_ge(S("turn_copied"), bank0[MEM_Q])
            for i in range(HEADS + 1):
                if i >= 1:
                    turn_probs(i - 1)
                    later(i - 1)
                if i < HEADS:
                    scores(i)
                if i >= 1:
                    values(i - 1)

            pe.wait_ge(S("o_normed"), 4)
            split_stage("out", o_cat)
            pe.wait_ge(S("split_lo"), SPLIT0["out"] + KD)
            for c in range(W_OUT, MEM_Q):
                project(c)
            pe.wait_ge(*chunk_out(MEM_Q - 1))
            split_stage("memx", x_res)
            pe.wait_ge(S("split_lo"), SPLIT0["memx"] + KD)
            project(MEM_Q)
            turn(MEM_Q)
            pe.wait_ge(S("turn_copied"), bank0[MEM_Q] + 2)

            def mem_scores(h):
                if h >= 2:
                    pe.wait_ge(S("mem_probs"), h - 1)
                for t in range(TT):
                    mm = pe.matmul(ps[h % 2][:, t * SEQ:(t + 1) * SEQ], qm_t[:, h, t * P:(t + 1) * P],
                                   km_t[:, h, :], start=True, stop=True)
                mm.then_inc(S("mem_scores"), 1)

            def mem_values(h):
                pe.wait_ge(S("mem_probs"), h + 1)
                if h >= 1:
                    pe.wait_ge(S("mem_pt"), h)
                for m in range(2):
                    for t in range(TT):
                        mm = pe.transpose(ps[4][:, m * SEQ + t * P:m * SEQ + (t + 1) * P],
                                          pm[:, h % 2, t, m * P:(m + 1) * P], ident[:, :])
                mm.then_inc(S("mem_pturned"), 1)
                pe.wait_ge(S("mem_pt"), h + 1)
                for t in range(TT):
                    for m in range(2):
                        mm = pe.matmul(ps[5 + t][:, h * HD:(h + 1) * HD],
                                       pmt[:, h % 2, m, t * P:(t + 1) * P],
                                       v_mem[:, m, h * HD:(h + 1) * HD], start=(m == 0), stop=(m == 1))
                mm.then_inc(S("mem_o"), 1)

            for i in range(MEM_HEADS + 1):
                if i < MEM_HEADS:
                    mem_scores(i)
                if i >= 1:
                    mem_values(i - 1)
            pe.wait_ge(S("mem_o_copied"), TT)
            split_stage("memo", o_mem)
            pe.wait_ge(S("split_lo"), SPLIT0["memo"] + MEM_HEADS)
            for c in range(MEM_O, CHUNKS):
                project(c)

            h_v = h_f[:, :, :].rearrange("p t (d k) -> p t k d", k=KD)
            pe.wait_ge(S("h_made"), TT)
            for kk in range(KD // 2):
                if kk >= 4:
                    pe.wait_ge(S("h_copied"), 2 * (kk - 4) + 2)
                for i in range(2):
                    for t in range(TT):
                        mm = pe.transpose(ps[4 + kk % 4][:, i * SEQ + t * P:i * SEQ + (t + 1) * P],
                                          h_v[:, t, 2 * kk + i, :], ident[:, :])
                mm.then_inc(S("h_turned"), 1)
            pe.wait_ge(S("h_copied"), KD)
            pe.wait_ge(S("router_loaded"), 4 * 16)
            for t in range(TT):
                for k in range(KD):
                    mm = pe.matmul(ps[t][:, 0:36], h_t[:, k, t * P:(t + 1) * P], w_r[:, k, :],
                                   start=(k == 0), stop=(k == KD - 1))
            mm.then_inc(S("logits"), 1)
            pe.wait_ge(S("chosen"), 1)
            sel = rt[:, 512:512 + TT * EXPERTS].rearrange("p (t e) -> p t e", t=TT)
            pe.matmul(ps[2][:, 0:EXPERTS], before, sel[:, 0], start=True, stop=True)
            pe.matmul(ps[2][:, EXPERTS:2 * EXPERTS], ones[:, :], sel[:, 0], start=True, stop=False)
            pe.matmul(ps[2][:, EXPERTS:2 * EXPERTS], before, sel[:, 1], start=False, stop=True)
            pe.matmul(ps[3][:, 0:EXPERTS], ones[:, :], sel[:, 0], start=True, stop=False)
            pe.matmul(ps[3][:, 0:EXPERTS], ones[:, :], sel[:, 1], start=False,
                      stop=True).then_inc(S("ranked"), 1)

            hi_v = a_hi[:, :, :].rearrange("p a b -> p (a b)").rearrange(
                "p (t d k) -> p t k d", t=TT, k=KD)
            lo_v = a_lo[:, :, :].rearrange("p a b -> p (a b)").rearrange(
                "p (t d k) -> p t k d", t=TT, k=KD)

            def expert(n, first=False):
                pe.wait_ge(S("hot_ready"), n + 1)
                if not first:
                    pe.wait_ge(S("xe_ready"), n)
                for k in range(KD):
                    for t in range(TT):
                        pe.matmul(ps[4][:, k * SLOTS:(k + 1) * SLOTS], hi_v[:, t, k, :],
                                  hot[:, t, :], start=(t == 0), stop=False)
                        mm = pe.matmul(ps[4][:, k * SLOTS:(k + 1) * SLOTS], lo_v[:, t, k, :],
                                       hot[:, t, :], start=False, stop=(t == TT - 1))
                mm.then_inc(S("gathered"), 1)
                pe.wait_ge(S("xe_ready"), n + 1)
                if not first:
                    pe.wait_ge(S("act_ready"), n)
                for b in range(2):
                    pe.wait_ge(S(f"gate_loaded{b}"), 16 * (n + 1))
                    pe.wait_ge(S(f"up_loaded{b}"), 16 * (n + 1))
                    for kk in range(KD // 2):
                        k = b * (KD // 2) + kk
                        for j in range(NJ):
                            mm = pe.matmul(
                                ps[5][j * SLOTS:(j + 1) * SLOTS, 0:2 * P].rearrange(
                                    "s (m f) -> s m f", m=2),
                                xe[:, k, :], gu[:, b, :, kk, j * P:(j + 1) * P],
                                start=(k == 0), stop=(k == KD - 1))
                    mm.then_inc(S(f"gu_used{b}"), 1)
                pe.wait_ge(S("act_ready"), n + 1)
                pe.transpose(ps[6][:, 0:P], act[:, :], ident[:, :]).then_inc(S("act_turned"), 1)
                pe.wait_ge(S("act_copied"), n + 1)
                if not first:
                    pe.wait_ge(S("y_copied"), n)
                for b, w in enumerate((down0, down1)):
                    pe.wait_ge(S(f"down_loaded{b}"), 16 * (n + 1))
                    for jj in range(2):
                        j = 2 * b + jj
                        for g in range(NJ):
                            mm = pe.matmul(ps[7][g * SLOTS:(g + 1) * SLOTS, :],
                                           act_t[:, j * SLOTS:(j + 1) * SLOTS],
                                           w[:, jj, g * UN:(g + 1) * UN],
                                           start=(j == 0), stop=(j == NJ - 1))
                    mm.then_inc(S(f"down_used{b}"), 1)

            pe.wait_ge(S("routed"), 1)
            total = pe.value_load(n_iter[0:1, 0:1], min_val=EXPERTS, max_val=MAX_PASSES * EXPERTS)
            expert(0, first=True)
            with pe.Fori(1, total) as n:
                expert(n)

        @block.scalar
        def _(sc):
            done = [0]

            def rounded(upto):
                for u in range(done[0], min(upto, len(UNITS))):
                    c, i = UNITS[u]
                    n = chunk_cols(c)
                    per = sum(16 * (UK if len(unit_src(*UNITS[v])[0].shape) == 4 else 1)
                              for v in range(u % RING, u + 1, RING))
                    sc.wait_ge(S(f"w_loaded{u % RING}"), per)
                    if u >= RING:
                        sc.wait_ge(S("w_used"), u - RING + 1)
                    sc.activation(w_hi[:, u % RING, :, 0:n], w_raw[:, u % RING, :, 0:n],
                                  ACT.Copy).then_inc(S("w_rounded"), 1)
                done[0] = max(done[0], upto)

            def square(src, t, col, width=None, junk=None):
                sc.activation(junk, src, ACT.Square,
                              accum_out=sums[:, col + t:col + t + 1]).then_inc(S("squared"), 1)

            def split_stage(name, g0, used, a0=0):
                k0, kn = SPLIT0[name], SPLIT_K[name]
                if used:
                    sc.wait_ge(S("w_used"), used)
                for k in range(kn):
                    b = (k0 + k) // 2
                    sc.wait_ge(S("split_turned"), b + 1)
                    i = k % 2
                    sc.activation(a_hi[:, a0 + k, :], ps[4 + b % 4][:, i * SEQ:(i + 1) * SEQ], ACT.Copy,
                                  scale=1.0 if g0 is None else g_t[:, g0 + k:g0 + k + 1]
                                  ).then_inc(S("split_hi"), 1)

            def chunk_copy(c, dst, col=None):
                sc.wait_ge(S("w_used"), UNIT0[c + 1])
                for t in range(TT):
                    ins = sc.activation(dst(t), ps[2 * (c % 2) + t][:, 0:chunk_cols(c)], ACT.Copy,
                                        scale=rstd[:, col + t:col + t + 1])
                ins.then_inc(S("chunk_copied"), 1)

            def to_nat(c, col):
                j = TURNED.index(c)
                if j >= 2:
                    sc.wait_ge(S("turned"), bank0[TURNED[j - 1]])
                chunk_copy(c, lambda t: nat[:, j % 2, t, :], col)

            for g, (gain, rows) in enumerate(((norm_mix, 16), (norm_mem_src, 16), (norm_mem_x, 16),
                                              (norm_q_lat, 4), (norm_kv_lat, 2), (norm_mla_out, 8),
                                              (norm_sb_out, 8))):
                r0 = (0, 16, 32, 48, 52, 54, 62)[g]
                sc.dma_start(g_nat[r0:r0 + rows, :], gain[0].rearrange("(k p) -> k p", p=P)
                             ).then_inc(S("gains_loaded"), 16)
            sc.dma_start(mem_sb[:, :, :], mem[0].rearrange("(t p) d -> p t d", p=P)).then_inc(
                S("mem_loaded"), 16)
            for t in range(TT):
                sc.dma_start(pos_i[:, t:t + 1], positions[0, t * P:(t + 1) * P].rearrange(
                    "(p a) -> p a", a=1)).then_inc(S("pos_loaded"), 16)
            sc.dma_start(x_res[:, :, :], x[0].rearrange("(t p) d -> p t d", p=P)).then_inc(
                S("x_loaded"), 16)
            sc.dma_start(g_ffn[:, :], norm_ffn[0].rearrange("(p k) -> p k", k=KD)).then_inc(
                S("ffn_gain_loaded"), 16)
            sc.wait_ge(S("angles"), 1)
            sc.activation(rope_cs[:, :, :, :], rope_cs[:, :, :, :], ACT.Sin).then_inc(S("rope_ready"), 1)
            sc.preload_act_table_set("natural_log_exp_and_others")
            sc.wait_ge(S("gains_turned"), 1)
            sc.activation(g_t[:, :], ps[0][:, 0:70], ACT.Copy).then_inc(S("gains_copied"), 1)
            sc.wait_ge(S("gains_copied"), 1)
            rounded(RING)
            sc.wait_ge(S("mem_loaded"), 16)
            split_stage("mem", 16, 0)
            junk = v_mla[:, :, :].rearrange("p t d -> p (t d)")
            for t in range(TT):
                square(mem_sb[:, t, :], t, SS_MEM, junk=junk)
                sc.wait_ge(S("squared"), t + 1)
            rounded(UNIT0[MEM_V] + RING)
            sc.wait_ge(S("rstd"), 1)
            to_nat(MEM_K, SS_MEM)
            rounded(UNIT0[Q_LAT] + RING)
            chunk_copy(MEM_V, lambda t: v_mem[:, t, :], SS_MEM)
            split_stage("mix", 0, UNIT0[Q_LAT])
            for t in range(TT):
                square(x_res[:, t, :], t, SS_X, junk=junk)
                sc.wait_ge(S("squared"), TT + t + 1)
            sc.wait_ge(S("rstd"), 2)
            for c in range(Q_LAT, Q_NOPE):
                rounded(UNIT0[c + 1] + RING)
                if c == Q_LAT:
                    chunk_copy(c, lambda t: c_q[:, t, :], SS_X)
                    sc.wait_ge(*chunk_out(c))
                    for t in range(TT):
                        square(c_q[:, t, :], t, SS_Q, junk=junk[:, 0:Q_RANK])
                        sc.wait_ge(S("squared"), 2 * TT + t + 1)
                elif c == KV_LAT:
                    chunk_copy(c, lambda t: c_kv[:, t, :], SS_X)
                    sc.wait_ge(*chunk_out(c))
                    for t in range(TT):
                        square(c_kv[:, t, 0:KV_RANK], t, SS_KV, junk=junk[:, 0:KV_RANK])
                        sc.wait_ge(S("squared"), 3 * TT + t + 1)
                elif c < SB_V:
                    to_nat(c, SS_X)
                else:
                    n0 = (c - SB_V) * UN
                    chunk_copy(c, lambda t: v_sb[:, t, n0:n0 + UN], SS_X)
            split_stage("q", 48, UNIT0[Q_NOPE])
            split_stage("kv", 52, UNIT0[Q_NOPE], a0=4)
            sc.wait_ge(S("rstd"), 4)
            for c in range(Q_NOPE, W_OUT):
                rounded(UNIT0[c + 1] + RING)
                if c < V_MLA:
                    to_nat(c, SS_Q if c <= Q_PE else SS_KV)
                else:
                    n0 = (c - V_MLA) * UN
                    chunk_copy(c, lambda t: v_mla[:, t, n0:n0 + UN], SS_KV)

            sc.wait_ge(S("w_used"), UNIT0[W_OUT])
            for i in range(HEADS + 1):
                if i >= 1:
                    h = i - 1
                    sc.wait_ge(S("probs_turned"), h + 1)
                    if h >= 2:
                        sc.wait_ge(S("o_made"), h - 1)
                    sc.activation(pt_mla[:, h % 2], ps[4][:, 0:BLK], ACT.Copy).then_inc(
                        S("probs_copied"), 1)
                    sc.wait_ge(S("sb_summed"), h + 1)
                    sc.activation(sb_b[:, h % 2], sb_b[:, h % 2], ACT.Exp).then_inc(S("sb_exp"), 1)
                if i < HEADS:
                    h = i
                    sc.wait_ge(S("mla_max"), h + 1)
                    for t, cols in enumerate((slice(0, P), slice(P, BLK))):
                        ins = sc.activation(p_mla[:, h % 2, cols], p_mla[:, h % 2, cols], ACT.Exp,
                                            bias=row_n[:, h, t:t + 1],
                                            accum_out=row_s[:, h, t:t + 1])
                    ins.then_inc(S("mla_probs"), 1)
                    sc.wait_ge(S("sb_scored"), h + 1)
                    if h >= 2:
                        sc.wait_ge(S("sb_logs"), h - 1)
                    sc.activation(sb_e[:, h % 2], ps[2 + h % 2][:, 0:BLK], ACT.Abs).then_inc(
                        S("sb_abs"), 1)
                    sc.wait_ge(S("sb_abs"), h + 1)
                    sc.activation(sb_e[:, h % 2], sb_e[:, h % 2], ACT.Exp, scale=-SC_SB).then_inc(
                        S("sb_expabs"), 1)
                    sc.wait_ge(S("sb_expabs"), h + 1)
                    sc.activation(sb_l[:, h % 2], sb_e[:, h % 2], ACT.Ln, bias=1.0).then_inc(
                        S("sb_log1p"), 1)
            sc.wait_ge(S("o_copied"), HEADS)
            for t in range(TT):
                for g, col in enumerate((SS_A, SS_B)):
                    square(o_cat[:, t, g * HEADS * HD:(g + 1) * HEADS * HD], t, col,
                           junk=junk[:, 0:HEADS * HD])
                    sc.wait_ge(S("squared"), 4 * TT + 2 * t + g + 1)
            sc.wait_ge(S("rstd"), 5)
            for t in range(TT):
                for g, col in enumerate((SS_A, SS_B)):
                    o = o_cat[:, t, g * HEADS * HD:(g + 1) * HEADS * HD]
                    sc.activation(o, o, ACT.Copy, scale=rstd[:, col + t:col + t + 1]).then_inc(
                        S("o_normed"), 1)
            split_stage("out", 54, 0)
            for c in range(W_OUT, MEM_Q):
                rounded(UNIT0[c + 1] + RING)
            sc.wait_ge(*chunk_out(MEM_Q - 1))
            split_stage("memx", 32, UNIT0[MEM_Q])
            for t in range(TT):
                square(x_res[:, t, :], t, SS_X1, junk=junk)
                sc.wait_ge(S("squared"), 6 * TT + t + 1)
            sc.wait_ge(S("rstd"), 6)
            rounded(UNIT0[MEM_Q + 1] + RING)
            to_nat(MEM_Q, SS_X1)
            sc.wait_ge(S("w_used"), UNIT0[MEM_O])
            for i in range(MEM_HEADS + 1):
                if i < MEM_HEADS:
                    h = i
                    sc.wait_ge(S("mem_max"), h + 1)
                    if h >= 2:
                        sc.wait_ge(S("mem_pturned"), h - 1)
                    for t in range(TT):
                        ins = sc.activation(pm[:, h % 2, t, :], ps[h % 2][:, t * SEQ:(t + 1) * SEQ],
                                            ACT.Exp, bias=mrow[:, 1, h, t:t + 1], scale=SC_SB,
                                            accum_out=mrow[:, 2, h, t:t + 1])
                    ins.then_inc(S("mem_probs"), 1)
                if i >= 1:
                    h = i - 1
                    sc.wait_ge(S("mem_pturned"), h + 1)
                    if h >= 2:
                        sc.wait_ge(S("mem_o"), h - 1)
                    sc.activation(pmt[:, h % 2].rearrange("p m t -> p (m t)"), ps[4][:, :],
                                  ACT.Copy).then_inc(S("mem_pt"), 1)
            split_stage("memo", None, UNIT0[MEM_O])
            for c in range(MEM_O, CHUNKS):
                rounded(UNIT0[c + 1] + RING)

            sc.wait_ge(*chunk_out(CHUNKS - 1))
            for t in range(TT):
                square(x_res[:, t, :], t, SS_X2, junk=w_hi[:, 0:2].rearrange(
                    "p r k n -> p (r k n)"))
                sc.wait_ge(S("squared"), 7 * TT + t + 1)
            sc.wait_ge(S("rstd"), 7)
            ah = a_hi[:, :, :].rearrange("p a b -> p (a b)").rearrange("p (t d) -> p t d", t=TT)
            for t in range(TT):
                sc.activation(h_f[:, t, :], x_res[:, t, :], ACT.Copy,
                              scale=rstd[:, SS_X2 + t:SS_X2 + t + 1]).then_inc(S("h_made"), 1)
            sc.wait_ge(S("h_made"), TT)
            for t in range(TT):
                sc.activation(ah[:, t, :], h_f[:, t, :], ACT.Copy).then_inc(S("h_rounded"), 1)
            sc.wait_ge(S("logits_ready"), 1)
            el = rt[:, 0:8]
            sc.activation(rt[:, 8:16], el, ACT.Exp).then_inc(S("group_exp"), 1)
            sc.wait_ge(S("second_gap"), 1)
            sc.activation(rt[:, 18:20], rt[:, 16:18], ACT.Exp).then_inc(S("second_exp"), 1)

            def expert(n, first=False):
                sc.wait_ge(S("gu_used1"), n + 1)
                if not first:
                    sc.wait_ge(S("act_ready"), n)
                sc.activation(sg[:, :], ps[5][:, 0:P], ACT.Silu).then_inc(S("silu"), 1)
                sc.wait_ge(S("act_turned"), n + 1)
                if not first:
                    sc.wait_ge(S("down_used1"), n)
                sc.activation(act_t[:, :], ps[6][:, 0:P], ACT.Copy).then_inc(S("act_copied"), 1)
                sc.wait_ge(S("down_used1"), n + 1)
                if not first:
                    sc.wait_ge(S("y_stored"), 16 * n)
                sc.activation(y_sb[:, :], ps[7][:, :], ACT.Copy).then_inc(S("y_copied"), 1)
                sc.wait_ge(S("y_copied"), n + 1)
                dst = y_dram.rearrange("(n s) d -> n s d", s=SLOTS)[n].rearrange(
                    "s (g d) -> g s d", g=NJ)
                sc.dma_start(dst, y_sb[:, :]).then_inc(S("y_stored"), 16)

            sc.wait_ge(S("routed"), 1)
            total = sc.value_load(n_iter[0:1, 0:1], min_val=EXPERTS, max_val=MAX_PASSES * EXPERTS)
            expert(0, first=True)
            with sc.Fori(1, total) as n:
                expert(n)
            sc.wait_ge(S("y_stored"), 16 * total)
            sc.sem_inc(S("all_stored"), 1)
            for t in range(TT):
                sc.wait_ge(S("y_added"), 2 * t + 2)
                sc.activation(y_pick[:, 0, t, :], x_res[:, t, :], ACT.Square,
                              accum_out=sums[:, t:t + 1]).then_inc(S("final_squared"), 1)

        @block.vector
        def _(ve):
            done = [0]
            steps = [0]

            def link(ins):
                steps[0] += 1
                ins.then_inc(S("vector_step"), 1)
                ve.wait_ge(S("vector_step"), steps[0])

            def split_w(upto):
                for u in range(done[0], min(upto, len(UNITS))):
                    n = chunk_cols(UNITS[u][0])
                    ve.wait_ge(S("w_rounded"), u + 1)
                    ve.tensor_tensor(w_lo[:, u % RING, :, 0:n], w_raw[:, u % RING, :, 0:n],
                                     w_hi[:, u % RING, :, 0:n], ALU.subtract).then_inc(
                                         S("w_split"), 1)
                done[0] = max(done[0], upto)

            def split_stage(name, g0, a0=0):
                k0, kn = SPLIT0[name], SPLIT_K[name]
                for k in range(kn):
                    b, i = (k0 + k) // 2, k % 2
                    ve.wait_ge(S("split_hi"), k0 + k - i + 2)
                    ve.scalar_tensor_tensor(
                        out=a_lo[:, a0 + k, :], in0=ps[4 + b % 4][:, i * SEQ:(i + 1) * SEQ],
                        scalar=1.0 if g0 is None else g_t[:, g0 + k:g0 + k + 1],
                        in1=a_hi[:, a0 + k, :], op0=ALU.mult, op1=ALU.subtract).then_inc(
                            S("split_lo"), 1)

            def copy_turned(c):
                dst = None if c == KV_LAT else turned_dst(c)
                for b in range(1 if c == KV_LAT else 2):
                    m = bank0[c] + b
                    ve.wait_ge(S("turned"), m + 1)
                    if c == KV_LAT:
                        ve.tensor_copy(kpe_t[:, :], ps[4 + m % 4][:, 0:SEQ]).then_inc(
                            S("turn_copied"), 1)
                    else:
                        ve.tensor_copy(dst[:, 2 * b:2 * b + 2, :].rearrange("p h t -> p (h t)"),
                                       ps[4 + m % 4][:, :]).then_inc(S("turn_copied"), 1)

            def rope(dst1, dst2, x1, x2, heads):
                c = rope_cs[:, 0]
                s = rope_cs[:, 1]
                for t in range(TT):
                    cb = c[:, t:t + 1, :].to_broadcast([P, heads, ROPE // 2])
                    sb = s[:, t:t + 1, :].to_broadcast([P, heads, ROPE // 2])
                    n = heads * ROPE // 2
                    a = rt_a[:, 0, 0:n].rearrange("p (h c) -> p h c", h=heads)
                    b = rt_a[:, 1, 0:n].rearrange("p (h c) -> p h c", h=heads)
                    d = rt_a[:, 2, 0:n].rearrange("p (h c) -> p h c", h=heads)
                    e = rt_a[:, 3, 0:n].rearrange("p (h c) -> p h c", h=heads)
                    ve.tensor_tensor(a, x1(t), cb, ALU.mult)
                    ve.tensor_tensor(b, x2(t), sb, ALU.mult)
                    ve.tensor_tensor(d, x2(t), cb, ALU.mult)
                    link(ve.tensor_tensor(e, x1(t), sb, ALU.mult))
                    ve.tensor_tensor(dst1(t), a, b, ALU.subtract)
                    link(ve.tensor_tensor(dst2(t), d, e, ALU.add))

            rt_a = place("rope_tmp", [P, 4, 256], offset=o_at)

            from math import pi
            import numpy as np
            half = ROPE // 2
            inv = small[:, 0:half]
            pf = small[:, 32:34]
            ve.wait_ge(S("inv_freq"), 1)
            ve.wait_ge(S("pos_loaded"), 16 * TT)
            link(ve.tensor_copy(pf, pos_i[:, :]))
            turns = rt_a2 = place("rope_turns", [P, TT, ROPE // 2], offset=o_at + 60 * 0 + 16 * 1024)
            for t in range(TT):
                ins = ve.tensor_scalar(rope_cs[:, 1, t, :], inv, pf[:, t:t + 1], None, ALU.mult)
            link(ins)
            magic = 1.5 * 2.0 ** 23
            c1 = 6.28125
            c2 = float(np.float32(2 * pi - c1))
            c3 = 2 * pi - c1 - c2
            ang, cosv = rope_cs[:, 1], rope_cs[:, 0]
            link(ve.tensor_scalar(turns[:, :, :], ang, 1.0 / (2 * pi), magic, ALU.mult, ALU.add))
            link(ve.tensor_scalar(turns[:, :, :], turns[:, :, :], -magic, None, ALU.add))
            for cc in (c1, c2, c3):
                link(ve.scalar_tensor_tensor(out=ang, in0=turns[:, :, :], scalar=-cc, in1=ang,
                                             op0=ALU.mult, op1=ALU.add))
            link(ve.tensor_scalar(cosv, ang, pi / 2, None, ALU.add))
            link(ve.tensor_scalar(turns[:, :, :], cosv, pi, -2 * pi, ALU.is_gt, ALU.mult))
            link(ve.tensor_tensor(cosv, cosv, turns[:, :, :], ALU.add))
            ve.tensor_scalar(rope_cs[:, :, :, :], rope_cs[:, :, :, :], 3.1415925, -3.1415925, ALU.min,
                             ALU.max).then_inc(S("angles"), 1)

            split_w(RING)
            ve.wait_ge(S("gains_copied"), 1)
            split_stage("mem", 16)
            split_w(UNIT0[MEM_V] + RING)
            split_w(UNIT0[Q_LAT] + RING)
            copy_turned(MEM_K)
            split_stage("mix", 0)
            for c in range(Q_LAT, Q_NOPE):
                split_w(UNIT0[c + 1] + RING)
                if SB_Q <= c - 1 < SB_V:
                    copy_turned(c - 1)
                    if c - 1 == SB_K + 1:
                        j = TURNED.index(KV_LAT)
                        ve.wait_ge(S("rope_ready"), 1)
                        ve.wait_ge(S("turned"), bank0[SB_K + 1])
                        ve.wait_ge(*chunk_out(KV_LAT))
                        kn = nat[:, j % 2]
                        rope(lambda t: kn[:, t:t + 1, 0:half], lambda t: kn[:, t:t + 1, half:ROPE],
                             lambda t: c_kv[:, t:t + 1, KV_RANK:KV_RANK + half],
                             lambda t: c_kv[:, t:t + 1, KV_RANK + half:KV_RANK + ROPE], 1)
                        ve.tensor_copy(kn[:, :, ROPE:2 * ROPE], kn[:, :, 0:ROPE]).then_inc(
                            S("roped"), 1)
            copy_turned(KV_LAT)
            split_stage("q", 48)
            split_stage("kv", 52, a0=4)
            for c in range(Q_NOPE, W_OUT):
                split_w(UNIT0[c + 1] + RING)
                if c == K_NOPE:
                    j = TURNED.index(Q_PE)
                    ve.wait_ge(*chunk_out(Q_PE))
                    qn = nat[:, j % 2].rearrange("p t (h c) -> p t h c", c=ROPE)
                    rope(lambda t: qn[:, t, :, 0:half], lambda t: qn[:, t, :, half:ROPE],
                         lambda t: qn[:, t, :, 0:half], lambda t: qn[:, t, :, half:ROPE], HEADS)
                    ve.tensor_copy(small[:, 62:63], small[:, 33:34]).then_inc(S("roped"), 1)
                if c - 1 in TURNED:
                    copy_turned(c - 1)

            ve.wait_ge(S("w_used"), UNIT0[W_OUT])
            for i in range(HEADS + 1):
                if i >= 1:
                    h = i - 1
                    ve.wait_ge(S("sb_later"), h + 1)
                    ve.tensor_tensor(sb_b[:, h % 2], ps[5][:, 0:BLK], sb_b[:, h % 2],
                                     ALU.add).then_inc(S("sb_summed"), 1)
                if i < HEADS:
                    h = i
                    ve.wait_ge(S("mla_scored"), h + 1)
                    if h >= 2:
                        ve.wait_ge(S("probs_turned"), h - 1)
                    ve.scalar_tensor_tensor(out=p_mla[:, h % 2], in0=ps[h % 2][:, 0:BLK], scalar=SC_MLA,
                                            in1=mla_mask[:, :], op0=ALU.mult, op1=ALU.add).then_inc(
                                                S("mla_masked"), 1)
                    ve.wait_ge(S("mla_masked"), h + 1)
                    ve.tensor_reduce(row_m[:, h, 0:1], p_mla[:, h % 2, 0:P], AX, ALU.max)
                    link(ve.tensor_reduce(row_m[:, h, 1:2], p_mla[:, h % 2, P:BLK], AX, ALU.max))
                    ve.tensor_scalar(row_n[:, h, :], row_m[:, h, :], -1.0, None, ALU.mult).then_inc(
                        S("mla_max"), 1)
                    ve.wait_ge(S("sb_log1p"), h + 1)
                    if h >= 2:
                        ve.wait_ge(S("sb_weights"), h - 1)
                    link(ve.tensor_scalar(sb_b[:, h % 2], ps[2 + h % 2][:, 0:BLK], SC_SB, 0.0, ALU.mult,
                                          ALU.min))
                    link(ve.tensor_tensor(sb_b[:, h % 2], sb_b[:, h % 2], sb_l[:, h % 2],
                                          ALU.subtract))
                    if h >= 2:
                        ve.wait_ge(S("sb_later"), h - 1)
                    ve.scalar_tensor_tensor(out=sb_m[:, h % 2], in0=ps[2 + h % 2][:, 0:BLK],
                                            scalar=-SC_SB, in1=sb_b[:, h % 2], op0=ALU.mult,
                                            op1=ALU.add).then_inc(S("sb_logs"), 1)
                if i >= 1:
                    h = i - 1
                    ve.wait_ge(S("o_made"), h + 1)
                    link(ve.reciprocal(row_r[:, h, :], row_s[:, h, :]))
                    o = ps[6 + h % 2]
                    for t in range(TT):
                        ve.tensor_scalar(o_cat[:, t, h * HD:(h + 1) * HD], o[:, t * P:(t + 1) * P],
                                         row_r[:, h, t:t + 1], None, ALU.mult)
                    ve.tensor_copy(o_cat[:, :, (HEADS + h) * HD:(HEADS + h + 1) * HD],
                                   o[:, 2 * P:4 * P].rearrange("p (t d) -> p t d", t=TT)).then_inc(
                                       S("o_copied"), 1)
            split_stage("out", 54)

            def add_chunk(c, n0):
                ve.wait_ge(S("w_used"), UNIT0[c + 1])
                for t in range(TT):
                    xs = x_res[:, t, n0:n0 + UN]
                    ins = ve.tensor_tensor(xs, ps[2 * (c % 2) + t][:, :], xs, ALU.add)
                ins.then_inc(S("chunk_added"), 1)

            for c in range(W_OUT, MEM_Q):
                split_w(UNIT0[c + 1] + RING)
                add_chunk(c, (c - W_OUT) * UN)
            split_stage("memx", 32)
            split_w(UNIT0[MEM_Q + 1] + RING)
            copy_turned(MEM_Q)
            ve.sem_inc(S("mem_turned_q"), 1)
            for i in range(MEM_HEADS):
                ve.wait_ge(S("mem_scores"), i + 1)
                link(ve.tensor_reduce(mrow[:, 0, i, :], ps[i % 2][:, :].rearrange(
                    "p (t m) -> p t m", t=TT), AX, ALU.max))
                ve.tensor_scalar(mrow[:, 1, i, :], mrow[:, 0, i, :], -SC_SB, None, ALU.mult).then_inc(
                    S("mem_max"), 1)
            ve.wait_ge(S("mem_probs"), MEM_HEADS)
            link(ve.reciprocal(mrow[:, 3], mrow[:, 2]))
            ve.wait_ge(S("mem_o"), MEM_HEADS)
            for t in range(TT):
                ve.tensor_tensor(o_mem[:, t, :].rearrange("p (h d) -> p h d", h=MEM_HEADS),
                                 ps[5 + t][:, :].rearrange("p (h d) -> p h d", h=MEM_HEADS),
                                 mrow[:, 3, :, t:t + 1].to_broadcast([P, MEM_HEADS, HD]),
                                 ALU.mult).then_inc(S("mem_o_copied"), 1)
            split_stage("memo", None)
            for c in range(MEM_O, CHUNKS):
                split_w(UNIT0[c + 1] + RING)
                add_chunk(c, (c - MEM_O) * UN)

            al = a_lo[:, :, :].rearrange("p a b -> p (a b)").rearrange("p (t d) -> p t d", t=TT)
            ah = a_hi[:, :, :].rearrange("p a b -> p (a b)").rearrange("p (t d) -> p t d", t=TT)
            ve.wait_ge(S("ffn_gain_loaded"), 16)
            for k in range(KD):
                ve.wait_ge(S("h_turned"), k // 2 + 1)
                ve.tensor_scalar(h_t[:, k, :], ps[4 + k // 2 % 4][:, k % 2 * SEQ:(k % 2 + 1) * SEQ],
                                 g_ffn[:, k:k + 1], None, ALU.mult).then_inc(S("h_copied"), 1)
            for t in range(TT):
                ve.wait_ge(S("h_rounded"), t + 1)
                ve.tensor_tensor(al[:, t, :], h_f[:, t, :], ah[:, t, :], ALU.subtract).then_inc(
                    S("h_split"), 1)

            def field(a, *dims):
                n = 1
                for d in dims:
                    n *= d
                v = rt[:, a:a + n]
                names = "abcd"[:len(dims)]
                if len(dims) > 1:
                    v = v.rearrange(f"p ({' '.join(names)}) -> p {' '.join(names)}",
                                    **{m: d for m, d in zip(names, dims)})
                return v

            def bc(v, *shape):
                return v.to_broadcast([P, *shape])

            lg = field(32, TT, 36)
            gl, el = lg[:, :, 0:GROUPS], lg[:, :, GROUPS:36]
            gm = field(104, TT, 1)
            gsum = field(106, TT, 1)
            gx, gexp = field(0, TT, GROUPS), field(8, TT, GROUPS)
            gap, r2 = field(16, TT), field(18, TT)
            ghot = field(112, TT, GROUPS)
            first_of = field(120, TT, GROUPS)
            best = field(128, TT, 1)
            prod = field(160, TT, GROUPS, PER_GROUP)
            cand = field(224, TT, PER_GROUP)
            m1, m2 = field(240, TT, 1), field(242, TT, 1)
            e1 = field(248, TT, PER_GROUP)
            hot1 = field(264, TT, PER_GROUP)
            hot2 = field(280, TT, PER_GROUP)
            den = field(296, TT)
            pg = field(298, TT)
            pick1 = field(320, TT, GROUPS, PER_GROUP)
            pick2 = field(384, TT, GROUPS, PER_GROUP)
            sel = field(512, TT, EXPERTS)
            row = field(576, TT, EXPERTS)
            tmpr = field(640, TT, EXPERTS)
            cnt = field(704, 8)
            falling = field(720, PER_GROUP)
            row0 = field(736, EXPERTS)

            ve.wait_ge(S("logits"), 1)
            ve.wait_ge(S("router_consts"), 2)
            for t in range(TT):
                ins = ve.tensor_tensor(lg[:, t, :], ps[t][:, 0:36], b_r[:, :], ALU.add)
            link(ins)
            link(ve.tensor_reduce(gm, gl, AX, ALU.max))
            ve.tensor_tensor(gx, gl, bc(gm, TT, GROUPS), ALU.subtract).then_inc(S("logits_ready"), 1)

            def first_hot(dst, values, top, scratch_, n, base_):
                link(ve.tensor_tensor(scratch_, values, bc(top, TT, n), ALU.is_equal))
                f = falling[:, 0:n].rearrange("p (a b) -> p a b", a=1)
                fb = bc(f, TT, n)
                link(ve.tensor_tensor(scratch_, scratch_, fb, ALU.mult))
                link(ve.tensor_reduce(best, scratch_, AX, ALU.max))
                link(ve.tensor_tensor(dst, fb, bc(best, TT, n), ALU.is_equal))

            first_hot(ghot, gl, gm, first_of, GROUPS, 0)
            gh4 = ghot.rearrange("p t (g e) -> p t g e", e=1)
            for t in range(TT):
                ins = ve.tensor_tensor(prod[:, t], el[:, t].rearrange("p (g e) -> p g e", g=GROUPS),
                                       bc(gh4[:, t], GROUPS, PER_GROUP), ALU.mult)
            link(ins)
            link(ve.tensor_reduce(cand, prod.rearrange("p t g e -> p t e g"), AX, ALU.add))
            link(ve.tensor_reduce(m1, cand, AX, ALU.max))
            first_hot(hot1, cand, m1, e1, PER_GROUP, 0)
            link(ve.scalar_tensor_tensor(out=cand, in0=hot1, scalar=-3.0e38, in1=cand, op0=ALU.mult,
                                         op1=ALU.add))
            link(ve.tensor_reduce(m2, cand, AX, ALU.max))
            ve.tensor_tensor(gap.rearrange("p (t a) -> p t a", a=1), m2, m1, ALU.subtract).then_inc(
                S("second_gap"), 1)
            first_hot(hot2, cand, m2, e1, PER_GROUP, 0)
            for t in range(TT):
                for hot_n, pick in ((hot1, pick1), (hot2, pick2)):
                    hb = hot_n[:, t:t + 1, :]
                    ins = ve.tensor_tensor(pick[:, t], bc(hb, GROUPS, PER_GROUP),
                                           bc(gh4[:, t], GROUPS, PER_GROUP), ALU.mult)
            link(ins)
            p1 = pick1.rearrange("p t g e -> p t (g e)")
            p2 = pick2.rearrange("p t g e -> p t (g e)")
            ve.tensor_tensor(sel, p1, p2, ALU.add).then_inc(S("chosen"), 1)
            ve.wait_ge(S("group_exp"), 1)
            ve.wait_ge(S("second_exp"), 1)
            link(ve.tensor_reduce(gsum, gexp, AX, ALU.add))
            link(ve.tensor_scalar(den, r2, 1.0, None, ALU.add))
            link(ve.tensor_tensor(den, den, gsum.rearrange("p t a -> p (t a)"), ALU.mult))
            link(ve.reciprocal(gate_w[:, 0, :], den))
            link(ve.tensor_tensor(gate_w[:, 1, :], gate_w[:, 0, :], r2, ALU.mult))
            ve.wait_ge(S("ranked"), 1)
            rank = ps[2][:, 0:TT * EXPERTS].rearrange("p (t e) -> p t e", t=TT)
            link(ve.tensor_scalar(row, rank, -(SLOTS - 1) / 2.0, 1.0 / SLOTS, ALU.add, ALU.mult))
            link(ve.tensor_scalar(row, row, magic, -magic, ALU.add, ALU.add))
            link(ve.tensor_scalar(row, row, float(SLOTS * EXPERTS - SLOTS), None, ALU.mult))
            link(ve.tensor_tensor(row, row, rank, ALU.add))
            r0 = row0.rearrange("p (a e) -> p a e", a=1)
            link(ve.tensor_tensor(row, row, bc(r0, TT, EXPERTS), ALU.add))
            for i, pk in enumerate((p1, p2)):
                link(ve.tensor_tensor(tmpr, row, pk, ALU.mult))
                link(ve.tensor_reduce(rel[:, i, :].rearrange("p (t a) -> p t a", a=1), tmpr, AX,
                                      ALU.add))
            ve.tensor_copy(y_idx[:, :, :, 0], rel[:, :, :])
            later_idx = field(760, 2, TT)
            link(ve.tensor_scalar(later_idx, rel[:, :, :], float(PASS_ROWS), 1048576.0, ALU.is_lt,
                                  ALU.mult))
            link(ve.tensor_tensor(later_idx, later_idx, rel[:, :, :], ALU.add))
            ve.tensor_copy(y_idx2[:, :, :, 0], later_idx)
            link(ve.tensor_reduce(cnt[:, 0:1], ps[3][:, 0:EXPERTS], AX, ALU.max))
            link(ve.tensor_scalar(cnt[:, 0:1], cnt[:, 0:1], (SLOTS - 1) / 2.0, 1.0 / SLOTS, ALU.add,
                                  ALU.mult))
            link(ve.tensor_scalar(cnt[:, 0:1], cnt[:, 0:1], magic, -magic, ALU.add, ALU.add))
            link(ve.tensor_scalar(cnt[:, 0:1], cnt[:, 0:1], float(EXPERTS), None, ALU.mult))
            ve.tensor_copy(n_iter[:, :], cnt[:, 0:1]).then_inc(S("routed"), 1)

            def expert(n, first=False):
                if not first:
                    ve.wait_ge(S("gathered"), n)
                    ve.wait_ge(S("hot_ready"), n)
                    ve.tensor_scalar(rel[:, :, :], rel[:, :, :], -float(SLOTS), None,
                                     ALU.add).then_inc(S("rel_moved"), 1)
                    ve.wait_ge(S("rel_moved"), n)
                it = iota32[:, :].rearrange("p (a s) -> p a s", a=1)
                for i in range(2):
                    rb = rel[:, i, :].rearrange("p (t a) -> p t a", a=1)
                    ve.tensor_tensor(hot_f[:, i], bc(it, TT, SLOTS), bc(rb, TT, SLOTS),
                                     ALU.is_equal).then_inc(S("pick_hot"), 1)
                ve.wait_ge(S("pick_hot"), 2 * (n + 1))
                ve.tensor_tensor(hot[:, :, :], hot_f[:, 0], hot_f[:, 1], ALU.add).then_inc(
                    S("hot_ready"), 1)
                ve.wait_ge(S("gathered"), n + 1)
                if not first:
                    ve.wait_ge(S("gu_used1"), n)
                gb = g_ffn[:, :].rearrange("p (k a) -> p k a", a=1)
                ve.tensor_tensor(xe[:, :, :], ps[4][:, :].rearrange("p (k s) -> p k s", k=KD),
                                 bc(gb, KD, SLOTS), ALU.mult).then_inc(S("xe_ready"), 1)
                ve.wait_ge(S("silu"), n + 1)
                if not first:
                    ve.wait_ge(S("act_turned"), n)
                ve.tensor_tensor(act[:, :], sg[:, :], ps[5][:, P:2 * P], ALU.mult).then_inc(
                    S("act_ready"), 1)

            ve.wait_ge(S("routed"), 1)
            total = ve.value_load(n_iter[0:1, 0:1], min_val=EXPERTS, max_val=MAX_PASSES * EXPERTS)
            expert(0, first=True)
            with ve.Fori(1, total) as n:
                expert(n)

            for t in range(TT):
                for i in range(2):
                    ve.wait_ge(S(f"picked{t}{i}"), 16)
                    if i:
                        ve.wait_ge(S("y_added"), 2 * t + 1)
                    ve.scalar_tensor_tensor(out=x_res[:, t, :], in0=y_pick[:, i, t, :],
                                            scalar=gate_w[:, i, t:t + 1], in1=x_res[:, t, :],
                                            op0=ALU.mult, op1=ALU.add).then_inc(S("y_added"), 1)
            ve.wait_ge(S("final_gain_loaded"), 16)
            for t in range(TT):
                ve.wait_ge(S("final_rstd"), t + 1)
                ve.scalar_tensor_tensor(out=x_res[:, t, :], in0=x_res[:, t, :], scalar=rstd[:, t:t + 1],
                                        in1=g_fin[:, :], op0=ALU.mult, op1=ALU.mult).then_inc(
                                            S("final"), 1)

        @block.gpsimd
        def _(gp):
            steps = [0]

            def link(ins):
                steps[0] += 1
                ins.then_inc(S("gp_step"), 1)
                gp.wait_ge(S("gp_step"), steps[0])

            half = ROPE // 2
            for i in range(half):
                ins = gp.memset(small[:, i:i + 1], float(10000.0 ** (-2.0 * i / ROPE)))
            ins.then_inc(S("inv_freq"), 1)
            gp.memset(ident[:, :], 0.0)
            gp.memset(ones[:, :], 1.0)
            gp.memset(sb_mask[:, :], 1.0)
            link(gp.memset(mla_mask[:, :], 0.0))
            gp.affine_select(out=ident[:, :], in_=ident[:, :], compare_op=ALU.not_equal, fill=1.0, base=0,
                             pattern=[[-1, P]], channel_multiplier=1)
            gp.affine_select(out=above[:, :], in_=ones[:, :], compare_op=ALU.is_gt, fill=0.0, base=0,
                             pattern=[[-1, P]], channel_multiplier=1)
            for lo in (0, SEQ):
                gp.affine_select(out=sb_mask[:, lo:lo + P], in_=sb_mask[:, lo:lo + P],
                                 compare_op=ALU.is_gt, fill=0.0, base=0, pattern=[[1, P]],
                                 channel_multiplier=-1)
                gp.affine_select(out=mla_mask[:, lo:lo + P], in_=mla_mask[:, lo:lo + P],
                                 compare_op=ALU.is_ge, fill=-1.0e30, base=0, pattern=[[-1, P]],
                                 channel_multiplier=1)
            link(gp.iota(iota32[:, :], [[1, SLOTS]], base=0, channel_multiplier=0,
                         allow_small_or_imprecise_dtypes=True))
            gp.sem_inc(S("consts"), 1)
            gp.memset(minus_half[:, :], -0.5)

            def norms(cols, width, squares):
                gp.wait_ge(S("squared"), squares)
                for col in cols:
                    r = rstd[:, col:col + TT]
                    link(gp.tensor_scalar(r, sums[:, col:col + TT], 1.0 / width, EPS, ALU.mult, ALU.add))
                    ins = gp.tensor_tensor(r, r, minus_half[:, :], ALU.pow)
                ins.then_inc(S("rstd"), 1)

            norms([SS_MEM], D, TT)
            norms([SS_X], D, 2 * TT)
            norms([SS_Q], Q_RANK, 3 * TT)
            norms([SS_KV], KV_RANK, 4 * TT)
            for i in range(HEADS + 1):
                if i >= 1:
                    h = i - 1
                    gp.wait_ge(S("sb_exp"), h + 1)
                    if h >= 2:
                        gp.wait_ge(S("o_made"), h - 1)
                    gp.tensor_tensor(sb_a[:, h % 2], sb_b[:, h % 2], sb_mask[:, :], ALU.mult).then_inc(
                        S("sb_weights"), 1)
                if i < HEADS:
                    gp.wait_ge(S("sb_logs"), i + 1)
                    gp.tensor_tensor(sb_m[:, i % 2], sb_m[:, i % 2], sb_mask[:, :], ALU.mult).then_inc(
                        S("sb_masked"), 1)
            norms([SS_A, SS_B], HEADS * HD, 6 * TT)
            norms([SS_X1], D, 7 * TT)
            gp.wait_ge(S("turned"), bank0[MEM_Q] + 2)
            gp.dma_start(w_r[:, :, 0:GROUPS], w_group[0].rearrange("(p k) g -> p k g", k=KD)).then_inc(
                S("router_loaded"), 16)
            gp.dma_start(w_r[:, :, GROUPS:36], w_expert_router[0].rearrange("(p k) g -> p k g", k=KD)
                         ).then_inc(S("router_loaded"), 16)
            gp.dma_start(b_r[:, 0:GROUPS], b_group[0:1, :].to_broadcast([P, GROUPS])).then_inc(
                S("router_loaded"), 16)
            gp.dma_start(b_r[:, GROUPS:36], b_expert[0:1, :].to_broadcast([P, EXPERTS])).then_inc(
                S("router_loaded"), 16)
            gp.iota(rt[:, 720:720 + PER_GROUP], [[-1, PER_GROUP]], base=PER_GROUP, channel_multiplier=0,
                    allow_small_or_imprecise_dtypes=True).then_inc(S("router_consts"), 1)
            gp.iota(rt[:, 736:736 + EXPERTS], [[SLOTS, EXPERTS]], base=0, channel_multiplier=0,
                    allow_small_or_imprecise_dtypes=True).then_inc(S("router_consts"), 1)
            norms([SS_X2], D, 8 * TT)
            gp.wait_ge(S("h_split"), TT)
            gp.wait_ge(S("h_copied"), KD)
            gp.dma_start(g_fin[:, :], norm_final.rearrange("(a d) -> a d", a=1).to_broadcast([P, D])
                         ).then_inc(S("final_gain_loaded"), 16)
            gp.wait_ge(S("routed"), 1)
            total = gp.value_load(n_iter[0:1, 0:1], min_val=EXPERTS, max_val=MAX_PASSES * EXPERTS)
            gp.wait_ge(S("all_stored"), 1)

            def fetch(idx, rows, landed):
                for t in range(TT):
                    for i in range(2):
                        gp.indirect_dma_start(
                            out=y_pick[:, i, t, :], out_offset=None, in_=y_dram[0:rows, :],
                            in_offset=bass.IndirectOffsetOnAxis(ap=idx[:, i, t, :], axis=0),
                            bounds_check=rows - 1, oob_is_err=False
                        ).then_inc(S(f"{landed}{t}{i}"), 16)

            with gp.If(total > EXPERTS):
                fetch(y_idx2, MAX_PASSES * PASS_ROWS, "late_picked")
                for t in range(TT):
                    for i in range(2):
                        gp.wait_ge(S(f"late_picked{t}{i}"), 16)
            fetch(y_idx, PASS_ROWS, "picked")
            for t in range(TT):
                gp.wait_ge(S("final_squared"), t + 1)
                link(gp.tensor_scalar(rstd[:, t:t + 1], sums[:, t:t + 1], 1.0 / D, EPS, ALU.mult,
                                      ALU.add))
                gp.tensor_tensor(rstd[:, t:t + 1], rstd[:, t:t + 1], minus_half[:, 0:1],
                                 ALU.pow).then_inc(S("final_rstd"), 1)


_INS = ["x", "mem", "positions", "norm_mix", "w_in", "norm_q_lat", "w_q_b", "norm_kv_lat", "w_kv_b",
        "norm_mla_out", "norm_sb_out", "w_out", "norm_mem_x", "norm_mem_src", "w_mem_q", "w_mem_kv",
        "w_mem_o", "norm_ffn", "w_group", "b_group", "w_expert_router", "b_expert", "w_gate", "w_up",
        "w_down", "norm_final"]


def kernel(**inputs):
    import numpy as _np
    import concourse.bacc as _bacc
    from concourse import mybir as _mybir
    from concourse.bass_utils import run_bass_kernel_spmd as _run

    nc = _bacc.Bacc("TRN2", target_bir_lowering=False, num_devices=1)
    arrays, args = {}, []
    for name in _INS:
        a = _np.ascontiguousarray(inputs[name])
        arrays[f"in_{name}"] = a
        args.append(nc.dram_tensor(f"in_{name}", a.shape, _mybir.dt.from_np(a.dtype),
                                   kind="ExternalInput").ap())
    args.append(nc.dram_tensor("out_0", (1, SEQ, D), F32, kind="ExternalOutput").ap())
    layer(nc, *args)
    r = _run(nc, [arrays], core_ids=[0])
    return r.results[0]["out_0"]
```

```python
from contextlib import ExitStack

import concourse.bass as bass
from concourse import mybir

F32 = mybir.dt.float32
F32R = mybir.dt.float32r
I32 = mybir.dt.int32
U32 = mybir.dt.uint32
ALU = mybir.AluOpType
ACT = mybir.ActivationFunctionType
AX = mybir.AxisListType.X

P = 128
KB = 256
SEQ, D = 256, 2048
TT = SEQ // P
KD = D // P
Q_RANK, KV_RANK, ROPE = 512, 256, 64
HEADS, HD = 8, 128
MEM_HEADS = 4
GROUPS, PER_GROUP = 4, 8
EXPERTS = GROUPS * PER_GROUP
FE = 512
SLOTS = 32
NJ = P // SLOTS
MAX_PASSES = SEQ // SLOTS
AHEAD = 3
PASS_ROWS = EXPERTS * SLOTS
EPS = 1e-6
SC_MLA = float(HD + ROPE) ** -0.5
SC_SB = float(HD) ** -0.5
BLK = 3 * P
RING = 4
UK = 2
UN = 512

Q_LAT, KV_LAT, SB_Q, SB_K, SB_V, Q_NOPE, Q_PE, K_NOPE, V_MLA = 0, 1, 2, 4, 6, 8, 10, 11, 13
MEM_K, MEM_V, W_OUT, MEM_Q, MEM_O, CHUNKS = 15, 16, 17, 21, 22, 26


def chunk_tiles(c):
    if Q_NOPE <= c <= Q_PE:
        return Q_RANK // P
    if K_NOPE <= c < MEM_K:
        return KV_RANK // P
    return MEM_HEADS if c >= MEM_O else KD


def chunk_cols(c):
    return KV_RANK + ROPE if c == KV_LAT else UN


UNIT0 = [0]
for _c in range(CHUNKS):
    UNIT0.append(UNIT0[-1] + chunk_tiles(_c) // UK)
UNITS = [(c, i) for c in range(CHUNKS) for i in range(chunk_tiles(c) // UK)]

TURNED = [SB_Q, SB_Q + 1, SB_K, SB_K + 1, KV_LAT, Q_NOPE, Q_NOPE + 1, Q_PE, K_NOPE, K_NOPE + 1,
          MEM_K, MEM_Q]
BY_VECTOR = list(range(W_OUT, MEM_Q)) + list(range(MEM_O, CHUNKS))
SPLITS = [("mix", KD), ("q", 4), ("kv", 2), ("mem", KD), ("out", KD), ("memx", KD), ("memo", MEM_HEADS)]
SPLIT0 = {}
_n = 0
for _name, _k in SPLITS:
    SPLIT0[_name] = _n
    _n += _k
SPLIT_K = dict(SPLITS)


def layer(nc, x, mem, positions, norm_mix, w_in, norm_q_lat, w_q_b, norm_kv_lat, w_kv_b,
          norm_mla_out, norm_sb_out, w_out, norm_mem_x, norm_mem_src, w_mem_q, w_mem_kv,
          w_mem_o, norm_ffn, w_group, b_group, w_expert_router, b_expert, w_gate, w_up,
          w_down, norm_final, out):
    ctx = ExitStack()
    sems = {}

    def S(name):
        if name not in sems:
            sems[name] = ctx.enter_context(nc.semaphore(name))
        return sems[name]

    with ctx:
        base = nc.sbuf_base + (-nc.sbuf_base) % 64
        at = [base]
        limit = nc.sbuf_usable_end

        def place(name, shape, dt=F32, offset=None):
            size = 4
            for s in shape[1:]:
                size *= s
            if offset is None:
                offset = at[0]
                at[0] += size + (-size) % 64
            assert offset + size <= limit, (name, offset + size, limit)
            return nc.alloc_sbuf_tensor_at(name, shape, dt, offset=offset)

        x_res = place("x_res", [P, TT, D])
        a_hi_at = at[0]
        a_hi = place("a_hi", [P, KD, SEQ], F32R)
        a_lo_at = at[0]
        a_lo = place("a_lo", [P, KD, SEQ], F32R)
        w_at = at[0]
        w_raw = place("w_raw", [P, RING, UK, UN])
        w_hi = place("w_hi", [P, RING, UK, UN], F32R)
        w_lo = place("w_lo", [P, RING, UK, UN], F32R)
        nat = place("nat", [P, 2, TT, UN])
        km_t = place("km_t", [P, MEM_HEADS, SEQ])
        v_mem = place("v_mem", [P, TT, UN])
        ident = place("ident", [P, P])
        ones = place("ones", [P, P])
        above_at = at[0]
        above = place("above", [P, P])
        sb_mask = place("sb_mask", [P, BLK])
        mla_mask_at = at[0]
        mla_mask = place("mla_mask", [P, BLK])
        before = sb_mask[:, 0:P]
        g_nat_at = at[0]
        g_nat = place("g_nat", [86, P])
        g_t = place("g_t", [P, 86])
        g_ffn = place("g_ffn", [P, KD])
        sums = place("sums", [P, 16])
        rstd = place("rstd", [P, 16])
        rope_cs = place("rope_cs", [P, 2, TT, ROPE // 2])
        small = place("small", [P, 64])
        minus_half = place("minus_half", [P, TT])
        iota32 = place("iota32", [P, SLOTS])
        gate_w = place("gate_w", [P, 2, TT])
        rel = place("rel", [P, 2, TT])
        chunk_ss = place("chunk_ss", [P, TT, 4])
        head_ss = place("head_ss", [P, TT, 2, HEADS])
        head_junk = place("head_junk", [P, HD])
        n_iter = place("n_iter", [P, 3], I32)
        pos_i = place("pos_i", [P, TT], I32)
        e_at = at[0]
        qsb_t = place("qsb_t", [P, HEADS, SEQ])
        ksb_t = place("ksb_t", [P, HEADS, SEQ])
        v_sb = place("v_sb", [P, TT, HEADS * HD])
        q_t = place("q_t", [P, HEADS, SEQ])
        qpe_t = place("qpe_t", [P, HEADS // 2, SEQ])
        k_t = place("k_t", [P, HEADS, SEQ])
        kpe_t = place("kpe_t", [P, SEQ])
        v_mla = place("v_mla", [P, TT, HEADS * HD])
        o_at = at[0]
        o_cat = place("o_cat", [P, TT, D])
        c_q = place("c_q", [P, TT, Q_RANK])
        c_kv = place("c_kv", [P, TT, KV_RANK + ROPE])
        mem_sb = place("mem_sb", [P, TT, D], offset=o_at)
        gu = [place("gu0", [P, 2, 2, KD // 2, FE], offset=e_at),
              place("gu1", [P, 2, 2, KD // 2, FE], offset=w_at)]
        down0 = place("down0", [P, 2, D], offset=e_at + 4 * 16 * 1024)
        down1 = place("down1", [P, 2, D], offset=a_lo_at)
        a2_hi = place("a2_hi", [P, KD, SEQ], F32R, offset=e_at)
        a2_lo = place("a2_lo", [P, KD, SEQ], F32R, offset=e_at + 16 * 1024)
        qm_t = place("qm_t", [P, MEM_HEADS, SEQ], offset=e_at + 36 * 1024)
        at[0] -= (Q_RANK + KV_RANK + ROPE) * TT * 4
        p_mla = place("p_mla", [P, 2, BLK])
        pt_mla = place("pt_mla", [P, BLK])
        sb_e = place("sb_e", [P, BLK])
        sb_l = place("sb_l", [P, BLK])
        sb_b = place("sb_b", [P, 2, BLK])
        sb_m = place("sb_m", [P, BLK])
        sb_a = place("sb_a", [P, BLK])
        row_m = place("row_m", [P, HEADS, TT])
        row_n = place("row_n", [P, HEADS, TT])
        row_s = place("row_s", [P, HEADS, TT])
        row_r = place("row_r", [P, HEADS, TT])
        pm = place("pm", [P, 2, TT, SEQ], offset=a_hi_at)
        pmt = place("pmt", [P, 2, TT, SEQ], offset=a_hi_at + 4096)
        mrow = place("mrow", [P, 4, MEM_HEADS, TT], offset=a_hi_at + 8192)
        o_mem = place("o_mem", [P, TT, UN], offset=a_hi_at + 16 * 1024 + 8192)
        h_t = place("h_t", [P, 2, 4, SEQ], offset=a_hi_at + 4096)
        junk1 = place("junk1", [P, UN], offset=e_at + 40 * 1024)
        junk2 = place("junk2", [P, UN], offset=a_hi_at + 12 * 1024)
        end_at = e_at + 80 * 1024
        w_r = place("w_r", [P, KD, 36], offset=end_at)
        b_r = place("b_r", [P, 36], offset=end_at + 2304)
        rt = place("rt", [P, 768], offset=end_at + 2496)
        xe = place("xe", [P, KD, SLOTS], offset=end_at)
        x_slots = place("x_slots", [P, UN], offset=end_at + 2048)
        y_sb = place("y_sb", [P, UN], offset=end_at + 4096)
        comb_0 = place("comb_0", [P, TT, SLOTS], offset=g_nat_at)
        hot = place("hot", [P, TT, SLOTS], offset=g_nat_at + 256)
        hot_f = place("hot_f", [P, 2, TT, SLOTS], offset=above_at)
        turned_6 = place("turned_6", [P, TT + 1, P], offset=mla_mask_at)
        comb = place("comb", [P, TT, NJ, SLOTS], offset=end_at + 6144)
        sg = place("sg", [P, P], offset=end_at + 6144 + 1024)
        act = place("act", [P, P], offset=end_at + 6144 + 1536)
        g_fin = place("g_fin", [P, D], offset=e_at)
        squares = place("squares", [P, UN], offset=w_at)
        comb_t, act_t = turned_6[:, 0:TT, :], turned_6[:, TT, :]
        h_nat = place("h_nat", [P, TT, KD, P], offset=a_hi_at)

        ps = [ctx.enter_context(nc.psum_tensor(f"ps{i}", [P, 512], F32)) for i in range(8)]

        def unit_src(c, i):
            rows = slice(i * UK * P, (i + 1) * UK * P)
            def cols(w, n0, n=UN):
                return w[0, rows, n0:n0 + n].rearrange("(k p) n -> p k n", p=P)
            def headed(w, width, h0, nh, lo, hi):
                return w[0, rows, h0 * width:(h0 + nh) * width].rearrange(
                    "(k p) (h c) -> p k h c", p=P, c=width)[:, :, :, lo:hi]
            if MEM_K <= c <= MEM_V:
                return [cols(w_mem_kv, (c - MEM_K) * UN)]
            if c < Q_NOPE:
                n0 = {Q_LAT: 0, KV_LAT: Q_RANK}.get(c, Q_RANK + KV_RANK + ROPE + (c - SB_Q) * UN)
                return [cols(w_in, n0, chunk_cols(c))]
            if c < Q_PE:
                return [headed(w_q_b, HD + ROPE, 4 * (c - Q_NOPE), 4, 0, HD)]
            if c == Q_PE:
                return [headed(w_q_b, HD + ROPE, 0, HEADS, HD, HD + ROPE)]
            if c < V_MLA:
                return [headed(w_kv_b, 2 * HD, 4 * (c - K_NOPE), 4, 0, HD)]
            if c < W_OUT:
                return [headed(w_kv_b, 2 * HD, 4 * (c - V_MLA), 4, HD, 2 * HD)]
            if c < MEM_Q:
                return [cols(w_out, (c - W_OUT) * UN)]
            if c == MEM_Q:
                return [cols(w_mem_q, 0)]
            return [cols(w_mem_o, (c - MEM_O) * UN)]

        def chunk_out(c):
            if c in BY_VECTOR:
                return S("chunk_added"), BY_VECTOR.index(c) + 1
            return S("chunk_copied"), sum(1 for d in range(c + 1) if d not in BY_VECTOR)

        def turned_dst(c):
            if c == MEM_K:
                return km_t[:, :, :]
            if c in (SB_Q, SB_Q + 1):
                return qsb_t[:, 4 * (c - SB_Q):4 * (c - SB_Q) + 4, :]
            if c in (SB_K, SB_K + 1):
                return ksb_t[:, 4 * (c - SB_K):4 * (c - SB_K) + 4, :]
            if c in (Q_NOPE, Q_NOPE + 1):
                return q_t[:, 4 * (c - Q_NOPE):4 * (c - Q_NOPE) + 4, :]
            if c == Q_PE:
                return qpe_t[:, :, :]
            if c in (K_NOPE, K_NOPE + 1):
                return k_t[:, 4 * (c - K_NOPE):4 * (c - K_NOPE) + 4, :]
            return qsb_t[:, 0:4, :]

        qm_t = qsb_t
        bank0 = {}
        n = 0
        for c in TURNED:
            bank0[c] = n
            n += 1 if c == KV_LAT else 2

        def acc_bank(c):
            return 2 if c in (MEM_K, MEM_V) else 2 * (c % 2)

        def bank_user(c):
            return {MEM_K: V_MLA, MEM_V: MEM_K, W_OUT: MEM_V, W_OUT + 1: V_MLA + 1}.get(c, c - 2)

        SS_MEM, SS_X, SS_Q, SS_KV, SS_A, SS_B, SS_X1, SS_X2, = range(0, 16, 2)

        block = ctx.enter_context(nc.Block())

        @block.sync
        def _(sp):
            for u, (c, i) in enumerate(UNITS):
                if u >= RING:
                    sp.wait_ge(S("w_split"), u - RING + 1)
                dst = w_raw[:, u % RING, :, 0:chunk_cols(c)]
                (src,) = unit_src(c, i)
                if len(src.shape) == 4:
                    for k in range(UK):
                        sp.dma_start(dst[:, k, :].rearrange("p (h c) -> p h c", h=src.shape[2]),
                                     src[:, k]).then_inc(S(f"w_loaded{u % RING}"), 16)
                else:
                    sp.dma_start(dst, src).then_inc(S(f"w_loaded{u % RING}"), 16)

            def load_gate_up(e, side, used=None, halves=(0, 1)):
                wg = w_gate[0, e].rearrange("(p k) f -> p (k f)", k=KD)
                wu = w_up[0, e].rearrange("(p k) f -> p (k f)", k=KD)
                half = KD // 2 * FE
                for b in halves:
                    if used is not None:
                        sp.wait_ge(S(f"gu_used{b}"), used)
                    for m, w in enumerate((wg, wu)):
                        sp.dma_start(gu[side][:, b, m].rearrange("p k f -> p (k f)"),
                                     w[:, b * half:(b + 1) * half]).then_inc(
                                         S(f"gu_loaded{side}{b}"), 16)

            def load_down(e, used=None):
                wd = w_down[0, e].rearrange("(j p) d -> p j d", p=P)
                for b, dst in enumerate((down0, down1)):
                    if used is not None:
                        sp.wait_ge(S(f"down_used{b}"), used)
                    elif b == 1:
                        sp.wait_ge(S("w_used"), len(UNITS))
                        sp.wait_ge(S("w_split"), len(UNITS))
                    sp.dma_start(dst[:, :, :], wd[:, 2 * b:2 * b + 2, :]).then_inc(
                        S(f"down_loaded{b}"), 16)

            sp.wait_ge(S("w_used"), UNIT0[MEM_O])
            sp.wait_ge(S("mem_scores"), MEM_HEADS)
            load_gate_up(0, 0)
            load_down(0)
            load_gate_up(1, 1)
            for e in range(2, AHEAD):
                load_gate_up(e, e % 2, e - 1)
                load_down(e - 1, e - 1)
            load_gate_up(AHEAD, AHEAD % 2, AHEAD - 1, halves=(0,))
            load_down(AHEAD - 1, AHEAD - 1)
            load_gate_up(AHEAD, AHEAD % 2, AHEAD - 1, halves=(1,))
            load_down(AHEAD, AHEAD)
            with sp.Fori(0, (EXPERTS - AHEAD - 1) // 2) as i:
                for m in range(2):
                    e = 2 * i + AHEAD + 1 + m
                    load_gate_up(e, (AHEAD + 1 + m) % 2, 2 * i + AHEAD + m)
                    load_down(e, 2 * i + AHEAD + 1 + m)
            sp.wait_ge(S("routed"), 1)
            total = sp.value_load(n_iter[0:1, 0:1], min_val=EXPERTS, max_val=MAX_PASSES * EXPERTS)
            with sp.If(total > EXPERTS):
                with sp.Fori(EXPERTS - 1, total - 1, EXPERTS) as before_:
                    with sp.Fori(0, EXPERTS // 2) as i:
                        for side in range(2):
                            load_gate_up(2 * i + side, side, before_ + 2 * i + side)
                            load_down(2 * i + side, before_ + 2 * i + 1 + side)
            sp.wait_ge(S("gu_used1"), total)
            sp.dma_start(g_fin[:, :], norm_final.rearrange("(a d) -> a d", a=1).to_broadcast([P, D])
                         ).then_inc(S("final_gain_loaded"), 16)
            for t in range(TT):
                for f in range(2):
                    sp.wait_ge(S("final"), 2 * t + f + 1)
                    cols = slice(f * D // 2, (f + 1) * D // 2)
                    sp.dma_start(out[0, t * P:(t + 1) * P, cols], x_res[:, t, cols]).then_inc(
                        S("stored"), 16)
            sp.wait_ge(S("stored"), 16 * 2 * TT)

        @block.tensor
        def _(pe):
            def split_turn(name, src, k_from=0, k_to=None):
                k0, kn = SPLIT0[name], SPLIT_K[name]
                for kk in range(k_from // 2, (kn if k_to is None else k_to) // 2):
                    b = k0 // 2 + kk
                    if b >= 4:
                        pe.wait_ge(S("split_lo"), 2 * (b - 4) + 2)
                    for i in range(2):
                        for t in range(TT):
                            k = 2 * kk + i
                            mm = pe.transpose(ps[4 + b % 4][:, i * SEQ + t * P:i * SEQ + (t + 1) * P],
                                              src[:, t, k * P:(k + 1) * P], ident[:, :])
                    mm.then_inc(S("split_turned"), 1)

            def project_units(c, units, a0=0, hi=a_hi, lo=a_lo):
                kn, n = chunk_tiles(c), chunk_cols(c)
                acc = [ps[acc_bank(c) + t] for t in range(TT)]
                for i in units:
                    if i == 0 and c >= 2:
                        pe.wait_ge(*chunk_out(bank_user(c)))
                    u = UNIT0[c] + i
                    pe.wait_ge(S("w_rounded"), u + 1)
                    pe.wait_ge(S("w_split"), u + 1)
                    for j in range(UK):
                        k = i * UK + j
                        for t in range(TT):
                            xh = hi[:, a0 + k, t * P:(t + 1) * P]
                            xl = lo[:, a0 + k, t * P:(t + 1) * P]
                            wh, wl = w_hi[:, u % RING, j, 0:n], w_lo[:, u % RING, j, 0:n]
                            pe.matmul(acc[t][:, 0:n], xh, wh, start=(k == 0), stop=False)
                            pe.matmul(acc[t][:, 0:n], xh, wl, start=False, stop=False)
                            mm = pe.matmul(acc[t][:, 0:n], xl, wh, start=False, stop=(k == kn - 1))
                    mm.then_inc(S("w_used"), 1)

            def project(c, a0=0, hi=a_hi, lo=a_lo):
                project_units(c, range(chunk_tiles(c) // UK), a0, hi, lo)

            def turn(c):
                j = TURNED.index(c)
                if c in (KV_LAT, Q_PE):
                    pe.wait_ge(S("roped"), 1 if c == KV_LAT else 2)
                else:
                    pe.wait_ge(*chunk_out(c))
                for b in range(1 if c == KV_LAT else 2):
                    m = bank0[c] + b
                    bank = ps[4 + m % 4]
                    if m >= 4:
                        pe.wait_ge(S("turn_copied"), m - 3)
                    for i in range(1 if c == KV_LAT else 2):
                        for t in range(TT):
                            f = 2 * b + i
                            mm = pe.transpose(bank[:, i * SEQ + t * P:i * SEQ + (t + 1) * P],
                                              nat[:, j % 2, t, f * P:(f + 1) * P], ident[:, :])
                    mm.then_inc(S("turned"), 1)

            pe.wait_ge(S("consts"), 1)
            pe.wait_ge(S("gains_loaded"), 8 * 16)
            pe.transpose(ps[0][:, 0:86], g_nat[:, :], ident[0:86, 0:86]).then_inc(S("gains_turned"), 1)
            pe.wait_ge(S("x_loaded"), 16 * TT)
            split_turn("mix", x_res)
            pe.wait_ge(S("gains_copied"), 1)
            pe.wait_ge(S("split_lo"), SPLIT0["mix"] + KD)
            for c in range(Q_LAT, Q_NOPE):
                project(c)
                if SB_Q <= c - 1 < SB_V:
                    turn(c - 1)
            turn(KV_LAT)
            pe.wait_ge(S("turn_copied"), bank0[Q_NOPE])
            split_turn("q", c_q)
            split_turn("kv", c_kv)
            pe.wait_ge(S("split_lo"), SPLIT0["kv"] + 2)
            for c in range(Q_NOPE, MEM_K):
                project(c, a0=0 if c <= Q_PE else 4)
                if c - 1 in TURNED:
                    turn(c - 1)

            def scores(h):
                s, z = ps[0], ps[1]
                if h == 0:
                    pe.wait_ge(*chunk_out(V_MLA + 1))
                else:
                    pe.wait_ge(S("mla_masked"), h)
                    pe.wait_ge(S("sb_logs"), h)
                po = ROPE * (h % 2)
                for t in range(TT):
                    n = (t + 1) * P
                    o = s[:, 0:P] if t == 0 else s[:, P:BLK]
                    q = slice(t * P, (t + 1) * P)
                    pe.matmul(o, q_t[:, h, q], k_t[:, h, 0:n], start=True, stop=False)
                    mm = pe.matmul(o, qpe_t[po:po + ROPE, h // 2, q], kpe_t[po:po + ROPE, 0:n],
                                   start=False, stop=True)
                mm.then_inc(S("mla_scored"), 1)
                pe.matmul(z[:, 0:SEQ], ksb_t[:, h, 0:P], qsb_t[:, h, :], start=True, stop=True)
                pe.matmul(z[:, SEQ:BLK], ksb_t[:, h, P:SEQ], qsb_t[:, h, P:SEQ], start=True,
                          stop=True).then_inc(S("sb_scored"), 1)

            def turn_probs(h):
                pe.wait_ge(S("mla_probs"), h + 1)
                if h >= 1:
                    pe.wait_ge(S("probs_copied"), h)
                for i in range(3):
                    mm = pe.transpose(ps[4][:, i * P:(i + 1) * P], p_mla[:, h % 2, i * P:(i + 1) * P],
                                      ident[:, :])
                mm.then_inc(S("probs_turned"), 1)

            def later(h):
                pe.wait_ge(S("sb_masked"), h + 1)
                if h >= 1:
                    pe.wait_ge(S("sb_summed"), h)
                m = sb_m
                pe.matmul(ps[5][:, 0:SEQ], above[:, :], m[:, 0:SEQ], start=True, stop=False)
                pe.matmul(ps[5][:, P:SEQ], ones[:, :], m[:, SEQ:BLK], start=False, stop=True)
                pe.matmul(ps[5][:, SEQ:BLK], above[:, :], m[:, SEQ:BLK], start=True,
                          stop=True).then_inc(S("sb_later"), 1)

            def values(h):
                o = ps[6]
                if h >= 1:
                    pe.wait_ge(S("o_copied"), h)
                d = slice(h * HD, (h + 1) * HD)
                for m, (ready, w, v) in enumerate((("probs_copied", pt_mla, v_mla),
                                                   ("sb_weights", sb_a, v_sb))):
                    pe.wait_ge(S(ready), h + 1)
                    pe.matmul(o[:, 2 * m * P:(2 * m + 1) * P], w[:, 0:P], v[:, 0, d],
                              start=True, stop=True)
                    pe.matmul(o[:, (2 * m + 1) * P:(2 * m + 2) * P], w[:, P:SEQ], v[:, 0, d],
                              start=True, stop=False)
                    mm = pe.matmul(o[:, (2 * m + 1) * P:(2 * m + 2) * P], w[:, SEQ:BLK],
                                   v[:, 1, d], start=False, stop=True)
                mm.then_inc(S("o_made"), 1)

            pe.wait_ge(S("turn_copied"), bank0[MEM_K])
            scores(0)
            pe.wait_ge(S("mem_loaded"), 16)
            split_turn("mem", mem_sb)
            pe.wait_ge(S("split_lo"), SPLIT0["mem"] + KD)
            mem_units = [(c, i) for c in (MEM_K, MEM_V) for i in range(KD // UK)]
            for i in range(HEADS + 1):
                if i >= 1:
                    turn_probs(i - 1)
                    later(i - 1)
                for c, j in mem_units[2 * i:2 * i + 1]:
                    project_units(c, [j])
                if 1 <= i < HEADS:
                    scores(i)
                for c, j in mem_units[2 * i + 1:2 * i + 2]:
                    project_units(c, [j])
                if i >= 1:
                    values(i - 1)

            pe.wait_ge(S("o_copied"), HEADS)
            turn(MEM_K)
            pe.wait_ge(S("turn_copied"), bank0[MEM_Q])
            pe.wait_ge(S("o_normed"), 2)
            pe.wait_ge(S("o_normed_v"), 2)
            split_turn("out", o_cat)
            pe.wait_ge(S("split_lo"), SPLIT0["out"] + KD)
            for c in range(W_OUT, MEM_Q + 1):
                if c < MEM_Q:
                    project(c)
                if c > W_OUT:
                    pe.wait_ge(*chunk_out(c - 1))
                    k = 4 * (c - 1 - W_OUT)
                    split_turn("memx", x_res, k, k + 4)
            pe.wait_ge(S("split_lo"), SPLIT0["memx"] + KD)
            project(MEM_Q, hi=a2_hi, lo=a2_lo)
            turn(MEM_Q)
            pe.wait_ge(S("turn_copied"), bank0[MEM_Q] + 2)

            def mem_scores(h):
                if h >= 2:
                    pe.wait_ge(S("mem_probs"), h - 1)
                for t in range(TT):
                    mm = pe.matmul(ps[h % 2][:, t * SEQ:(t + 1) * SEQ], qm_t[:, h, t * P:(t + 1) * P],
                                   km_t[:, h, :], start=True, stop=True)
                mm.then_inc(S("mem_scores"), 1)

            def mem_values(h):
                pe.wait_ge(S("mem_probs"), h + 1)
                if h >= 1:
                    pe.wait_ge(S("mem_pt"), h)
                for m in range(2):
                    for t in range(TT):
                        mm = pe.transpose(ps[4][:, m * SEQ + t * P:m * SEQ + (t + 1) * P],
                                          pm[:, h % 2, t, m * P:(m + 1) * P], ident[:, :])
                mm.then_inc(S("mem_pturned"), 1)
                pe.wait_ge(S("mem_pt"), h + 1)
                for t in range(TT):
                    for m in range(2):
                        mm = pe.matmul(ps[5 + t][:, h * HD:(h + 1) * HD],
                                       pmt[:, h % 2, m, t * P:(t + 1) * P],
                                       v_mem[:, m, h * HD:(h + 1) * HD], start=(m == 0), stop=(m == 1))
                mm.then_inc(S("mem_o"), 1)

            for i in range(MEM_HEADS + 1):
                if i < MEM_HEADS:
                    mem_scores(i)
                if i >= 1:
                    mem_values(i - 1)
            pe.wait_ge(S("mem_o_copied"), TT)
            split_turn("memo", o_mem)
            pe.wait_ge(S("split_lo"), SPLIT0["memo"] + MEM_HEADS)

            def router_turn(q):
                pe.wait_ge(*chunk_out(MEM_O + q))
                for b in range(2):
                    if q >= 1:
                        pe.wait_ge(S("h_copied"), 4 * q - 2 + 2 * b)
                    for i in range(2):
                        for t in range(TT):
                            k = 4 * q + 2 * b + i
                            mm = pe.transpose(ps[4 + b][:, i * SEQ + t * P:i * SEQ + (t + 1) * P],
                                              x_res[:, t, k * P:(k + 1) * P], ident[:, :])
                    mm.then_inc(S("h_turned"), 1)

            def router_logits(q):
                pe.wait_ge(S("h_copied"), 4 * q + 4)
                for i in range(4):
                    k = 4 * q + i
                    for t in range(TT):
                        mm = pe.matmul(ps[6 + t][:, 0:36], h_t[:, q % 2, i, t * P:(t + 1) * P],
                                       w_r[:, k, :], start=(k == 0), stop=(k == KD - 1))
                mm.then_inc(S("logits"), 1)

            pe.wait_ge(S("router_loaded"), 4 * 16)
            for c in range(MEM_O, CHUNKS):
                project(c)
                if c - 1 >= MEM_O:
                    router_turn(c - 1 - MEM_O)
                if c - 2 >= MEM_O:
                    router_logits(c - 2 - MEM_O)
            router_turn(3)
            router_logits(2)
            router_logits(3)

            pe.wait_ge(S("chosen"), 1)
            sel = rt[:, 512:512 + TT * EXPERTS].rearrange("p (t e) -> p t e", t=TT)
            pe.wait_ge(*chunk_out(CHUNKS - 1))
            pe.matmul(ps[2][:, 0:EXPERTS], before, sel[:, 0], start=True, stop=True)
            pe.matmul(ps[2][:, EXPERTS:2 * EXPERTS], ones[:, :], sel[:, 0], start=True, stop=False)
            pe.matmul(ps[2][:, EXPERTS:2 * EXPERTS], before, sel[:, 1], start=False, stop=True)
            pe.matmul(ps[3][:, 0:EXPERTS], ones[:, :], sel[:, 0], start=True, stop=False)
            pe.matmul(ps[3][:, 0:EXPERTS], ones[:, :], sel[:, 1], start=False,
                      stop=True).then_inc(S("ranked"), 1)

            def gather(n, first=False):
                pe.wait_ge(S("hot_ready"), n + 1)
                if first:
                    pe.wait_ge(S("h_ready"), TT)
                    pe.wait_ge(S("h_copied"), 16)
                else:
                    pe.wait_ge(S("xe_ready"), n)
                for t in range(TT):
                    for g in range(NJ):
                        mm = pe.matmul(ps[4][g * SLOTS:(g + 1) * SLOTS, :], hot[:, t, :],
                                       h_nat[:, t, 4 * g:4 * g + 4, :].rearrange("p k d -> p (k d)"),
                                       start=(t == 0), stop=(t == TT - 1))
                mm.then_inc(S("gathered"), 1)

            def gather_turn(n):
                pe.wait_ge(S("slots_copied"), n + 1)
                for j in range(NJ):
                    mm = pe.transpose(ps[4][:, j * P:(j + 1) * P], x_slots[:, j * P:(j + 1) * P],
                                      ident[:, :])
                mm.then_inc(S("slots_turned"), 1)

            def gate_up(b, side, loads):
                pe.wait_ge(S(f"gu_loaded{side}{b}"), 32 * loads)
                for kk in range(KD // 2):
                    k = b * (KD // 2) + kk
                    for j in range(NJ):
                        mm = pe.matmul(
                            ps[5][j * SLOTS:(j + 1) * SLOTS, 0:2 * P].rearrange(
                                "s (m f) -> s m f", m=2),
                            xe[:, k, :], gu[side][:, b, :, kk, j * P:(j + 1) * P],
                            start=(k == 0), stop=(k == KD - 1))
                mm.then_inc(S(f"gu_used{b}"), 1)

            def combine(t, g):
                rows = slice(g * SLOTS, (g + 1) * SLOTS)
                return pe.matmul(ps[g][:, :], turned_6[rows, t, :], y_sb[rows, :], start=True, stop=True)

            def expert(n, side, loads, m=None):
                for b in range(2):
                    if m is not None:
                        if b == 0:
                            pe.wait_ge(S("y_copied"), n)
                        else:
                            pe.wait_ge(S("y_added"), TT * m + 1)
                        for g in range(NJ):
                            mm = combine(b, g)
                        mm.then_inc(S("combined"), 1)
                    if b == 0:
                        pe.wait_ge(S("xe_ready"), n + 1)
                        if m is not None:
                            pe.wait_ge(S("act_ready"), n)
                    gate_up(b, side, loads)
                gather(n + 1)
                gather_turn(n + 1)
                pe.wait_ge(S("comb_ready"), TT * (n + 1))
                pe.wait_ge(S("act_ready"), n + 1)
                if m is not None:
                    pe.wait_ge(S("bank6_copied"), n)
                for t in range(TT):
                    mm = pe.transpose(ps[6][:, t * P:(t + 1) * P],
                                      comb[:, t].rearrange("p g s -> p (g s)"), ident[:, :])
                pe.transpose(ps[6][:, TT * P:(TT + 1) * P], act[:, :], ident[:, :]).then_inc(
                    S("bank6_turned"), 1)
                pe.wait_ge(S("bank6_copied"), n + 1)
                if m is not None:
                    pe.wait_ge(S("y_copied"), n)
                for b, w in enumerate((down0, down1)):
                    pe.wait_ge(S(f"down_loaded{b}"), 16 * (n + 1))
                    for jj in range(2):
                        j = 2 * b + jj
                        for g in range(NJ):
                            mm = pe.matmul(ps[7][g * SLOTS:(g + 1) * SLOTS, :],
                                           act_t[:, j * SLOTS:(j + 1) * SLOTS],
                                           w[:, jj, g * UN:(g + 1) * UN],
                                           start=(j == 0), stop=(j == NJ - 1))
                    mm.then_inc(S(f"down_used{b}"), 1)
                if m is not None:
                    pe.wait_ge(S("y_added"), TT * m + TT)

            gather(0, first=True)
            gather_turn(0)
            pe.wait_ge(S("routed"), 1)
            pairs = pe.value_load(n_iter[0:1, 2:3], min_val=EXPERTS // 2 - 1,
                                  max_val=MAX_PASSES * EXPERTS // 2 - 1)
            expert(0, 0, 1)
            with pe.Fori(0, pairs) as i:
                expert(2 * i + 1, 1, i + 1, 2 * i)
                expert(2 * i + 2, 0, i + 2, 2 * i + 1)
            expert(2 * pairs + 1, 1, pairs + 1, 2 * pairs)
            pe.wait_ge(S("y_copied"), 2 * pairs + 2)
            for t in range(TT):
                for g in range(NJ):
                    if t:
                        pe.wait_ge(S("last_added"), g + 1)
                    combine(t, g).then_inc(S("last_combined"), 1)

        @block.scalar
        def _(sc):
            done = [0]

            def rounded(upto):
                for u in range(done[0], min(upto, len(UNITS))):
                    c, i = UNITS[u]
                    n = chunk_cols(c)
                    per = sum(16 * (UK if len(unit_src(*UNITS[v])[0].shape) == 4 else 1)
                              for v in range(u % RING, u + 1, RING))
                    sc.wait_ge(S(f"w_loaded{u % RING}"), per)
                    if u >= RING:
                        sc.wait_ge(S("w_used"), u - RING + 1)
                    sc.activation(w_hi[:, u % RING, :, 0:n], w_raw[:, u % RING, :, 0:n],
                                  ACT.Copy).then_inc(S("w_rounded"), 1)
                done[0] = max(done[0], upto)

            def square(src, acc, junk):
                sc.activation(junk, src, ACT.Square, accum_out=acc).then_inc(S("squared"), 1)

            sq = [0]

            def squares_of(src, col, junk):
                for t in range(TT):
                    square(src[:, t], sums[:, col + t:col + t + 1], junk)
                    sq[0] += 1
                    sc.wait_ge(S("squared"), sq[0])

            def split_head(name, g0, used=0, a0=0, hi=a_hi, k_from=0, k_to=None):
                k0, kn = SPLIT0[name], SPLIT_K[name]
                if used:
                    sc.wait_ge(S("w_used"), used)
                for k in range(k_from, kn if k_to is None else k_to):
                    b = (k0 + k) // 2
                    sc.wait_ge(S("split_turned"), b + 1)
                    i = k % 2
                    sc.activation(hi[:, a0 + k, :], ps[4 + b % 4][:, i * SEQ:(i + 1) * SEQ], ACT.Copy,
                                  scale=1.0 if g0 is None else g_t[:, g0 + k:g0 + k + 1]
                                  ).then_inc(S("split_hi"), 1)

            def chunk_copy(c, dst, col=None):
                sc.wait_ge(S("w_used"), UNIT0[c + 1])
                for t in range(TT):
                    ins = sc.activation(dst(t), ps[acc_bank(c) + t][:, 0:chunk_cols(c)], ACT.Copy,
                                        scale=rstd[:, col + t:col + t + 1])
                ins.then_inc(S("chunk_copied"), 1)

            def to_nat(c, col):
                j = TURNED.index(c)
                if j >= 2:
                    sc.wait_ge(S("turned"), bank0[TURNED[j - 1]])
                chunk_copy(c, lambda t: nat[:, j % 2, t, :], col)

            def x_squares(q, chunk_junk):
                for t in range(TT):
                    if xsq[0]:
                        sc.wait_ge(S("x_squared"), xsq[0])
                    sc.activation(chunk_junk[:, :], x_res[:, t, q * UN:(q + 1) * UN], ACT.Square,
                                  accum_out=chunk_ss[:, t, q:q + 1]).then_inc(S("x_squared"), 1)
                    xsq[0] += 1

            xsq = [0]
            for t in range(TT):
                sc.dma_start(x_res[:, t, :], x[0, t * P:(t + 1) * P, :]).then_inc(S("x_loaded"), 16)
            for gain, r0, rows in ((norm_mix, 0, 16), (norm_mem_src, 16, 16), (norm_mem_x, 32, 16),
                                   (norm_q_lat, 48, 4), (norm_kv_lat, 52, 2), (norm_mla_out, 54, 8),
                                   (norm_sb_out, 62, 8), (norm_ffn, 70, 16)):
                sc.dma_start(g_nat[r0:r0 + rows, :], gain[0].rearrange("(k p) -> k p", p=P)
                             ).then_inc(S("gains_loaded"), 16)
            for t in range(TT):
                sc.dma_start(pos_i[:, t:t + 1], positions[0, t * P:(t + 1) * P].rearrange(
                    "(p a) -> p a", a=1)).then_inc(S("pos_loaded"), 16)
            sc.dma_start(g_ffn[:, :], norm_ffn[0].rearrange("(p k) -> p k", k=KD)).then_inc(
                S("ffn_gain_loaded"), 16)
            sc.preload_act_table_set("natural_log_exp_and_others")
            sc.wait_ge(S("gains_turned"), 1)
            sc.activation(g_t[:, :], ps[0][:, 0:86], ACT.Copy).then_inc(S("gains_copied"), 1)
            sc.wait_ge(S("gains_copied"), 1)
            rounded(RING)
            split_head("mix", 0)
            junk = v_mla[:, :, :].rearrange("p t d -> p (t d)")
            squares_of(x_res, SS_X, junk)
            sc.wait_ge(S("angles"), 1)
            sc.activation(rope_cs[:, :, :, :], rope_cs[:, :, :, :], ACT.Sin).then_inc(S("rope_ready"), 1)
            sc.preload_act_table_set("natural_log_exp_and_others")
            sc.wait_ge(S("rstd"), 1)
            for c in range(Q_LAT, Q_NOPE):
                rounded(UNIT0[c + 1] + RING)
                if c == Q_LAT:
                    chunk_copy(c, lambda t: c_q[:, t, :], SS_X)
                    sc.wait_ge(*chunk_out(c))
                    squares_of(c_q, SS_Q, junk[:, 0:Q_RANK])
                elif c == KV_LAT:
                    chunk_copy(c, lambda t: c_kv[:, t, :], SS_X)
                    sc.wait_ge(*chunk_out(c))
                    squares_of(c_kv[:, :, 0:KV_RANK], SS_KV, junk[:, 0:KV_RANK])
                    sc.dma_start(mem_sb[:, :, :], mem[0].rearrange("(t p) d -> p t d", p=P)).then_inc(
                        S("mem_loaded"), 16)
                elif c < SB_V:
                    to_nat(c, SS_X)
                else:
                    n0 = (c - SB_V) * UN
                    chunk_copy(c, lambda t: v_sb[:, t, n0:n0 + UN], SS_X)
            sc.wait_ge(S("mem_loaded"), 16)
            squares_of(mem_sb, SS_MEM, junk)
            split_head("q", 48, UNIT0[Q_NOPE])
            split_head("kv", 52, UNIT0[Q_NOPE], a0=4)
            sc.wait_ge(S("rstd"), 4)
            for c in range(Q_NOPE, MEM_K):
                rounded(UNIT0[c + 1] + RING)
                if c < V_MLA:
                    to_nat(c, SS_Q if c <= Q_PE else SS_KV)
                else:
                    n0 = (c - V_MLA) * UN
                    chunk_copy(c, lambda t: v_mla[:, t, n0:n0 + UN], SS_KV)

            def head_norm(h):
                sc.wait_ge(S("o_copied"), h + 1)
                for t in range(TT):
                    for g in range(2):
                        d = (g * HEADS + h) * HD
                        if steps[0]:
                            sc.wait_ge(S("head_squared"), steps[0])
                        sc.activation(head_junk[:, :], o_cat[:, t, d:d + HD], ACT.Square,
                                      accum_out=head_ss[:, t, g, h:h + 1]).then_inc(
                                          S("head_squared"), 1)
                        steps[0] += 1

            steps = [0]
            split_head("mem", 16, UNIT0[MEM_K])
            for i in range(HEADS + 1):
                rounded(min(UNIT0[MEM_K] + 2 * i, UNIT0[W_OUT]) + RING)
                if i == 4:
                    to_nat(MEM_K, SS_MEM)
                if i >= 1:
                    h = i - 1
                    sc.wait_ge(S("probs_turned"), h + 1)
                    if h >= 1:
                        sc.wait_ge(S("o_made"), h)
                    sc.activation(pt_mla[:, :], ps[4][:, 0:BLK], ACT.Copy).then_inc(
                        S("probs_copied"), 1)
                    sc.wait_ge(S("sb_summed"), h + 1)
                    sc.activation(sb_b[:, h % 2], sb_b[:, h % 2], ACT.Exp).then_inc(S("sb_exp"), 1)
                if i < HEADS:
                    h = i
                    sc.wait_ge(S("mla_max"), h + 1)
                    for t, cols in enumerate((slice(0, P), slice(P, BLK))):
                        ins = sc.activation(p_mla[:, h % 2, cols], p_mla[:, h % 2, cols], ACT.Exp,
                                            bias=row_n[:, h, t:t + 1],
                                            accum_out=row_s[:, h, t:t + 1])
                    ins.then_inc(S("mla_probs"), 1)
                    sc.wait_ge(S("sb_scored"), h + 1)
                    sc.activation(sb_e[:, :], ps[1][:, 0:BLK], ACT.Abs).then_inc(S("sb_abs"), 1)
                    sc.wait_ge(S("sb_abs"), h + 1)
                    sc.activation(sb_e[:, :], sb_e[:, :], ACT.Exp, scale=-SC_SB).then_inc(
                        S("sb_expabs"), 1)
                    sc.wait_ge(S("sb_expabs"), h + 1)
                    if h >= 1:
                        sc.wait_ge(S("sb_logs"), h)
                    sc.activation(sb_l[:, :], sb_e[:, :], ACT.Ln, bias=1.0).then_inc(
                        S("sb_log1p"), 1)
                if i >= 2:
                    head_norm(i - 2)
            head_norm(HEADS - 1)
            chunk_copy(MEM_V, lambda t: v_mem[:, t, :], SS_MEM)
            sc.wait_ge(S("rstd"), 5)
            for g, col in enumerate((SS_A, SS_B)):
                o = o_cat[:, 0, g * HEADS * HD:(g + 1) * HEADS * HD]
                sc.activation(o, o, ACT.Copy, scale=rstd[:, col:col + 1]).then_inc(S("o_normed"), 1)
            split_head("out", 54, UNIT0[W_OUT])
            for c in range(W_OUT, MEM_Q + 1):
                if c < MEM_Q:
                    rounded(UNIT0[c + 1] + RING)
                if c > W_OUT:
                    q = c - 1 - W_OUT
                    split_head("memx", 32, hi=a2_hi, k_from=4 * q, k_to=4 * q + 4)
                    x_squares(q, junk1)
            sc.wait_ge(S("rstd"), 6)
            rounded(UNIT0[MEM_Q + 1] + RING)
            to_nat(MEM_Q, SS_X1)
            sc.wait_ge(S("w_used"), UNIT0[MEM_O])
            for i in range(MEM_HEADS + 1):
                if i < MEM_HEADS:
                    h = i
                    sc.wait_ge(S("mem_max"), h + 1)
                    if h >= 2:
                        sc.wait_ge(S("mem_pturned"), h - 1)
                    for t in range(TT):
                        ins = sc.activation(pm[:, h % 2, t, :], ps[h % 2][:, t * SEQ:(t + 1) * SEQ],
                                            ACT.Exp, bias=mrow[:, 1, h, t:t + 1], scale=SC_SB,
                                            accum_out=mrow[:, 2, h, t:t + 1])
                    ins.then_inc(S("mem_probs"), 1)
                if i >= 1:
                    h = i - 1
                    sc.wait_ge(S("mem_pturned"), h + 1)
                    if h >= 2:
                        sc.wait_ge(S("mem_o"), h - 1)
                    sc.activation(pmt[:, h % 2].rearrange("p m t -> p (m t)"), ps[4][:, :],
                                  ACT.Copy).then_inc(S("mem_pt"), 1)
            split_head("memo", None, UNIT0[MEM_O])
            for c in range(MEM_O, CHUNKS + 1):
                if c < CHUNKS:
                    rounded(UNIT0[c + 1] + RING)
                if c > MEM_O:
                    sc.wait_ge(*chunk_out(c - 1))
                    x_squares(c - 1 - MEM_O, junk2)

            sc.wait_ge(S("rstd"), 7)
            sc.wait_ge(S("w_used"), len(UNITS))
            sc.wait_ge(S("logits"), 4)
            for t in range(TT):
                sc.activation(h_nat[:, t], x_res[:, t, :].rearrange("q (p k) -> q k p", k=KD), ACT.Copy,
                              scale=rstd[:, SS_X2 + t:SS_X2 + t + 1]).then_inc(S("h_ready"), 1)
            sc.wait_ge(S("logits_ready"), 1)
            el = rt[:, 0:8]
            sc.activation(rt[:, 8:16], el, ACT.Exp).then_inc(S("group_exp"), 1)
            sc.wait_ge(S("second_gap"), 1)
            sc.activation(rt[:, 18:20], rt[:, 16:18], ACT.Exp).then_inc(S("second_exp"), 1)

            def slots_copy(n, first=False):
                sc.wait_ge(S("gathered"), n + 1)
                if not first:
                    sc.wait_ge(S("slots_turned"), n)
                sc.activation(x_slots[:, :], ps[4][:, :], ACT.Copy).then_inc(S("slots_copied"), 1)

            def expert(n, m=None):
                sc.wait_ge(S("gu_used1"), n + 1)
                if m is not None:
                    sc.wait_ge(S("act_ready"), n)
                sc.activation(sg[:, :], ps[5][:, 0:P], ACT.Silu).then_inc(S("silu"), 1)
                slots_copy(n + 1)
                sc.wait_ge(S("bank6_turned"), n + 1)
                if m is not None:
                    sc.wait_ge(S("combined"), TT * m + TT)
                    sc.wait_ge(S("down_used1"), n)
                sc.activation(turned_6[:, :, :], ps[6][:, 0:(TT + 1) * P].rearrange(
                    "p (t a) -> p t a", t=TT + 1), ACT.Copy).then_inc(S("bank6_copied"), 1)
                sc.wait_ge(S("down_used1"), n + 1)
                sc.activation(y_sb[:, :], ps[7][:, :], ACT.Copy).then_inc(S("y_copied"), 1)

            slots_copy(0, first=True)
            sc.wait_ge(S("routed"), 1)
            last = sc.value_load(n_iter[0:1, 1:2], min_val=EXPERTS - 1,
                                 max_val=MAX_PASSES * EXPERTS - 1)
            expert(0)
            with sc.Fori(0, last) as m:
                expert(m + 1, m)
            for i in range(TT * NJ):
                t, g = divmod(i, NJ)
                sc.wait_ge(S("last_added"), i + 1)
                if i:
                    sc.wait_ge(S("final_squared"), i)
                sc.activation(squares[:, :], x_res[:, t, g * UN:(g + 1) * UN], ACT.Square,
                              accum_out=chunk_ss[:, t, g:g + 1]).then_inc(S("final_squared"), 1)

        @block.vector
        def _(ve):
            done = [0]
            steps = [0]

            def link(ins):
                steps[0] += 1
                ins.then_inc(S("vector_step"), 1)
                ve.wait_ge(S("vector_step"), steps[0])

            def split_w(upto):
                for u in range(done[0], min(upto, len(UNITS))):
                    n = chunk_cols(UNITS[u][0])
                    ve.wait_ge(S("w_rounded"), u + 1)
                    ve.tensor_tensor(w_lo[:, u % RING, :, 0:n], w_raw[:, u % RING, :, 0:n],
                                     w_hi[:, u % RING, :, 0:n], ALU.subtract).then_inc(
                                         S("w_split"), 1)
                done[0] = max(done[0], upto)

            def split_rest(name, g0, a0=0, hi=a_hi, lo=a_lo, k_from=0, k_to=None):
                k0, kn = SPLIT0[name], SPLIT_K[name]
                for k in range(k_from, kn if k_to is None else k_to):
                    b, i = (k0 + k) // 2, k % 2
                    ve.wait_ge(S("split_hi"), k0 + k - i + 2)
                    ve.scalar_tensor_tensor(
                        out=lo[:, a0 + k, :], in0=ps[4 + b % 4][:, i * SEQ:(i + 1) * SEQ],
                        scalar=1.0 if g0 is None else g_t[:, g0 + k:g0 + k + 1],
                        in1=hi[:, a0 + k, :], op0=ALU.mult, op1=ALU.subtract).then_inc(
                            S("split_lo"), 1)

            def copy_turned(c):
                dst = None if c == KV_LAT else turned_dst(c)
                for b in range(1 if c == KV_LAT else 2):
                    m = bank0[c] + b
                    ve.wait_ge(S("turned"), m + 1)
                    if c == KV_LAT:
                        ve.tensor_copy(kpe_t[:, :], ps[4 + m % 4][:, 0:SEQ]).then_inc(
                            S("turn_copied"), 1)
                    else:
                        ve.tensor_copy(dst[:, 2 * b:2 * b + 2, :].rearrange("p h t -> p (h t)"),
                                       ps[4 + m % 4][:, :]).then_inc(S("turn_copied"), 1)

            def rope(dst1, dst2, x1, x2, heads):
                c = rope_cs[:, 0]
                s = rope_cs[:, 1]
                for t in range(TT):
                    cb = c[:, t:t + 1, :].to_broadcast([P, heads, ROPE // 2])
                    sb = s[:, t:t + 1, :].to_broadcast([P, heads, ROPE // 2])
                    n = heads * ROPE // 2
                    a = rt_a[:, 0, 0:n].rearrange("p (h c) -> p h c", h=heads)
                    b = rt_a[:, 1, 0:n].rearrange("p (h c) -> p h c", h=heads)
                    d = rt_a[:, 2, 0:n].rearrange("p (h c) -> p h c", h=heads)
                    e = rt_a[:, 3, 0:n].rearrange("p (h c) -> p h c", h=heads)
                    ve.tensor_tensor(a, x1(t), cb, ALU.mult)
                    ve.tensor_tensor(b, x2(t), sb, ALU.mult)
                    ve.tensor_tensor(d, x2(t), cb, ALU.mult)
                    link(ve.tensor_tensor(e, x1(t), sb, ALU.mult))
                    ve.tensor_tensor(dst1(t), a, b, ALU.subtract)
                    link(ve.tensor_tensor(dst2(t), d, e, ALU.add))

            rt_a = place("rope_tmp", [P, 4, 256], offset=e_at + 80 * 1024)

            from math import pi
            import numpy as np
            half = ROPE // 2
            inv = small[:, 0:half]
            pf = small[:, 32:34]
            ve.wait_ge(S("inv_freq"), 1)
            ve.wait_ge(S("pos_loaded"), 16 * TT)
            link(ve.tensor_copy(pf, pos_i[:, :]))
            turns = place("rope_turns", [P, TT, ROPE // 2], offset=e_at + 84 * 1024)
            for t in range(TT):
                ins = ve.tensor_scalar(rope_cs[:, 1, t, :], inv, pf[:, t:t + 1], None, ALU.mult)
            link(ins)
            magic = 1.5 * 2.0 ** 23
            c1 = 6.28125
            c2 = float(np.float32(2 * pi - c1))
            c3 = 2 * pi - c1 - c2
            ang, cosv = rope_cs[:, 1], rope_cs[:, 0]
            link(ve.tensor_scalar(turns[:, :, :], ang, 1.0 / (2 * pi), magic, ALU.mult, ALU.add))
            link(ve.tensor_scalar(turns[:, :, :], turns[:, :, :], -magic, None, ALU.add))
            for cc in (c1, c2, c3):
                link(ve.scalar_tensor_tensor(out=ang, in0=turns[:, :, :], scalar=-cc, in1=ang,
                                             op0=ALU.mult, op1=ALU.add))
            link(ve.tensor_scalar(cosv, ang, pi / 2, None, ALU.add))
            link(ve.tensor_scalar(turns[:, :, :], cosv, pi, -2 * pi, ALU.is_gt, ALU.mult))
            link(ve.tensor_tensor(cosv, cosv, turns[:, :, :], ALU.add))
            ve.tensor_scalar(rope_cs[:, :, :, :], rope_cs[:, :, :, :], 3.1415925, -3.1415925, ALU.min,
                             ALU.max).then_inc(S("angles"), 1)
            split_w(RING)
            ve.wait_ge(S("gains_copied"), 1)
            split_rest("mix", 0)
            for c in range(Q_LAT, Q_NOPE):
                split_w(UNIT0[c + 1] + RING)
                if SB_Q <= c - 1 < SB_V:
                    copy_turned(c - 1)
                    if c - 1 == SB_K + 1:
                        j = TURNED.index(KV_LAT)
                        ve.wait_ge(S("rope_ready"), 1)
                        ve.wait_ge(S("turned"), bank0[SB_K + 1])
                        ve.wait_ge(*chunk_out(KV_LAT))
                        kn = nat[:, j % 2]
                        rope(lambda t: kn[:, t:t + 1, 0:half], lambda t: kn[:, t:t + 1, half:ROPE],
                             lambda t: c_kv[:, t:t + 1, KV_RANK:KV_RANK + half],
                             lambda t: c_kv[:, t:t + 1, KV_RANK + half:KV_RANK + ROPE], 1)
                        ve.tensor_copy(kn[:, :, ROPE:2 * ROPE], kn[:, :, 0:ROPE]).then_inc(
                            S("roped"), 1)
            copy_turned(KV_LAT)
            split_rest("q", 48)
            split_rest("kv", 52, a0=4)
            for c in range(Q_NOPE, MEM_K):
                split_w(UNIT0[c + 1] + RING)
                if c == K_NOPE:
                    j = TURNED.index(Q_PE)
                    ve.wait_ge(*chunk_out(Q_PE))
                    qn = nat[:, j % 2].rearrange("p t (h c) -> p t h c", c=ROPE)
                    rope(lambda t: qn[:, t, :, 0:half], lambda t: qn[:, t, :, half:ROPE],
                         lambda t: qn[:, t, :, 0:half], lambda t: qn[:, t, :, half:ROPE], HEADS)
                    ve.tensor_copy(small[:, 62:63], small[:, 33:34]).then_inc(S("roped"), 1)
                if c - 1 in TURNED:
                    copy_turned(c - 1)

            ve.wait_ge(S("w_used"), UNIT0[MEM_K])
            for i in range(HEADS + 1):
                if i >= 1:
                    split_w(min(UNIT0[MEM_K] + 2 * i, UNIT0[W_OUT]) + RING)
                    h = i - 1
                    ve.wait_ge(S("sb_later"), h + 1)
                    ve.tensor_tensor(sb_b[:, h % 2], ps[5][:, 0:BLK], sb_b[:, h % 2],
                                     ALU.add).then_inc(S("sb_summed"), 1)
                if i < HEADS:
                    h = i
                    ve.wait_ge(S("mla_scored"), h + 1)
                    if h >= 2:
                        ve.wait_ge(S("probs_turned"), h - 1)
                    ve.scalar_tensor_tensor(out=p_mla[:, h % 2], in0=ps[0][:, 0:BLK], scalar=SC_MLA,
                                            in1=mla_mask[:, :], op0=ALU.mult, op1=ALU.add).then_inc(
                                                S("mla_masked"), 1)
                    ve.wait_ge(S("mla_masked"), h + 1)
                    ve.tensor_reduce(row_m[:, h, 0:1], p_mla[:, h % 2, 0:P], AX, ALU.max)
                    link(ve.tensor_reduce(row_m[:, h, 1:2], p_mla[:, h % 2, P:BLK], AX, ALU.max))
                    ve.tensor_scalar(row_n[:, h, :], row_m[:, h, :], -1.0, None, ALU.mult).then_inc(
                        S("mla_max"), 1)
                    if h == 0:
                        split_rest("mem", 16)
                        split_w(UNIT0[MEM_K] + RING)
                    ve.wait_ge(S("sb_log1p"), h + 1)
                    if h >= 2:
                        ve.wait_ge(S("sb_weights"), h - 1)
                    link(ve.tensor_scalar(sb_b[:, h % 2], ps[1][:, 0:BLK], SC_SB, 0.0, ALU.mult,
                                          ALU.min))
                    link(ve.tensor_tensor(sb_b[:, h % 2], sb_b[:, h % 2], sb_l[:, :],
                                          ALU.subtract))
                    if h >= 1:
                        ve.wait_ge(S("sb_later"), h)
                    ve.scalar_tensor_tensor(out=sb_m[:, :], in0=ps[1][:, 0:BLK],
                                            scalar=-SC_SB, in1=sb_b[:, h % 2], op0=ALU.mult,
                                            op1=ALU.add).then_inc(S("sb_logs"), 1)
                if i >= 1:
                    h = i - 1
                    ve.wait_ge(S("o_made"), h + 1)
                    link(ve.reciprocal(row_r[:, h, :], row_s[:, h, :]))
                    o = ps[6]
                    for t in range(TT):
                        ve.tensor_scalar(o_cat[:, t, h * HD:(h + 1) * HD], o[:, t * P:(t + 1) * P],
                                         row_r[:, h, t:t + 1], None, ALU.mult)
                    ve.tensor_copy(o_cat[:, :, (HEADS + h) * HD:(HEADS + h + 1) * HD],
                                   o[:, 2 * P:4 * P].rearrange("p (t d) -> p t d", t=TT)).then_inc(
                                       S("o_copied"), 1)
            copy_turned(MEM_K)
            ve.wait_ge(S("head_squared"), 4 * HEADS)
            for g, col in enumerate((SS_A, SS_B)):
                ins = ve.tensor_reduce(sums[:, col:col + TT].rearrange("p (t a) -> p t a", a=1),
                                       head_ss[:, :, g, :], AX, ALU.add)
            ins.then_inc(S("sums_made"), 1)
            ve.wait_ge(S("rstd"), 5)
            for g, col in enumerate((SS_A, SS_B)):
                o = o_cat[:, 1, g * HEADS * HD:(g + 1) * HEADS * HD]
                ve.tensor_scalar(o, o, rstd[:, col + 1:col + 2], None, ALU.mult).then_inc(
                    S("o_normed_v"), 1)
            split_rest("out", 54)

            def add_chunk(c, n0):
                ve.wait_ge(S("w_used"), UNIT0[c + 1])
                for t in range(TT):
                    xs = x_res[:, t, n0:n0 + UN]
                    ins = ve.tensor_tensor(xs, ps[acc_bank(c) + t][:, :], xs, ALU.add)
                ins.then_inc(S("chunk_added"), 1)

            def x_sums(col, squares_):
                ve.wait_ge(S("x_squared"), squares_)
                ve.tensor_reduce(sums[:, col:col + TT].rearrange("p (t a) -> p t a", a=1),
                                 chunk_ss[:, :, :], AX, ALU.add).then_inc(S("sums_made"), 1)

            for c in range(W_OUT, MEM_Q + 1):
                if c < MEM_Q:
                    split_w(UNIT0[c + 1] + RING)
                    add_chunk(c, (c - W_OUT) * UN)
                if c > W_OUT:
                    q = c - 1 - W_OUT
                    split_rest("memx", 32, hi=a2_hi, lo=a2_lo, k_from=4 * q, k_to=4 * q + 4)
            x_sums(SS_X1, 4 * TT)
            split_w(UNIT0[MEM_Q + 1] + RING)
            copy_turned(MEM_Q)
            for i in range(MEM_HEADS):
                ve.wait_ge(S("mem_scores"), i + 1)
                link(ve.tensor_reduce(mrow[:, 0, i, :], ps[i % 2][:, :].rearrange(
                    "p (t m) -> p t m", t=TT), AX, ALU.max))
                ve.tensor_scalar(mrow[:, 1, i, :], mrow[:, 0, i, :], -SC_SB, None, ALU.mult).then_inc(
                    S("mem_max"), 1)
            ve.wait_ge(S("mem_probs"), MEM_HEADS)
            link(ve.reciprocal(mrow[:, 3], mrow[:, 2]))
            ve.wait_ge(S("mem_o"), MEM_HEADS)
            for t in range(TT):
                ve.tensor_tensor(o_mem[:, t, :].rearrange("p (h d) -> p h d", h=MEM_HEADS),
                                 ps[5 + t][:, :].rearrange("p (h d) -> p h d", h=MEM_HEADS),
                                 mrow[:, 3, :, t:t + 1].to_broadcast([P, MEM_HEADS, HD]),
                                 ALU.mult).then_inc(S("mem_o_copied"), 1)
            split_rest("memo", None)
            for c in range(MEM_O, CHUNKS + 1):
                if c < CHUNKS:
                    split_w(UNIT0[c + 1] + RING)
                    add_chunk(c, (c - MEM_O) * UN)
                if c > MEM_O:
                    q = c - 1 - MEM_O
                    for i in range(4):
                        ve.wait_ge(S("h_turned"), 2 * q + i // 2 + 1)
                        if q >= 2:
                            ve.wait_ge(S("logits"), q - 1)
                        ve.tensor_scalar(h_t[:, q % 2, i, :],
                                         ps[4 + i // 2][:, i % 2 * SEQ:(i % 2 + 1) * SEQ],
                                         g_t[:, 70 + 4 * q + i:71 + 4 * q + i], None,
                                         ALU.mult).then_inc(S("h_copied"), 1)
            x_sums(SS_X2, 8 * TT)

            def field(a, *dims):
                n = 1
                for d in dims:
                    n *= d
                v = rt[:, a:a + n]
                names = "abcd"[:len(dims)]
                if len(dims) > 1:
                    v = v.rearrange(f"p ({' '.join(names)}) -> p {' '.join(names)}",
                                    **{m: d for m, d in zip(names, dims)})
                return v

            def bc(v, *shape):
                return v.to_broadcast([P, *shape])

            lg = field(32, TT, 36)
            gl, el = lg[:, :, 0:GROUPS], lg[:, :, GROUPS:36]
            gm = field(104, TT, 1)
            gsum = field(106, TT, 1)
            gx, gexp = field(0, TT, GROUPS), field(8, TT, GROUPS)
            gap, r2 = field(16, TT), field(18, TT)
            ghot = field(112, TT, GROUPS)
            first_of = field(120, TT, GROUPS)
            best = field(128, TT, 1)
            prod = field(160, TT, GROUPS, PER_GROUP)
            cand = field(224, TT, PER_GROUP)
            m1, m2 = field(240, TT, 1), field(242, TT, 1)
            e1 = field(248, TT, PER_GROUP)
            hot1 = field(264, TT, PER_GROUP)
            hot2 = field(280, TT, PER_GROUP)
            den = field(296, TT)
            pg = field(298, TT)
            pick1 = field(320, TT, GROUPS, PER_GROUP)
            pick2 = field(384, TT, GROUPS, PER_GROUP)
            sel = field(512, TT, EXPERTS)
            row = field(576, TT, EXPERTS)
            tmpr = field(640, TT, EXPERTS)
            cnt = field(704, 8)
            falling = field(720, PER_GROUP)
            row0 = field(736, EXPERTS)

            ve.wait_ge(S("rstd"), 7)
            ve.wait_ge(S("logits"), 4)
            ve.wait_ge(S("router_consts"), 2)
            for t in range(TT):
                ins = ve.scalar_tensor_tensor(out=lg[:, t, :], in0=ps[6 + t][:, 0:36],
                                              scalar=rstd[:, SS_X2 + t:SS_X2 + t + 1],
                                              in1=b_r[:, :], op0=ALU.mult, op1=ALU.add)
            link(ins)
            link(ve.tensor_reduce(gm, gl, AX, ALU.max))
            ve.tensor_tensor(gx, gl, bc(gm, TT, GROUPS), ALU.subtract).then_inc(S("logits_ready"), 1)

            def first_hot(dst, values, top, scratch_, n, base_):
                link(ve.tensor_tensor(scratch_, values, bc(top, TT, n), ALU.is_equal))
                f = falling[:, 0:n].rearrange("p (a b) -> p a b", a=1)
                fb = bc(f, TT, n)
                link(ve.tensor_tensor(scratch_, scratch_, fb, ALU.mult))
                link(ve.tensor_reduce(best, scratch_, AX, ALU.max))
                link(ve.tensor_tensor(dst, fb, bc(best, TT, n), ALU.is_equal))

            first_hot(ghot, gl, gm, first_of, GROUPS, 0)
            gh4 = ghot.rearrange("p t (g e) -> p t g e", e=1)
            for t in range(TT):
                ins = ve.tensor_tensor(prod[:, t], el[:, t].rearrange("p (g e) -> p g e", g=GROUPS),
                                       bc(gh4[:, t], GROUPS, PER_GROUP), ALU.mult)
            link(ins)
            link(ve.tensor_reduce(cand, prod.rearrange("p t g e -> p t e g"), AX, ALU.add))
            link(ve.tensor_reduce(m1, cand, AX, ALU.max))
            first_hot(hot1, cand, m1, e1, PER_GROUP, 0)
            link(ve.scalar_tensor_tensor(out=cand, in0=hot1, scalar=-3.0e38, in1=cand, op0=ALU.mult,
                                         op1=ALU.add))
            link(ve.tensor_reduce(m2, cand, AX, ALU.max))
            ve.tensor_tensor(gap.rearrange("p (t a) -> p t a", a=1), m2, m1, ALU.subtract).then_inc(
                S("second_gap"), 1)
            first_hot(hot2, cand, m2, e1, PER_GROUP, 0)
            for t in range(TT):
                for hot_n, pick in ((hot1, pick1), (hot2, pick2)):
                    hb = hot_n[:, t:t + 1, :]
                    ins = ve.tensor_tensor(pick[:, t], bc(hb, GROUPS, PER_GROUP),
                                           bc(gh4[:, t], GROUPS, PER_GROUP), ALU.mult)
            link(ins)
            p1 = pick1.rearrange("p t g e -> p t (g e)")
            p2 = pick2.rearrange("p t g e -> p t (g e)")
            ve.tensor_tensor(sel, p1, p2, ALU.add).then_inc(S("chosen"), 1)
            ve.wait_ge(S("group_exp"), 1)
            ve.wait_ge(S("second_exp"), 1)
            link(ve.tensor_reduce(gsum, gexp, AX, ALU.add))
            link(ve.tensor_scalar(den, r2, 1.0, None, ALU.add))
            link(ve.tensor_tensor(den, den, gsum.rearrange("p t a -> p (t a)"), ALU.mult))
            link(ve.reciprocal(gate_w[:, 0, :], den))
            link(ve.tensor_tensor(gate_w[:, 1, :], gate_w[:, 0, :], r2, ALU.mult))
            ve.wait_ge(S("ranked"), 1)
            rank = ps[2][:, 0:TT * EXPERTS].rearrange("p (t e) -> p t e", t=TT)
            link(ve.tensor_scalar(row, rank, -(SLOTS - 1) / 2.0, 1.0 / SLOTS, ALU.add, ALU.mult))
            link(ve.tensor_scalar(row, row, magic, -magic, ALU.add, ALU.add))
            link(ve.tensor_scalar(row, row, float(SLOTS * EXPERTS - SLOTS), None, ALU.mult))
            link(ve.tensor_tensor(row, row, rank, ALU.add))
            r0 = row0.rearrange("p (a e) -> p a e", a=1)
            link(ve.tensor_tensor(row, row, bc(r0, TT, EXPERTS), ALU.add))
            for i, pk in enumerate((p1, p2)):
                link(ve.tensor_tensor(tmpr, row, pk, ALU.mult))
                link(ve.tensor_reduce(rel[:, i, :].rearrange("p (t a) -> p t a", a=1), tmpr, AX,
                                      ALU.add))
            link(ve.tensor_reduce(cnt[:, 0:1], ps[3][:, 0:EXPERTS], AX, ALU.max))
            link(ve.tensor_scalar(cnt[:, 0:1], cnt[:, 0:1], (SLOTS - 1) / 2.0, 1.0 / SLOTS, ALU.add,
                                  ALU.mult))
            link(ve.tensor_scalar(cnt[:, 0:1], cnt[:, 0:1], magic, -magic, ALU.add, ALU.add))
            link(ve.tensor_scalar(cnt[:, 0:1], cnt[:, 0:1], float(EXPERTS), None, ALU.mult))
            ve.tensor_scalar(cnt[:, 1:2], cnt[:, 0:1], -1.0, None, ALU.add)
            link(ve.tensor_scalar(cnt[:, 2:3], cnt[:, 0:1], 0.5, -1.0, ALU.mult, ALU.add))
            ve.tensor_copy(n_iter[:, :], cnt[:, 0:3]).then_inc(S("routed"), 1)

            def pick_hot(n):
                it = iota32[:, :].rearrange("p (a s) -> p a s", a=1)
                for i in range(2):
                    rb = rel[:, i, :].rearrange("p (t a) -> p t a", a=1)
                    ve.tensor_tensor(hot_f[:, i], bc(it, TT, SLOTS), bc(rb, TT, SLOTS),
                                     ALU.is_equal).then_inc(S("pick_hot"), 1)
                ve.wait_ge(S("pick_hot"), 2 * (n + 1))
                ve.tensor_tensor(hot[:, :, :], hot_f[:, 0], hot_f[:, 1], ALU.add).then_inc(
                    S("hot_ready"), 1)

            def gained(n):
                ve.wait_ge(S("slots_turned"), n + 1)
                for g in range(NJ):
                    gb = g_ffn[:, 4 * g:4 * g + 4].rearrange("p (k a) -> p k a", a=1)
                    bank = ps[4][:, :].rearrange("p (j g s) -> p j g s", j=4, g=NJ)
                    ins = ve.tensor_tensor(xe[:, 4 * g:4 * g + 4, :], bank[:, :, g, :],
                                           bc(gb, 4, SLOTS), ALU.mult)
                ins.then_inc(S("xe_ready"), 1)

            def add_y(m, t):
                ve.wait_ge(S("combined"), TT * m + t + 1)
                for g in range(NJ):
                    xs = x_res[:, t, g * UN:(g + 1) * UN]
                    ins = ve.tensor_tensor(xs, ps[g][:, :], xs, ALU.add)
                ins.then_inc(S("y_added"), 1)

            def expert(n, m=None):
                if m is not None:
                    ve.wait_ge(S("bank6_turned"), n)
                for t in range(TT):
                    ve.tensor_scalar(comb_0[:, t, :], hot_f[:, 0, t, :], gate_w[:, 0, t:t + 1], None,
                                     ALU.mult).then_inc(S("comb_half"), 1)
                ve.wait_ge(S("comb_half"), TT * (n + 1))
                for t in range(TT):
                    ve.scalar_tensor_tensor(
                        out=comb[:, t], in0=bc(hot_f[:, 1, t:t + 1, :], NJ, SLOTS),
                        scalar=gate_w[:, 1, t:t + 1], in1=bc(comb_0[:, t:t + 1, :], NJ, SLOTS),
                        op0=ALU.mult, op1=ALU.add).then_inc(S("comb_ready"), 1)
                ve.wait_ge(S("gathered"), n + 1)
                ve.wait_ge(S("comb_ready"), TT * (n + 1))
                ve.tensor_scalar(rel[:, :, :], rel[:, :, :], -float(SLOTS), None,
                                 ALU.add).then_inc(S("rel_moved"), 1)
                ve.wait_ge(S("rel_moved"), n + 1)
                pick_hot(n + 1)
                if m is not None:
                    for t in range(TT):
                        add_y(m, t)
                ve.wait_ge(S("silu"), n + 1)
                if m is not None:
                    ve.wait_ge(S("bank6_turned"), n)
                ve.tensor_tensor(act[:, :], sg[:, :], ps[5][:, P:2 * P], ALU.mult).then_inc(
                    S("act_ready"), 1)
                ve.wait_ge(S("gu_used1"), n + 1)
                gained(n + 1)

            pick_hot(0)
            gained(0)
            ve.wait_ge(S("routed"), 1)
            last = ve.value_load(n_iter[0:1, 1:2], min_val=EXPERTS - 1,
                                 max_val=MAX_PASSES * EXPERTS - 1)
            expert(0)
            with ve.Fori(0, last) as m:
                expert(m + 1, m)
            def last_add(t, g):
                ve.wait_ge(S("last_combined"), NJ * t + g + 1)
                xs = x_res[:, t, g * UN:(g + 1) * UN]
                ve.tensor_tensor(xs, ps[g][:, :], xs, ALU.add).then_inc(S("last_added"), 1)

            def last_sum(t):
                ve.wait_ge(S("final_squared"), NJ * (t + 1))
                ve.tensor_reduce(sums[:, t:t + 1], chunk_ss[:, t, :], AX, ALU.add).then_inc(
                    S("final_summed"), 1)

            def final(t):
                ve.wait_ge(S("final_rstd"), t + 1)
                for f in range(2):
                    cols = slice(f * D // 2, (f + 1) * D // 2)
                    ve.scalar_tensor_tensor(out=x_res[:, t, cols], in0=x_res[:, t, cols],
                                            scalar=rstd[:, t:t + 1], in1=g_fin[:, cols], op0=ALU.mult,
                                            op1=ALU.mult).then_inc(S("final"), 1)

            for g in range(NJ):
                last_add(0, g)
            last_add(1, 0)
            last_add(1, 1)
            last_sum(0)
            last_add(1, 2)
            last_add(1, 3)
            ve.wait_ge(S("final_gain_loaded"), 16)
            final(0)
            last_sum(1)
            final(1)

        @block.gpsimd
        def _(gp):
            steps = [0]

            def link(ins):
                steps[0] += 1
                ins.then_inc(S("gp_step"), 1)
                gp.wait_ge(S("gp_step"), steps[0])

            half = ROPE // 2
            for i in range(half):
                ins = gp.memset(small[:, i:i + 1], float(10000.0 ** (-2.0 * i / ROPE)))
            ins.then_inc(S("inv_freq"), 1)
            gp.memset(ident[:, :], 0.0)
            gp.memset(ones[:, :], 1.0)
            gp.memset(sb_mask[:, :], 1.0)
            link(gp.memset(mla_mask[:, :], 0.0))
            gp.affine_select(out=ident[:, :], in_=ident[:, :], compare_op=ALU.not_equal, fill=1.0, base=0,
                             pattern=[[-1, P]], channel_multiplier=1)
            gp.affine_select(out=above[:, :], in_=ones[:, :], compare_op=ALU.is_gt, fill=0.0, base=0,
                             pattern=[[-1, P]], channel_multiplier=1)
            for lo in (0, SEQ):
                gp.affine_select(out=sb_mask[:, lo:lo + P], in_=sb_mask[:, lo:lo + P],
                                 compare_op=ALU.is_gt, fill=0.0, base=0, pattern=[[1, P]],
                                 channel_multiplier=-1)
                gp.affine_select(out=mla_mask[:, lo:lo + P], in_=mla_mask[:, lo:lo + P],
                                 compare_op=ALU.is_ge, fill=-1.0e30, base=0, pattern=[[-1, P]],
                                 channel_multiplier=1)
            link(gp.iota(iota32[:, :], [[1, SLOTS]], base=0, channel_multiplier=0,
                         allow_small_or_imprecise_dtypes=True))
            gp.sem_inc(S("consts"), 1)
            gp.memset(minus_half[:, :], -0.5)

            def norms(cols, width, made, count):
                gp.wait_ge(S(made), count)
                for col in cols:
                    r = rstd[:, col:col + TT]
                    link(gp.tensor_scalar(r, sums[:, col:col + TT], 1.0 / width, EPS, ALU.mult, ALU.add))
                    ins = gp.tensor_tensor(r, r, minus_half[:, :], ALU.pow)
                ins.then_inc(S("rstd"), 1)

            norms([SS_X], D, "squared", TT)
            norms([SS_Q], Q_RANK, "squared", 2 * TT)
            norms([SS_KV], KV_RANK, "squared", 3 * TT)
            norms([SS_MEM], D, "squared", 4 * TT)
            for i in range(HEADS + 1):
                if i >= 1:
                    h = i - 1
                    gp.wait_ge(S("sb_exp"), h + 1)
                    if h >= 1:
                        gp.wait_ge(S("o_made"), h)
                    gp.tensor_tensor(sb_a[:, :], sb_b[:, h % 2], sb_mask[:, :], ALU.mult).then_inc(
                        S("sb_weights"), 1)
                if i < HEADS:
                    gp.wait_ge(S("sb_logs"), i + 1)
                    gp.tensor_tensor(sb_m[:, :], sb_m[:, :], sb_mask[:, :], ALU.mult).then_inc(
                        S("sb_masked"), 1)
            norms([SS_A, SS_B], HEADS * HD, "sums_made", 1)
            norms([SS_X1], D, "sums_made", 2)
            gp.wait_ge(S("turned"), bank0[MEM_Q] + 2)
            gp.dma_start(w_r[:, :, 0:GROUPS], w_group[0].rearrange("(k p) g -> p k g", p=P)).then_inc(
                S("router_loaded"), 16)
            gp.dma_start(w_r[:, :, GROUPS:36], w_expert_router[0].rearrange("(k p) g -> p k g", p=P)
                         ).then_inc(S("router_loaded"), 16)
            gp.dma_start(b_r[:, 0:GROUPS], b_group[0:1, :].to_broadcast([P, GROUPS])).then_inc(
                S("router_loaded"), 16)
            gp.dma_start(b_r[:, GROUPS:36], b_expert[0:1, :].to_broadcast([P, EXPERTS])).then_inc(
                S("router_loaded"), 16)
            gp.iota(rt[:, 720:720 + PER_GROUP], [[-1, PER_GROUP]], base=PER_GROUP, channel_multiplier=0,
                    allow_small_or_imprecise_dtypes=True).then_inc(S("router_consts"), 1)
            gp.iota(rt[:, 736:736 + EXPERTS], [[SLOTS, EXPERTS]], base=0, channel_multiplier=0,
                    allow_small_or_imprecise_dtypes=True).then_inc(S("router_consts"), 1)
            norms([SS_X2], D, "sums_made", 3)
            gp.wait_ge(S("rstd"), 7)
            for t in range(TT):
                gp.wait_ge(S("final_summed"), t + 1)
                link(gp.tensor_scalar(rstd[:, t:t + 1], sums[:, t:t + 1], 1.0 / D, EPS, ALU.mult,
                                      ALU.add))
                gp.tensor_tensor(rstd[:, t:t + 1], rstd[:, t:t + 1], minus_half[:, 0:1],
                                 ALU.pow).then_inc(S("final_rstd"), 1)


_INS = ["x", "mem", "positions", "norm_mix", "w_in", "norm_q_lat", "w_q_b", "norm_kv_lat", "w_kv_b",
        "norm_mla_out", "norm_sb_out", "w_out", "norm_mem_x", "norm_mem_src", "w_mem_q", "w_mem_kv",
        "w_mem_o", "norm_ffn", "w_group", "b_group", "w_expert_router", "b_expert", "w_gate", "w_up",
        "w_down", "norm_final"]


def kernel(**inputs):
    import numpy as _np
    import concourse.bacc as _bacc
    from concourse import mybir as _mybir
    from concourse.bass_utils import run_bass_kernel_spmd as _run

    nc = _bacc.Bacc("TRN2", target_bir_lowering=False, num_devices=1)
    arrays, args = {}, []
    for name in _INS:
        a = _np.ascontiguousarray(inputs[name])
        arrays[f"in_{name}"] = a
        args.append(nc.dram_tensor(f"in_{name}", a.shape, _mybir.dt.from_np(a.dtype),
                                   kind="ExternalInput").ap())
    args.append(nc.dram_tensor("out_0", (1, SEQ, D), F32, kind="ExternalOutput").ap())
    layer(nc, *args)
    r = _run(nc, [arrays], core_ids=[0])
    return r.results[0]["out_0"]
```

```python
from contextlib import ExitStack

import concourse.bass as bass
from concourse import mybir

F32 = mybir.dt.float32
F32R = mybir.dt.float32r
I32 = mybir.dt.int32
ALU = mybir.AluOpType
ACT = mybir.ActivationFunctionType
AX = mybir.AxisListType.X

P = 128
SEQ, D = 256, 2048
TT = SEQ // P
KD = D // P
Q_RANK, KV_RANK, ROPE = 512, 256, 64
HEADS, HD = 8, 128
MEM_HEADS = 4
GROUPS, PER_GROUP = 4, 8
EXPERTS = GROUPS * PER_GROUP
FE = 512
SLOTS = 32
NJ = P // SLOTS
MAX_PASSES = SEQ // SLOTS
AHEAD = 3
PASS_ROWS = EXPERTS * SLOTS
EPS = 1e-6
SC_MLA = float(HD + ROPE) ** -0.5
SC_SB = float(HD) ** -0.5
BLK = 3 * P
RING = 4
UK = 2
UN = 512

Q_LAT, KV_LAT, SB_Q, SB_K, SB_V, Q_PE, Q_NOPE, K_NOPE, V_MLA = 0, 1, 2, 4, 6, 8, 9, 11, 13
MEM_K, MEM_V, W_OUT, MEM_Q, MEM_O, CHUNKS = 15, 16, 17, 25, 26, 30


def chunk_tiles(c):
    if Q_PE <= c < K_NOPE:
        return Q_RANK // P
    if K_NOPE <= c < MEM_K:
        return KV_RANK // P
    if W_OUT <= c < MEM_Q:
        return HEADS
    return MEM_HEADS if c >= MEM_O else KD


def chunk_cols(c):
    return KV_RANK + ROPE if c == KV_LAT else UN


UNIT0 = [0]
for _c in range(CHUNKS):
    UNIT0.append(UNIT0[-1] + chunk_tiles(_c) // UK)
UNITS = [(c, i) for c in range(CHUNKS) for i in range(chunk_tiles(c) // UK)]

TURNED = [SB_Q, SB_Q + 1, SB_K, SB_K + 1, KV_LAT, Q_PE, Q_NOPE, Q_NOPE + 1, K_NOPE, K_NOPE + 1,
          MEM_K, MEM_Q]
BY_VECTOR = list(range(W_OUT, MEM_Q)) + list(range(MEM_O, CHUNKS))
SPLITS = [("mix", KD), ("q", 4), ("kv", 2), ("mem", KD), ("out", KD), ("memx", KD), ("memo", MEM_HEADS)]
SPLIT0 = {}
_n = 0
for _name, _k in SPLITS:
    SPLIT0[_name] = _n
    _n += _k
SPLIT_K = dict(SPLITS)


def layer(nc, x, mem, positions, norm_mix, w_in, norm_q_lat, w_q_b, norm_kv_lat, w_kv_b,
          norm_mla_out, norm_sb_out, w_out, norm_mem_x, norm_mem_src, w_mem_q, w_mem_kv,
          w_mem_o, norm_ffn, w_group, b_group, w_expert_router, b_expert, w_gate, w_up,
          w_down, norm_final, out):
    ctx = ExitStack()
    sems = {}

    def S(name):
        if name not in sems:
            sems[name] = ctx.enter_context(nc.semaphore(name))
        return sems[name]

    with ctx:
        base = nc.sbuf_base + (-nc.sbuf_base) % 64
        at = [base]
        limit = nc.sbuf_usable_end

        def place(name, shape, dt=F32, offset=None):
            size = 4
            for s in shape[1:]:
                size *= s
            if offset is None:
                offset = at[0]
                at[0] += size + (-size) % 64
            assert offset + size <= limit, (name, offset + size, limit)
            return nc.alloc_sbuf_tensor_at(name, shape, dt, offset=offset)

        x_res = place("x_res", [P, TT, D])
        a_hi_at = at[0]
        a_hi = place("a_hi", [P, KD, SEQ], F32R)
        a_lo_at = at[0]
        a_lo = place("a_lo", [P, KD, SEQ], F32R)
        w_at = at[0]
        w_raw = place("w_raw", [P, RING, UK, UN])
        w_hi = place("w_hi", [P, RING, UK, UN], F32R)
        w_lo = place("w_lo", [P, RING, UK, UN], F32R)
        nat = place("nat", [P, 2, TT, UN])
        km_t = place("km_t", [P, MEM_HEADS, SEQ])
        v_mem = place("v_mem", [P, TT, UN])
        ident = place("ident", [P, P])
        ones = place("ones", [P, P])
        above_at = at[0]
        above = place("above", [P, P])
        sb_mask = place("sb_mask", [P, BLK])
        mla_mask_at = at[0]
        mla_mask = place("mla_mask", [P, BLK])
        before = sb_mask[:, 0:P]
        g_nat_at = at[0]
        g_nat = place("g_nat", [86, P])
        g_t = place("g_t", [P, 86])
        g_ffn = place("g_ffn", [P, KD])
        sums = place("sums", [P, 16])
        rstd = place("rstd", [P, 16])
        rope_cs = place("rope_cs", [P, 2, TT, ROPE // 2])
        small = place("small", [P, 64])
        minus_half = place("minus_half", [P, TT])
        iota32 = place("iota32", [P, SLOTS])
        gate_w = place("gate_w", [P, 2, TT])
        rel = place("rel", [P, 2, TT])
        chunk_ss = place("chunk_ss", [P, TT, 4])
        head_ss = place("head_ss", [P, TT, 2, HEADS])
        head_junk = place("head_junk", [P, HD])
        n_iter = place("n_iter", [P, 3], I32)
        pos_i = place("pos_i", [P, TT], I32)
        e_at = at[0]
        qsb_t = place("qsb_t", [P, HEADS, SEQ])
        ksb_t = place("ksb_t", [P, HEADS, SEQ])
        v_sb = place("v_sb", [P, TT, HEADS * HD])
        q_t = place("q_t", [P, HEADS, SEQ])
        qpe_t = place("qpe_t", [P, HEADS // 2, SEQ])
        k_t = place("k_t", [P, HEADS, SEQ])
        kpe_t = place("kpe_t", [P, SEQ])
        v_mla = place("v_mla", [P, TT, HEADS * HD])
        o_at = at[0]
        o_cat = place("o_cat", [P, TT, D])
        c_q = place("c_q", [P, TT, Q_RANK])
        c_kv = place("c_kv", [P, TT, KV_RANK + ROPE])
        mem_sb = place("mem_sb", [P, TT, D], offset=o_at)
        gu = [place("gu0", [P, 2, 2, KD // 2, FE], offset=e_at),
              place("gu1", [P, 2, 2, KD // 2, FE], offset=w_at)]
        down0 = place("down0", [P, 2, D], offset=e_at + 4 * 16 * 1024)
        down1 = place("down1", [P, 2, D], offset=a_lo_at)
        a2_hi = place("a2_hi", [P, KD, SEQ], F32R, offset=e_at)
        a2_lo = place("a2_lo", [P, KD, SEQ], F32R, offset=e_at + 16 * 1024)
        at[0] -= (Q_RANK + KV_RANK + ROPE) * TT * 4
        p_mla = place("p_mla", [P, 2, BLK])
        pt_mla = place("pt_mla", [P, BLK])
        sb_e = place("sb_e", [P, BLK])
        sb_l = place("sb_l", [P, BLK])
        sb_b = place("sb_b", [P, 2, BLK])
        sb_m = place("sb_m", [P, BLK])
        sb_a = place("sb_a", [P, BLK])
        row_m = place("row_m", [P, HEADS, TT])
        row_n = place("row_n", [P, HEADS, TT])
        row_s = place("row_s", [P, HEADS, TT])
        row_r = place("row_r", [P, HEADS, TT])
        pm = place("pm", [P, 2, TT, SEQ], offset=a_hi_at)
        pmt = place("pmt", [P, 2, TT, SEQ], offset=a_hi_at + 4096)
        mrow = place("mrow", [P, 4, MEM_HEADS, TT], offset=a_hi_at + 8192)
        o_mem = place("o_mem", [P, TT, UN], offset=w_at + 48 * 1024)
        memo_lo = place("memo_lo", [P, MEM_HEADS, SEQ], F32R, offset=w_at + 52 * 1024)
        h_t = place("h_t", [P, 2, 4, SEQ], offset=a_hi_at + 4096)
        junk1 = place("junk1", [P, UN], offset=e_at + 40 * 1024)
        junk2 = place("junk2", [P, UN], offset=a_hi_at + 12 * 1024)
        end_at = e_at + 80 * 1024
        w_r = place("w_r", [P, KD, 36], offset=end_at)
        b_r = place("b_r", [P, 36], offset=end_at + 2304)
        rt = place("rt", [P, 768], offset=end_at + 2496)
        xe = place("xe", [P, KD, SLOTS], offset=end_at)
        x_slots = place("x_slots", [P, UN], offset=end_at + 2048)
        y_sb = place("y_sb", [P, UN], offset=end_at + 4096)
        comb_0 = place("comb_0", [P, TT, SLOTS], offset=g_nat_at)
        hot = place("hot", [P, TT, SLOTS], offset=g_nat_at + 256)
        hot_f = place("hot_f", [P, 2, TT, SLOTS], offset=above_at)
        turned_6 = place("turned_6", [P, TT + 1, P], offset=mla_mask_at)
        comb = place("comb", [P, TT, NJ, SLOTS], offset=end_at + 6144)
        sg = place("sg", [P, P], offset=end_at + 6144 + 1024)
        act = place("act", [P, P], offset=end_at + 6144 + 1536)
        g_fin = place("g_fin", [P, D], offset=e_at)
        squares = place("squares", [P, UN], offset=w_at)
        comb_t, act_t = turned_6[:, 0:TT, :], turned_6[:, TT, :]
        h_nat = place("h_nat", [P, TT, KD, P], offset=a_hi_at)

        ps = [ctx.enter_context(nc.psum_tensor(f"ps{i}", [P, 512], F32)) for i in range(8)]

        def unit_src(c, i):
            rows = slice(i * UK * P, (i + 1) * UK * P)
            def cols(w, n0, n=UN):
                return w[0, rows, n0:n0 + n].rearrange("(k p) n -> p k n", p=P)
            def headed(w, width, h0, nh, lo, hi):
                return w[0, rows, h0 * width:(h0 + nh) * width].rearrange(
                    "(k p) (h c) -> p k h c", p=P, c=width)[:, :, :, lo:hi]
            if MEM_K <= c <= MEM_V:
                return [cols(w_mem_kv, (c - MEM_K) * UN)]
            if c < Q_PE:
                n0 = {Q_LAT: 0, KV_LAT: Q_RANK}.get(c, Q_RANK + KV_RANK + ROPE + (c - SB_Q) * UN)
                return [cols(w_in, n0, chunk_cols(c))]
            if c == Q_PE:
                return [headed(w_q_b, HD + ROPE, 0, HEADS, HD, HD + ROPE)]
            if c < K_NOPE:
                return [headed(w_q_b, HD + ROPE, 4 * (c - Q_NOPE), 4, 0, HD)]
            if c < V_MLA:
                return [headed(w_kv_b, 2 * HD, 4 * (c - K_NOPE), 4, 0, HD)]
            if c < W_OUT:
                return [headed(w_kv_b, 2 * HD, 4 * (c - V_MLA), 4, HD, 2 * HD)]
            if c < MEM_Q:
                q, g = divmod(c - W_OUT, 2)
                rows = slice((g * HEADS + i * UK) * P, (g * HEADS + (i + 1) * UK) * P)
                return [w_out[0, rows, q * UN:(q + 1) * UN].rearrange("(k p) n -> p k n", p=P)]
            if c == MEM_Q:
                return [cols(w_mem_q, 0)]
            return [cols(w_mem_o, (c - MEM_O) * UN)]

        def chunk_out(c):
            if c in BY_VECTOR:
                return S("chunk_added"), BY_VECTOR.index(c) + 1
            return S("chunk_copied"), sum(1 for d in range(c + 1) if d not in BY_VECTOR)

        def turned_dst(c):
            if c == MEM_K:
                return km_t[:, :, :]
            if c in (SB_Q, SB_Q + 1):
                return qsb_t[:, 4 * (c - SB_Q):4 * (c - SB_Q) + 4, :]
            if c in (SB_K, SB_K + 1):
                return ksb_t[:, 4 * (c - SB_K):4 * (c - SB_K) + 4, :]
            if c in (Q_NOPE, Q_NOPE + 1):
                return q_t[:, 4 * (c - Q_NOPE):4 * (c - Q_NOPE) + 4, :]
            if c == Q_PE:
                return qpe_t[:, :, :]
            if c in (K_NOPE, K_NOPE + 1):
                return k_t[:, 4 * (c - K_NOPE):4 * (c - K_NOPE) + 4, :]
            return qsb_t[:, 0:4, :]

        qm_t = qsb_t
        bank0 = {}
        n = 0
        for c in TURNED:
            bank0[c] = n
            n += 1 if c == KV_LAT else 2

        def acc_bank(c):
            if c in (MEM_K, MEM_V):
                return 2
            return 2 * ((c - W_OUT) % 2) if c >= W_OUT else 2 * (c % 2)

        def bank_user(c):
            return {MEM_K: V_MLA, MEM_V: MEM_K, W_OUT: V_MLA + 1, W_OUT + 1: MEM_V}.get(c, c - 2)

        SS_MEM, SS_X, SS_Q, SS_KV, SS_A, SS_B, SS_X1, SS_X2, = range(0, 16, 2)

        block = ctx.enter_context(nc.Block())

        @block.sync
        def _(sp):
            for t in range(TT):
                sp.dma_start(x_res[:, t, :], x[0, t * P:(t + 1) * P, :]).then_inc(S("x_loaded"), 16)
            sp.wait_ge(S("x_loaded"), 16 * TT)
            for u, (c, i) in enumerate(UNITS):
                if u >= RING:
                    sp.wait_ge(S("w_split"), u - RING + 1)
                dst = w_raw[:, u % RING, :, 0:chunk_cols(c)]
                (src,) = unit_src(c, i)
                if len(src.shape) == 4:
                    for k in range(UK):
                        sp.dma_start(dst[:, k, :].rearrange("p (h c) -> p h c", h=src.shape[2]),
                                     src[:, k]).then_inc(S(f"w_loaded{u % RING}"), 16)
                else:
                    sp.dma_start(dst, src).then_inc(S(f"w_loaded{u % RING}"), 16)

            def load_gate_up(e, side, used=None, halves=(0, 1)):
                wg = w_gate[0, e].rearrange("(p k) f -> p (k f)", k=KD)
                wu = w_up[0, e].rearrange("(p k) f -> p (k f)", k=KD)
                half = KD // 2 * FE
                for b in halves:
                    if used is not None:
                        sp.wait_ge(S(f"gu_used{b}"), used)
                    for m, w in enumerate((wg, wu)):
                        sp.dma_start(gu[side][:, b, m].rearrange("p k f -> p (k f)"),
                                     w[:, b * half:(b + 1) * half]).then_inc(
                                         S(f"gu_loaded{side}{b}"), 16)

            def load_down(e, used=None):
                wd = w_down[0, e].rearrange("(j p) d -> p j d", p=P)
                for b, dst in enumerate((down0, down1)):
                    if used is not None:
                        sp.wait_ge(S(f"down_used{b}"), used)
                    sp.dma_start(dst[:, :, :], wd[:, 2 * b:2 * b + 2, :]).then_inc(
                        S(f"down_loaded{b}"), 16)

            sp.wait_ge(S("w_used"), UNIT0[MEM_O])
            sp.wait_ge(S("mem_scores"), MEM_HEADS)
            load_gate_up(0, 0)
            load_down(0)
            sp.wait_ge(S("w_used"), len(UNITS))
            sp.wait_ge(S("w_split"), len(UNITS))
            load_gate_up(1, 1)
            for e in range(2, AHEAD):
                load_gate_up(e, e % 2, e - 1)
                load_down(e - 1, e - 1)
            load_gate_up(AHEAD, AHEAD % 2, AHEAD - 1, halves=(0,))
            load_down(AHEAD - 1, AHEAD - 1)
            load_gate_up(AHEAD, AHEAD % 2, AHEAD - 1, halves=(1,))
            load_down(AHEAD, AHEAD)
            with sp.Fori(0, (EXPERTS - AHEAD - 1) // 2) as i:
                for m in range(2):
                    e = 2 * i + AHEAD + 1 + m
                    load_gate_up(e, (AHEAD + 1 + m) % 2, 2 * i + AHEAD + m)
                    load_down(e, 2 * i + AHEAD + 1 + m)
            sp.wait_ge(S("routed"), 1)
            total = sp.value_load(n_iter[0:1, 0:1], min_val=EXPERTS, max_val=MAX_PASSES * EXPERTS)
            with sp.If(total > EXPERTS):
                with sp.Fori(EXPERTS - 1, total - 1, EXPERTS) as before_:
                    with sp.Fori(0, EXPERTS // 2) as i:
                        for side in range(2):
                            load_gate_up(2 * i + side, side, before_ + 2 * i + side)
                            load_down(2 * i + side, before_ + 2 * i + 1 + side)
            sp.wait_ge(S("gu_used1"), total)
            sp.dma_start(g_fin[:, :], norm_final.rearrange("(a d) -> a d", a=1).to_broadcast([P, D])
                         ).then_inc(S("final_gain_loaded"), 16)
            for t in range(TT):
                for f in range(2):
                    sp.wait_ge(S("final"), 2 * t + f + 1)
                    cols = slice(f * D // 2, (f + 1) * D // 2)
                    sp.dma_start(out[0, t * P:(t + 1) * P, cols], x_res[:, t, cols]).then_inc(
                        S("stored"), 16)
            sp.wait_ge(S("stored"), 16 * 2 * TT)

        @block.tensor
        def _(pe):
            def split_turn(name, src, k_from=0, k_to=None):
                k0, kn = SPLIT0[name], SPLIT_K[name]
                for kk in range(k_from // 2, (kn if k_to is None else k_to) // 2):
                    b = k0 // 2 + kk
                    if b >= 4:
                        pe.wait_ge(S("split_lo"), 2 * (b - 4) + 2)
                    for i in range(2):
                        for t in range(TT):
                            k = 2 * kk + i
                            mm = pe.transpose(ps[4 + b % 4][:, i * SEQ + t * P:i * SEQ + (t + 1) * P],
                                              src[:, t, k * P:(k + 1) * P], ident[:, :])
                    mm.then_inc(S("split_turned"), 1)

            def project_units(c, units, a0=0, hi=a_hi, lo=a_lo):
                kn, n = chunk_tiles(c), chunk_cols(c)
                acc = [ps[acc_bank(c) + t] for t in range(TT)]
                for i in units:
                    if i == 0 and c >= 2:
                        pe.wait_ge(*chunk_out(bank_user(c)))
                    u = UNIT0[c] + i
                    pe.wait_ge(S("w_rounded"), u + 1)
                    pe.wait_ge(S("w_split"), u + 1)
                    for j in range(UK):
                        k = i * UK + j
                        for t in range(TT):
                            xh = hi[:, a0 + k, t * P:(t + 1) * P]
                            xl = lo[:, a0 + k, t * P:(t + 1) * P]
                            wh, wl = w_hi[:, u % RING, j, 0:n], w_lo[:, u % RING, j, 0:n]
                            pe.matmul(acc[t][:, 0:n], xh, wh, start=(k == 0), stop=False)
                            pe.matmul(acc[t][:, 0:n], xh, wl, start=False, stop=False)
                            mm = pe.matmul(acc[t][:, 0:n], xl, wh, start=False, stop=(k == kn - 1))
                    mm.then_inc(S("w_used"), 1)

            def project(c, a0=0, hi=a_hi, lo=a_lo):
                project_units(c, range(chunk_tiles(c) // UK), a0, hi, lo)

            def split_project(name, src, units, lag=3, first=0):
                kn = SPLIT_K[name]
                for kk in range(first, max(kn // 2, len(units) + lag)):
                    if kk < kn // 2:
                        split_turn(name, src, 2 * kk, 2 * kk + 2)
                    if lag <= kk < len(units) + lag:
                        c, i, a0 = units[kk - lag]
                        pe.wait_ge(S("split_lo"), SPLIT0[name] + 2 * (kk - lag) + 2)
                        project_units(c, [i], a0)

            def turn(c):
                j = TURNED.index(c)
                if c in (KV_LAT, Q_PE):
                    pe.wait_ge(S("roped"), 1 if c == KV_LAT else 2)
                else:
                    pe.wait_ge(*chunk_out(c))
                for b in range(1 if c == KV_LAT else 2):
                    m = bank0[c] + b
                    bank = ps[4 + m % 4]
                    if m >= 4:
                        pe.wait_ge(S("turn_copied"), m - 3)
                    for i in range(1 if c == KV_LAT else 2):
                        for t in range(TT):
                            f = 2 * b + i
                            mm = pe.transpose(bank[:, i * SEQ + t * P:i * SEQ + (t + 1) * P],
                                              nat[:, j % 2, t, f * P:(f + 1) * P], ident[:, :])
                    mm.then_inc(S("turned"), 1)

            pe.wait_ge(S("consts"), 1)
            pe.wait_ge(S("gains_loaded"), 8 * 16)
            pe.transpose(ps[0][:, 0:86], g_nat[:, :], ident[0:86, 0:86]).then_inc(S("gains_turned"), 1)
            pe.wait_ge(S("x_loaded"), 16 * TT)
            pe.wait_ge(S("gains_copied"), 1)
            split_project("mix", x_res, [(Q_LAT, i, 0) for i in range(KD // UK)])
            for c in range(Q_LAT, Q_PE):
                if c > Q_LAT:
                    project(c)
                if SB_Q <= c - 1 < SB_V:
                    turn(c - 1)
            turn(KV_LAT)
            pe.wait_ge(S("turn_copied"), bank0[Q_PE])
            split_turn("q", c_q)
            split_turn("kv", c_kv)
            pe.wait_ge(S("split_lo"), SPLIT0["q"] + 4)
            for c in range(Q_PE, MEM_K):
                if c == Q_NOPE:
                    pe.wait_ge(S("split_lo"), SPLIT0["kv"] + 2)
                project(c, a0=0 if c < K_NOPE else 4)
                if c - 1 in TURNED:
                    turn(c - 1)

            def scores(h):
                s, z = ps[0], ps[1]
                if h == 0:
                    pe.wait_ge(*chunk_out(V_MLA + 1))
                else:
                    pe.wait_ge(S("mla_masked"), h)
                    pe.wait_ge(S("sb_logs"), h)
                po = ROPE * (h % 2)
                for t in range(TT):
                    n = (t + 1) * P
                    o = s[:, 0:P] if t == 0 else s[:, P:BLK]
                    q = slice(t * P, (t + 1) * P)
                    pe.matmul(o, q_t[:, h, q], k_t[:, h, 0:n], start=True, stop=False)
                    mm = pe.matmul(o, qpe_t[po:po + ROPE, h // 2, q], kpe_t[po:po + ROPE, 0:n],
                                   start=False, stop=True)
                mm.then_inc(S("mla_scored"), 1)
                pe.matmul(z[:, 0:SEQ], ksb_t[:, h, 0:P], qsb_t[:, h, :], start=True, stop=True)
                pe.matmul(z[:, SEQ:BLK], ksb_t[:, h, P:SEQ], qsb_t[:, h, P:SEQ], start=True,
                          stop=True).then_inc(S("sb_scored"), 1)

            def turn_probs(h):
                pe.wait_ge(S("mla_probs"), h + 1)
                if h >= 1:
                    pe.wait_ge(S("probs_copied"), h)
                for i in range(3):
                    mm = pe.transpose(ps[4][:, i * P:(i + 1) * P], p_mla[:, h % 2, i * P:(i + 1) * P],
                                      ident[:, :])
                mm.then_inc(S("probs_turned"), 1)

            def later(h):
                pe.wait_ge(S("sb_masked"), h + 1)
                if h >= 1:
                    pe.wait_ge(S("sb_summed"), h)
                m = sb_m
                pe.matmul(ps[5][:, 0:SEQ], above[:, :], m[:, 0:SEQ], start=True, stop=False)
                pe.matmul(ps[5][:, P:SEQ], ones[:, :], m[:, SEQ:BLK], start=False, stop=True)
                pe.matmul(ps[5][:, SEQ:BLK], above[:, :], m[:, SEQ:BLK], start=True,
                          stop=True).then_inc(S("sb_later"), 1)

            def values(h):
                o = ps[6]
                if h >= 1:
                    pe.wait_ge(S("o_copied"), h)
                d = slice(h * HD, (h + 1) * HD)
                for m, (ready, w, v) in enumerate((("probs_copied", pt_mla, v_mla),
                                                   ("sb_weights", sb_a, v_sb))):
                    pe.wait_ge(S(ready), h + 1)
                    pe.matmul(o[:, 2 * m * P:(2 * m + 1) * P], w[:, 0:P], v[:, 0, d],
                              start=True, stop=True)
                    pe.matmul(o[:, (2 * m + 1) * P:(2 * m + 2) * P], w[:, P:SEQ], v[:, 0, d],
                              start=True, stop=False)
                    mm = pe.matmul(o[:, (2 * m + 1) * P:(2 * m + 2) * P], w[:, SEQ:BLK],
                                   v[:, 1, d], start=False, stop=True)
                mm.then_inc(S("o_made"), 1)

            pe.wait_ge(S("turn_copied"), bank0[MEM_K])
            pe.wait_ge(S("mem_loaded"), 16)
            split_turn("mem", mem_sb, 0, 8)
            scores(0)
            mem_units = [(c, i) for c in (MEM_K, MEM_V) for i in range(KD // UK)]
            split_project("mem", mem_sb, [(c, i, 0) for c, i in mem_units[0:2]], lag=4,
                          first=4)
            pe.wait_ge(S("split_lo"), SPLIT0["mem"] + KD)
            for i in range(HEADS + 1):
                if i >= 1:
                    turn_probs(i - 1)
                    later(i - 1)
                for c, j in mem_units[2 * i:2 * i + 1] if i else ():
                    project_units(c, [j])
                if 1 <= i < HEADS:
                    scores(i)
                for c, j in mem_units[2 * i + 1:2 * i + 2] if i else ():
                    project_units(c, [j])
                if i >= 1:
                    values(i - 1)

            pe.wait_ge(S("o_copied"), HEADS)
            pe.wait_ge(S("split_hi"), SPLIT0["mem"] + KD)
            split_project("out", o_cat, [(W_OUT + g, i, g * HEADS) for g in range(2)
                                         for i in range(HEADS // UK)])
            for q in range(1, D // UN):
                project(W_OUT + 2 * q)
                pe.wait_ge(*chunk_out(W_OUT + 2 * q - 1))
                split_turn("memx", x_res, 4 * (q - 1), 4 * q)
                project(W_OUT + 2 * q + 1, a0=HEADS)
            pe.wait_ge(S("split_lo"), SPLIT0["memx"] + KD - 4)
            project_units(MEM_Q, range(0, 3), 0, a2_hi, a2_lo)
            pe.wait_ge(*chunk_out(MEM_Q - 1))
            split_turn("memx", x_res, KD - 4, KD)
            project_units(MEM_Q, range(3, 6), 0, a2_hi, a2_lo)
            pe.wait_ge(S("split_lo"), SPLIT0["memx"] + KD)
            project_units(MEM_Q, range(6, 8), 0, a2_hi, a2_lo)
            turn(MEM_K)
            turn(MEM_Q)
            pe.wait_ge(S("turn_copied"), bank0[MEM_Q] + 2)

            def mem_scores(h):
                for t in range(TT):
                    mm = pe.matmul(ps[h][:, t * SEQ:(t + 1) * SEQ], qm_t[:, h, t * P:(t + 1) * P],
                                   km_t[:, h, :], start=True, stop=True)
                mm.then_inc(S("mem_scores"), 1)

            def mem_turn(h):
                pe.wait_ge(S("mem_probs"), h + 1)
                if h >= 2:
                    pe.wait_ge(S("mem_pt"), h - 1)
                for m in range(2):
                    for t in range(TT):
                        mm = pe.transpose(ps[4 + 3 * (h % 2)][:, m * SEQ + t * P:m * SEQ + (t + 1) * P],
                                          pm[:, h % 2, t, m * P:(m + 1) * P], ident[:, :])
                mm.then_inc(S("mem_pturned"), 1)

            def mem_values(h):
                pe.wait_ge(S("mem_pt"), h + 1)
                for t in range(TT):
                    for m in range(2):
                        mm = pe.matmul(ps[5 + t][:, h * HD:(h + 1) * HD],
                                       pmt[:, h % 2, m, t * P:(t + 1) * P],
                                       v_mem[:, m, h * HD:(h + 1) * HD], start=(m == 0), stop=(m == 1))
                mm.then_inc(S("mem_o"), 1)

            pe.wait_ge(*chunk_out(MEM_Q - 1))
            for h in range(MEM_HEADS):
                mem_scores(h)
            for i in range(MEM_HEADS + 1):
                if i < MEM_HEADS:
                    mem_turn(i)
                if i >= 1:
                    mem_values(i - 1)
            pe.wait_ge(S("mem_o_copied"), TT)
            split_turn("memo", o_mem)
            pe.wait_ge(S("split_lo"), SPLIT0["memo"] + MEM_HEADS)

            def router_turn(q):
                pe.wait_ge(*chunk_out(MEM_O + q))
                for b in range(2):
                    if q >= 1:
                        pe.wait_ge(S("h_copied"), 4 * q - 2 + 2 * b)
                    for i in range(2):
                        for t in range(TT):
                            k = 4 * q + 2 * b + i
                            mm = pe.transpose(ps[4 + b][:, i * SEQ + t * P:i * SEQ + (t + 1) * P],
                                              x_res[:, t, k * P:(k + 1) * P], ident[:, :])
                    mm.then_inc(S("h_turned"), 1)

            def router_logits(q):
                pe.wait_ge(S("h_copied"), 4 * q + 4)
                for i in range(4):
                    k = 4 * q + i
                    for t in range(TT):
                        mm = pe.matmul(ps[6 + t][:, 0:36], h_t[:, q % 2, i, t * P:(t + 1) * P],
                                       w_r[:, k, :], start=(k == 0), stop=(k == KD - 1))
                mm.then_inc(S("logits"), 1)

            pe.wait_ge(S("router_loaded"), 4 * 16)
            for q in range(4):
                project_units(MEM_O + q, [0], lo=memo_lo)
                if q >= 1:
                    router_turn(q - 1)
                project_units(MEM_O + q, [1], lo=memo_lo)
                if q >= 2:
                    router_logits(q - 2)
            router_turn(3)
            router_logits(2)
            router_logits(3)

            pe.wait_ge(S("chosen"), 1)
            sel = rt[:, 512:512 + TT * EXPERTS].rearrange("p (t e) -> p t e", t=TT)
            pe.wait_ge(*chunk_out(CHUNKS - 1))
            pe.matmul(ps[2][:, 0:EXPERTS], before, sel[:, 0], start=True, stop=True)
            pe.matmul(ps[2][:, EXPERTS:2 * EXPERTS], ones[:, :], sel[:, 0], start=True, stop=False)
            pe.matmul(ps[2][:, EXPERTS:2 * EXPERTS], before, sel[:, 1], start=False, stop=True)
            pe.matmul(ps[3][:, 0:EXPERTS], ones[:, :], sel[:, 0], start=True, stop=False)
            pe.matmul(ps[3][:, 0:EXPERTS], ones[:, :], sel[:, 1], start=False,
                      stop=True).then_inc(S("ranked"), 1)

            def gather(n, first=False):
                pe.wait_ge(S("hot_ready"), n + 1)
                if first:
                    pe.wait_ge(S("h_ready"), TT)
                    pe.wait_ge(S("h_copied"), 16)
                else:
                    pe.wait_ge(S("xe_ready"), n)
                for t in range(TT):
                    for g in range(NJ):
                        mm = pe.matmul(ps[4][g * SLOTS:(g + 1) * SLOTS, :], hot[:, t, :],
                                       h_nat[:, t, 4 * g:4 * g + 4, :].rearrange("p k d -> p (k d)"),
                                       start=(t == 0), stop=(t == TT - 1))
                mm.then_inc(S("gathered"), 1)

            def gather_turn(n):
                pe.wait_ge(S("slots_copied"), n + 1)
                for j in range(NJ):
                    mm = pe.transpose(ps[4][:, j * P:(j + 1) * P], x_slots[:, j * P:(j + 1) * P],
                                      ident[:, :])
                mm.then_inc(S("slots_turned"), 1)

            def gate_up(b, side, loads):
                pe.wait_ge(S(f"gu_loaded{side}{b}"), 32 * loads)
                for kk in range(KD // 2):
                    k = b * (KD // 2) + kk
                    for j in range(NJ):
                        mm = pe.matmul(
                            ps[5][j * SLOTS:(j + 1) * SLOTS, 0:2 * P].rearrange(
                                "s (m f) -> s m f", m=2),
                            xe[:, k, :], gu[side][:, b, :, kk, j * P:(j + 1) * P],
                            start=(k == 0), stop=(k == KD - 1))
                mm.then_inc(S(f"gu_used{b}"), 1)

            def combine(t, g):
                rows = slice(g * SLOTS, (g + 1) * SLOTS)
                return pe.matmul(ps[g][:, :], turned_6[rows, t, :], y_sb[rows, :], start=True, stop=True)

            def expert(n, side, loads, m=None):
                for b in range(2):
                    if m is not None:
                        if b == 0:
                            pe.wait_ge(S("y_copied"), n)
                        else:
                            pe.wait_ge(S("y_added"), TT * m + 1)
                        for g in range(NJ):
                            mm = combine(b, g)
                        mm.then_inc(S("combined"), 1)
                    if b == 0:
                        pe.wait_ge(S("xe_ready"), n + 1)
                        if m is not None:
                            pe.wait_ge(S("act_ready"), n)
                    gate_up(b, side, loads)
                gather(n + 1)
                gather_turn(n + 1)
                pe.wait_ge(S("comb_ready"), TT * (n + 1))
                pe.wait_ge(S("act_ready"), n + 1)
                if m is not None:
                    pe.wait_ge(S("bank6_copied"), n)
                for t in range(TT):
                    mm = pe.transpose(ps[6][:, t * P:(t + 1) * P],
                                      comb[:, t].rearrange("p g s -> p (g s)"), ident[:, :])
                pe.transpose(ps[6][:, TT * P:(TT + 1) * P], act[:, :], ident[:, :]).then_inc(
                    S("bank6_turned"), 1)
                pe.wait_ge(S("bank6_copied"), n + 1)
                if m is not None:
                    pe.wait_ge(S("y_copied"), n)
                for b, w in enumerate((down0, down1)):
                    pe.wait_ge(S(f"down_loaded{b}"), 16 * (n + 1))
                    for jj in range(2):
                        j = 2 * b + jj
                        for g in range(NJ):
                            mm = pe.matmul(ps[7][g * SLOTS:(g + 1) * SLOTS, :],
                                           act_t[:, j * SLOTS:(j + 1) * SLOTS],
                                           w[:, jj, g * UN:(g + 1) * UN],
                                           start=(j == 0), stop=(j == NJ - 1))
                    mm.then_inc(S(f"down_used{b}"), 1)
                if m is not None:
                    pe.wait_ge(S("y_added"), TT * m + TT)

            gather(0, first=True)
            gather_turn(0)
            pe.wait_ge(S("routed"), 1)
            pairs = pe.value_load(n_iter[0:1, 2:3], min_val=EXPERTS // 2 - 1,
                                  max_val=MAX_PASSES * EXPERTS // 2 - 1)
            expert(0, 0, 1)
            with pe.Fori(0, pairs) as i:
                expert(2 * i + 1, 1, i + 1, 2 * i)
                expert(2 * i + 2, 0, i + 2, 2 * i + 1)
            expert(2 * pairs + 1, 1, pairs + 1, 2 * pairs)
            pe.wait_ge(S("y_copied"), 2 * pairs + 2)
            for t in range(TT):
                for g in range(NJ):
                    if t:
                        pe.wait_ge(S("last_added"), g + 1)
                    combine(t, g).then_inc(S("last_combined"), 1)

        @block.scalar
        def _(sc):
            done = [0]

            def rounded(upto):
                for u in range(done[0], min(upto, len(UNITS))):
                    c, i = UNITS[u]
                    n = chunk_cols(c)
                    per = sum(16 * (UK if len(unit_src(*UNITS[v])[0].shape) == 4 else 1)
                              for v in range(u % RING, u + 1, RING))
                    sc.wait_ge(S(f"w_loaded{u % RING}"), per)
                    if u >= RING:
                        sc.wait_ge(S("w_used"), u - RING + 1)
                    sc.activation(w_hi[:, u % RING, :, 0:n], w_raw[:, u % RING, :, 0:n],
                                  ACT.Copy).then_inc(S("w_rounded"), 1)
                done[0] = max(done[0], upto)

            def square(src, acc, junk):
                sc.activation(junk, src, ACT.Square, accum_out=acc).then_inc(S("squared"), 1)

            sq = [0]

            def squares_of(src, col, junk):
                for t in range(TT):
                    square(src[:, t], sums[:, col + t:col + t + 1], junk)
                    sq[0] += 1
                    sc.wait_ge(S("squared"), sq[0])

            def split_head(name, g0, used=0, a0=0, hi=a_hi, k_from=0, k_to=None):
                k0, kn = SPLIT0[name], SPLIT_K[name]
                if used:
                    sc.wait_ge(S("w_used"), used)
                for k in range(k_from, kn if k_to is None else k_to):
                    b = (k0 + k) // 2
                    sc.wait_ge(S("split_turned"), b + 1)
                    i = k % 2
                    sc.activation(hi[:, a0 + k, :], ps[4 + b % 4][:, i * SEQ:(i + 1) * SEQ], ACT.Copy,
                                  scale=1.0 if g0 is None else g_t[:, g0 + k:g0 + k + 1]
                                  ).then_inc(S("split_hi"), 1)

            def heads_and_units(name, g0, unit, used=0, lag=3):
                for kk in range(SPLIT_K[name] // 2):
                    split_head(name, g0, 0 if kk else used, k_from=2 * kk, k_to=2 * kk + 2)
                    rounded(unit + RING + kk - lag)

            def chunk_copy(c, dst, col=None):
                sc.wait_ge(S("w_used"), UNIT0[c + 1])
                for t in range(TT):
                    ins = sc.activation(dst(t), ps[acc_bank(c) + t][:, 0:chunk_cols(c)], ACT.Copy,
                                        scale=rstd[:, col + t:col + t + 1])
                ins.then_inc(S("chunk_copied"), 1)

            def to_nat(c, col):
                j = TURNED.index(c)
                if j >= 2:
                    sc.wait_ge(S("turned"), bank0[TURNED[j - 1]])
                chunk_copy(c, lambda t: nat[:, j % 2, t, :], col)

            def x_squares(q, chunk_junk):
                for t in range(TT):
                    if xsq[0]:
                        sc.wait_ge(S("x_squared"), xsq[0])
                    sc.activation(chunk_junk[:, :], x_res[:, t, q * UN:(q + 1) * UN], ACT.Square,
                                  accum_out=chunk_ss[:, t, q:q + 1]).then_inc(S("x_squared"), 1)
                    xsq[0] += 1

            xsq = [0]
            for gain, r0, rows in ((norm_mix, 0, 16), (norm_mem_src, 16, 16), (norm_mem_x, 32, 16),
                                   (norm_q_lat, 48, 4), (norm_kv_lat, 52, 2), (norm_mla_out, 54, 8),
                                   (norm_sb_out, 62, 8), (norm_ffn, 70, 16)):
                sc.dma_start(g_nat[r0:r0 + rows, :], gain[0].rearrange("(k p) -> k p", p=P)
                             ).then_inc(S("gains_loaded"), 16)
            for t in range(TT):
                sc.dma_start(pos_i[:, t:t + 1], positions[0, t * P:(t + 1) * P].rearrange(
                    "(p a) -> p a", a=1)).then_inc(S("pos_loaded"), 16)
            sc.dma_start(g_ffn[:, :], norm_ffn[0].rearrange("(p k) -> p k", k=KD)).then_inc(
                S("ffn_gain_loaded"), 16)
            sc.preload_act_table_set("natural_log_exp_and_others")
            sc.wait_ge(S("gains_turned"), 1)
            sc.activation(g_t[:, :], ps[0][:, 0:86], ACT.Copy).then_inc(S("gains_copied"), 1)
            sc.wait_ge(S("gains_copied"), 1)
            heads_and_units("mix", 0, 0)
            junk = v_mla[:, :, :].rearrange("p t d -> p (t d)")
            squares_of(x_res, SS_X, junk)
            sc.wait_ge(S("rstd"), 1)
            for c in range(Q_LAT, Q_PE):
                rounded(UNIT0[c + 1] + RING)
                if c == Q_LAT:
                    chunk_copy(c, lambda t: c_q[:, t, :], SS_X)
                    sc.wait_ge(*chunk_out(c))
                    squares_of(c_q, SS_Q, junk[:, 0:Q_RANK])
                elif c == KV_LAT:
                    chunk_copy(c, lambda t: c_kv[:, t, :], SS_X)
                    sc.wait_ge(*chunk_out(c))
                    squares_of(c_kv[:, :, 0:KV_RANK], SS_KV, junk[:, 0:KV_RANK])
                    sc.dma_start(mem_sb[:, :, :], mem[0].rearrange("(t p) d -> p t d", p=P)).then_inc(
                        S("mem_loaded"), 16)
                elif c < SB_V:
                    to_nat(c, SS_X)
                    if c == SB_Q:
                        sc.wait_ge(S("angles"), 1)
                        sc.activation(rope_cs[:, :, :, :], rope_cs[:, :, :, :], ACT.Sin).then_inc(
                            S("rope_ready"), 1)
                        sc.preload_act_table_set("natural_log_exp_and_others")
                else:
                    n0 = (c - SB_V) * UN
                    chunk_copy(c, lambda t: v_sb[:, t, n0:n0 + UN], SS_X)
            split_head("q", 48, UNIT0[Q_PE])
            split_head("kv", 52, UNIT0[Q_PE], a0=4)
            sc.wait_ge(S("rstd"), 3)
            for c in range(Q_PE, MEM_K):
                first = c in (Q_PE, V_MLA + 1)
                rounded(UNIT0[c + 1] + RING - first)
                if c < V_MLA:
                    to_nat(c, SS_Q if c < K_NOPE else SS_KV)
                    if c == Q_PE:
                        rounded(UNIT0[c + 1] + RING)
                        sc.wait_ge(S("mem_loaded"), 16)
                        squares_of(mem_sb, SS_MEM, junk)
                else:
                    n0 = (c - V_MLA) * UN
                    chunk_copy(c, lambda t: v_mla[:, t, n0:n0 + UN], SS_KV)
                    rounded(UNIT0[c + 1] + RING)

            def head_norm(h):
                sc.wait_ge(S("o_copied"), h + 1)
                for t in range(TT):
                    for g in range(2):
                        d = (g * HEADS + h) * HD
                        if steps[0]:
                            sc.wait_ge(S("head_squared"), steps[0])
                        sc.activation(head_junk[:, :], o_cat[:, t, d:d + HD], ACT.Square,
                                      accum_out=head_ss[:, t, g, h:h + 1]).then_inc(
                                          S("head_squared"), 1)
                        steps[0] += 1

            steps = [0]
            split_head("mem", 16, UNIT0[MEM_K], k_to=KD // 2)
            for i in range(HEADS + 1):
                rounded(min(UNIT0[MEM_K] + 2 * i, UNIT0[W_OUT]) + RING)
                if i == 4:
                    to_nat(MEM_K, SS_MEM)
                if i >= 1:
                    h = i - 1
                    sc.wait_ge(S("probs_turned"), h + 1)
                    if h >= 1:
                        sc.wait_ge(S("o_made"), h)
                    sc.activation(pt_mla[:, :], ps[4][:, 0:BLK], ACT.Copy).then_inc(
                        S("probs_copied"), 1)
                    sc.wait_ge(S("sb_summed"), h + 1)
                    sc.activation(sb_b[:, h % 2], sb_b[:, h % 2], ACT.Exp).then_inc(S("sb_exp"), 1)
                if i < HEADS:
                    h = i
                    sc.wait_ge(S("sb_scored"), h + 1)
                    sc.activation(sb_e[:, :], ps[1][:, 0:BLK], ACT.Abs).then_inc(S("sb_abs"), 1)
                    sc.wait_ge(S("sb_abs"), h + 1)
                    sc.activation(sb_e[:, :], sb_e[:, :], ACT.Exp, scale=-SC_SB).then_inc(
                        S("sb_expabs"), 1)
                    sc.wait_ge(S("sb_expabs"), h + 1)
                    if h >= 1:
                        sc.wait_ge(S("sb_logs"), h)
                    sc.activation(sb_l[:, :], sb_e[:, :], ACT.Ln, bias=1.0).then_inc(
                        S("sb_log1p"), 1)
                    sc.wait_ge(S("mla_max"), h + 1)
                    for t, cols in enumerate((slice(0, P), slice(P, BLK))):
                        ins = sc.activation(p_mla[:, h % 2, cols], p_mla[:, h % 2, cols], ACT.Exp,
                                            bias=row_n[:, h, t:t + 1],
                                            accum_out=row_s[:, h, t:t + 1])
                    ins.then_inc(S("mla_probs"), 1)
                if i == 0:
                    split_head("mem", 16, k_from=KD // 2)
                if i >= 2:
                    head_norm(i - 2)
            sc.wait_ge(S("rstd"), 4)
            chunk_copy(MEM_V, lambda t: v_mem[:, t, :], SS_MEM)
            heads_and_units("out", 54, UNIT0[W_OUT], UNIT0[W_OUT])
            head_norm(HEADS - 1)

            def memx_heads(q):
                split_head("memx", 32, hi=a2_hi, k_from=4 * q, k_to=4 * q + 4)
                x_squares(q, junk1)

            for c in range(W_OUT, MEM_Q):
                rounded(UNIT0[c + 1] + RING)
                if c > W_OUT and (c - W_OUT) % 2 == 0:
                    memx_heads((c - W_OUT) // 2 - 1)
            memx_heads(3)
            rounded(UNIT0[MEM_Q + 1] + RING)
            sc.wait_ge(S("rstd"), 6)
            to_nat(MEM_Q, SS_X1)
            sc.wait_ge(S("w_used"), UNIT0[MEM_O])
            for i in range(MEM_HEADS + 1):
                if i < MEM_HEADS:
                    h = i
                    sc.wait_ge(S("mem_max"), h + 1)
                    if h >= 2:
                        sc.wait_ge(S("mem_pturned"), h - 1)
                    for t in range(TT):
                        ins = sc.activation(pm[:, h % 2, t, :], ps[h][:, t * SEQ:(t + 1) * SEQ],
                                            ACT.Exp, bias=mrow[:, 1, h, t:t + 1], scale=SC_SB,
                                            accum_out=mrow[:, 2, h, t:t + 1])
                    ins.then_inc(S("mem_probs"), 1)
                if i >= 1:
                    h = i - 1
                    sc.wait_ge(S("mem_pturned"), h + 1)
                    if h >= 2:
                        sc.wait_ge(S("mem_o"), h - 1)
                    sc.activation(pmt[:, h % 2].rearrange("p m t -> p (m t)"),
                                  ps[4 + 3 * (h % 2)][:, :],
                                  ACT.Copy).then_inc(S("mem_pt"), 1)
            split_head("memo", None, UNIT0[MEM_O])
            for q in range(4):
                if q >= 1:
                    sc.wait_ge(*chunk_out(MEM_O + q - 1))
                    x_squares(q - 1, junk2)
                rounded(UNIT0[MEM_O + q + 1] + RING)
            sc.wait_ge(S("h_turned"), 8)
            sc.wait_ge(S("logits"), 2)
            for i in (2, 3):
                sc.activation(h_t[:, 1, i, :], ps[5][:, i % 2 * SEQ:(i % 2 + 1) * SEQ], ACT.Copy,
                              scale=g_t[:, 82 + i:83 + i]).then_inc(S("h_copied"), 1)
            sc.wait_ge(*chunk_out(CHUNKS - 1))
            x_squares(3, junk2)

            sc.wait_ge(S("rstd"), 7)
            sc.wait_ge(S("w_used"), len(UNITS))
            sc.wait_ge(S("logits"), 4)
            for t in range(TT):
                sc.activation(h_nat[:, t], x_res[:, t, :].rearrange("q (p k) -> q k p", k=KD), ACT.Copy,
                              scale=rstd[:, SS_X2 + t:SS_X2 + t + 1]).then_inc(S("h_ready"), 1)
            sc.wait_ge(S("logits_ready"), 1)
            el = rt[:, 0:8]
            sc.activation(rt[:, 8:16], el, ACT.Exp).then_inc(S("group_exp"), 1)
            sc.wait_ge(S("second_gap"), 1)
            sc.activation(rt[:, 18:20], rt[:, 16:18], ACT.Exp).then_inc(S("second_exp"), 1)

            def slots_copy(n, first=False):
                sc.wait_ge(S("gathered"), n + 1)
                if not first:
                    sc.wait_ge(S("slots_turned"), n)
                sc.activation(x_slots[:, :], ps[4][:, :], ACT.Copy).then_inc(S("slots_copied"), 1)

            def expert(n, m=None):
                sc.wait_ge(S("gu_used1"), n + 1)
                if m is not None:
                    sc.wait_ge(S("act_ready"), n)
                sc.activation(sg[:, :], ps[5][:, 0:P], ACT.Silu).then_inc(S("silu"), 1)
                slots_copy(n + 1)
                sc.wait_ge(S("bank6_turned"), n + 1)
                if m is not None:
                    sc.wait_ge(S("combined"), TT * m + TT)
                    sc.wait_ge(S("down_used1"), n)
                sc.activation(turned_6[:, :, :], ps[6][:, 0:(TT + 1) * P].rearrange(
                    "p (t a) -> p t a", t=TT + 1), ACT.Copy).then_inc(S("bank6_copied"), 1)
                sc.wait_ge(S("down_used1"), n + 1)
                sc.activation(y_sb[:, :], ps[7][:, :], ACT.Copy).then_inc(S("y_copied"), 1)

            slots_copy(0, first=True)
            sc.wait_ge(S("routed"), 1)
            last = sc.value_load(n_iter[0:1, 1:2], min_val=EXPERTS - 1,
                                 max_val=MAX_PASSES * EXPERTS - 1)
            expert(0)
            with sc.Fori(0, last) as m:
                expert(m + 1, m)
            for i in range(TT * NJ):
                t, g = divmod(i, NJ)
                sc.wait_ge(S("last_added"), i + 1)
                if i:
                    sc.wait_ge(S("final_squared"), i)
                sc.activation(squares[:, :], x_res[:, t, g * UN:(g + 1) * UN], ACT.Square,
                              accum_out=chunk_ss[:, t, g:g + 1]).then_inc(S("final_squared"), 1)

        @block.vector
        def _(ve):
            done = [0]
            steps = [0]

            def link(ins):
                steps[0] += 1
                ins.then_inc(S("vector_step"), 1)
                ve.wait_ge(S("vector_step"), steps[0])

            def split_w(upto):
                for u in range(done[0], min(upto, len(UNITS))):
                    n = chunk_cols(UNITS[u][0])
                    ve.wait_ge(S("w_rounded"), u + 1)
                    ve.tensor_tensor(w_lo[:, u % RING, :, 0:n], w_raw[:, u % RING, :, 0:n],
                                     w_hi[:, u % RING, :, 0:n], ALU.subtract).then_inc(
                                         S("w_split"), 1)
                done[0] = max(done[0], upto)

            def split_rest(name, g0, a0=0, hi=a_hi, lo=a_lo, k_from=0, k_to=None):
                k0, kn = SPLIT0[name], SPLIT_K[name]
                for k in range(k_from, kn if k_to is None else k_to):
                    b, i = (k0 + k) // 2, k % 2
                    ve.wait_ge(S("split_hi"), k0 + k - i + 2)
                    ve.scalar_tensor_tensor(
                        out=lo[:, a0 + k, :], in0=ps[4 + b % 4][:, i * SEQ:(i + 1) * SEQ],
                        scalar=1.0 if g0 is None else g_t[:, g0 + k:g0 + k + 1],
                        in1=hi[:, a0 + k, :], op0=ALU.mult, op1=ALU.subtract).then_inc(
                            S("split_lo"), 1)

            def rests_and_units(name, g0, unit, lag=3):
                for kk in range(SPLIT_K[name] // 2):
                    split_rest(name, g0, k_from=2 * kk, k_to=2 * kk + 2)
                    split_w(unit + RING + kk - lag)

            def copy_turned(c):
                dst = None if c == KV_LAT else turned_dst(c)
                for b in range(1 if c == KV_LAT else 2):
                    m = bank0[c] + b
                    ve.wait_ge(S("turned"), m + 1)
                    if c == KV_LAT:
                        ve.tensor_copy(kpe_t[:, :], ps[4 + m % 4][:, 0:SEQ]).then_inc(
                            S("turn_copied"), 1)
                    else:
                        ve.tensor_copy(dst[:, 2 * b:2 * b + 2, :].rearrange("p h t -> p (h t)"),
                                       ps[4 + m % 4][:, :]).then_inc(S("turn_copied"), 1)

            def rope(dst1, dst2, x1, x2, heads):
                c = rope_cs[:, 0]
                s = rope_cs[:, 1]
                for t in range(TT):
                    cb = c[:, t:t + 1, :].to_broadcast([P, heads, ROPE // 2])
                    sb = s[:, t:t + 1, :].to_broadcast([P, heads, ROPE // 2])
                    n = heads * ROPE // 2
                    a = rt_a[:, 0, 0:n].rearrange("p (h c) -> p h c", h=heads)
                    b = rt_a[:, 1, 0:n].rearrange("p (h c) -> p h c", h=heads)
                    d = rt_a[:, 2, 0:n].rearrange("p (h c) -> p h c", h=heads)
                    e = rt_a[:, 3, 0:n].rearrange("p (h c) -> p h c", h=heads)
                    ve.tensor_tensor(a, x1(t), cb, ALU.mult)
                    ve.tensor_tensor(b, x2(t), sb, ALU.mult)
                    ve.tensor_tensor(d, x2(t), cb, ALU.mult)
                    link(ve.tensor_tensor(e, x1(t), sb, ALU.mult))
                    ve.tensor_tensor(dst1(t), a, b, ALU.subtract)
                    link(ve.tensor_tensor(dst2(t), d, e, ALU.add))

            rt_a = place("rope_tmp", [P, 4, 256], offset=e_at + 80 * 1024)

            from math import pi
            import numpy as np
            half = ROPE // 2
            inv = small[:, 0:half]
            pf = small[:, 32:34]
            ve.wait_ge(S("inv_freq"), 1)
            ve.wait_ge(S("pos_loaded"), 16 * TT)
            link(ve.tensor_copy(pf, pos_i[:, :]))
            turns = place("rope_turns", [P, TT, ROPE // 2], offset=e_at + 84 * 1024)
            for t in range(TT):
                ins = ve.tensor_scalar(rope_cs[:, 1, t, :], inv, pf[:, t:t + 1], None, ALU.mult)
            link(ins)
            magic = 1.5 * 2.0 ** 23
            c1 = 6.28125
            c2 = float(np.float32(2 * pi - c1))
            c3 = 2 * pi - c1 - c2
            ang, cosv = rope_cs[:, 1], rope_cs[:, 0]
            link(ve.tensor_scalar(turns[:, :, :], ang, 1.0 / (2 * pi), magic, ALU.mult, ALU.add))
            link(ve.tensor_scalar(turns[:, :, :], turns[:, :, :], -magic, None, ALU.add))
            for cc in (c1, c2, c3):
                link(ve.scalar_tensor_tensor(out=ang, in0=turns[:, :, :], scalar=-cc, in1=ang,
                                             op0=ALU.mult, op1=ALU.add))
            link(ve.tensor_scalar(cosv, ang, pi / 2, None, ALU.add))
            link(ve.tensor_scalar(turns[:, :, :], cosv, pi, -2 * pi, ALU.is_gt, ALU.mult))
            link(ve.tensor_tensor(cosv, cosv, turns[:, :, :], ALU.add))
            ve.tensor_scalar(rope_cs[:, :, :, :], rope_cs[:, :, :, :], 3.1415925, -3.1415925, ALU.min,
                             ALU.max).then_inc(S("angles"), 1)
            ve.wait_ge(S("gains_copied"), 1)
            rests_and_units("mix", 0, 0)
            for c in range(Q_LAT, Q_PE):
                split_w(UNIT0[c + 1] + RING)
                if SB_Q <= c - 1 < SB_V:
                    copy_turned(c - 1)
                    if c - 1 == SB_K + 1:
                        j = TURNED.index(KV_LAT)
                        ve.wait_ge(S("rope_ready"), 1)
                        ve.wait_ge(S("turned"), bank0[SB_K + 1])
                        ve.wait_ge(*chunk_out(KV_LAT))
                        kn = nat[:, j % 2]
                        rope(lambda t: kn[:, t:t + 1, 0:half], lambda t: kn[:, t:t + 1, half:ROPE],
                             lambda t: c_kv[:, t:t + 1, KV_RANK:KV_RANK + half],
                             lambda t: c_kv[:, t:t + 1, KV_RANK + half:KV_RANK + ROPE], 1)
                        ve.tensor_copy(kn[:, :, ROPE:2 * ROPE], kn[:, :, 0:ROPE]).then_inc(
                            S("roped"), 1)
            copy_turned(KV_LAT)
            split_rest("q", 48)
            split_rest("kv", 52, a0=4)
            for c in range(Q_PE, MEM_K):
                if c == Q_NOPE:
                    j = TURNED.index(Q_PE)
                    ve.wait_ge(*chunk_out(Q_PE))
                    qn = nat[:, j % 2].rearrange("p t (h c) -> p t h c", c=ROPE)
                    rope(lambda t: qn[:, t, :, 0:half], lambda t: qn[:, t, :, half:ROPE],
                         lambda t: qn[:, t, :, 0:half], lambda t: qn[:, t, :, half:ROPE], HEADS)
                    ve.tensor_copy(small[:, 62:63], small[:, 33:34]).then_inc(S("roped"), 1)
                split_w(UNIT0[c + 1] + RING - (c == Q_PE))
                if c - 1 in TURNED:
                    copy_turned(c - 1)

            ve.wait_ge(S("w_used"), UNIT0[MEM_K])
            for i in range(HEADS + 1):
                if i >= 1:
                    split_w(min(UNIT0[MEM_K] + 2 * i, UNIT0[W_OUT]) + RING)
                    h = i - 1
                    ve.wait_ge(S("sb_later"), h + 1)
                    ve.tensor_tensor(sb_b[:, h % 2], ps[5][:, 0:BLK], sb_b[:, h % 2],
                                     ALU.add).then_inc(S("sb_summed"), 1)
                if i < HEADS:
                    h = i
                    ve.wait_ge(S("mla_scored"), h + 1)
                    if h >= 2:
                        ve.wait_ge(S("probs_turned"), h - 1)
                    ve.scalar_tensor_tensor(out=p_mla[:, h % 2], in0=ps[0][:, 0:BLK], scalar=SC_MLA,
                                            in1=mla_mask[:, :], op0=ALU.mult, op1=ALU.add).then_inc(
                                                S("mla_masked"), 1)
                    ve.wait_ge(S("mla_masked"), h + 1)
                    ve.tensor_reduce(row_m[:, h, 0:1], p_mla[:, h % 2, 0:P], AX, ALU.max)
                    link(ve.tensor_reduce(row_m[:, h, 1:2], p_mla[:, h % 2, P:BLK], AX, ALU.max))
                    ve.tensor_scalar(row_n[:, h, :], row_m[:, h, :], -1.0, None, ALU.mult).then_inc(
                        S("mla_max"), 1)
                    if h == 0:
                        split_rest("mem", 16, k_to=KD // 2)
                    ve.wait_ge(S("sb_log1p"), h + 1)
                    if h >= 2:
                        ve.wait_ge(S("sb_weights"), h - 1)
                    link(ve.tensor_scalar(sb_b[:, h % 2], ps[1][:, 0:BLK], SC_SB, 0.0, ALU.mult,
                                          ALU.min))
                    link(ve.tensor_tensor(sb_b[:, h % 2], sb_b[:, h % 2], sb_l[:, :],
                                          ALU.subtract))
                    if h >= 1:
                        ve.wait_ge(S("sb_later"), h)
                    ve.scalar_tensor_tensor(out=sb_m[:, :], in0=ps[1][:, 0:BLK],
                                            scalar=-SC_SB, in1=sb_b[:, h % 2], op0=ALU.mult,
                                            op1=ALU.add).then_inc(S("sb_logs"), 1)
                    if h == 0:
                        split_rest("mem", 16, k_from=KD // 2)
                        split_w(UNIT0[MEM_K] + RING)
                if i >= 1:
                    h = i - 1
                    ve.wait_ge(S("o_made"), h + 1)
                    link(ve.reciprocal(row_r[:, h, :], row_s[:, h, :]))
                    o = ps[6]
                    for t in range(TT):
                        ve.tensor_scalar(o_cat[:, t, h * HD:(h + 1) * HD], o[:, t * P:(t + 1) * P],
                                         row_r[:, h, t:t + 1], None, ALU.mult)
                    ve.tensor_copy(o_cat[:, :, (HEADS + h) * HD:(HEADS + h + 1) * HD],
                                   o[:, 2 * P:4 * P].rearrange("p (t d) -> p t d", t=TT)).then_inc(
                                       S("o_copied"), 1)
            rests_and_units("out", 54, UNIT0[W_OUT])
            ve.wait_ge(S("head_squared"), 4 * HEADS)
            for g, col in enumerate((SS_A, SS_B)):
                ins = ve.tensor_reduce(sums[:, col:col + TT].rearrange("p (t a) -> p t a", a=1),
                                       head_ss[:, :, g, :], AX, ALU.add)
            ins.then_inc(S("sums_made"), 1)

            def add_chunk(c, n0):
                ve.wait_ge(S("w_used"), UNIT0[c + 1])
                for t in range(TT):
                    xs = x_res[:, t, n0:n0 + UN]
                    ins = ve.tensor_tensor(xs, ps[acc_bank(c) + t][:, :], xs, ALU.add)
                ins.then_inc(S("chunk_added"), 1)

            def add_heads(c):
                q, g = divmod(c - W_OUT, 2)
                col = (SS_A, SS_B)[g]
                ve.wait_ge(S("w_used"), UNIT0[c + 1])
                for t in range(TT):
                    xs = x_res[:, t, q * UN:(q + 1) * UN]
                    if g:
                        ve.wait_ge(S("half_added"), 2 * q + t + 1)
                    ins = ve.scalar_tensor_tensor(out=xs, in0=ps[acc_bank(c) + t][:, :],
                                                  scalar=rstd[:, col + t:col + t + 1], in1=xs,
                                                  op0=ALU.mult, op1=ALU.add)
                    if g == 0:
                        ins.then_inc(S("half_added"), 1)
                if g == 0:
                    ve.wait_ge(S("half_added"), 2 * q + 2)
                    ve.sem_inc(S("chunk_added"), 1)
                else:
                    ins.then_inc(S("chunk_added"), 1)

            def x_sums(col, squares_):
                ve.wait_ge(S("x_squared"), squares_)
                ve.tensor_reduce(sums[:, col:col + TT].rearrange("p (t a) -> p t a", a=1),
                                 chunk_ss[:, :, :], AX, ALU.add).then_inc(S("sums_made"), 1)

            def memx_rests(q):
                split_rest("memx", 32, hi=a2_hi, lo=a2_lo, k_from=4 * q, k_to=4 * q + 4)

            ve.wait_ge(S("rstd"), 5)
            for c in range(W_OUT, MEM_Q):
                split_w(UNIT0[c + 1] + RING)
                add_heads(c)
                if c > W_OUT and (c - W_OUT) % 2 == 0:
                    memx_rests((c - W_OUT) // 2 - 1)
            memx_rests(3)
            split_w(UNIT0[MEM_Q + 1] + RING - 2)
            x_sums(SS_X1, 4 * TT)
            split_w(UNIT0[MEM_Q + 1] + RING)
            copy_turned(MEM_K)
            copy_turned(MEM_Q)
            for i in range(MEM_HEADS):
                ve.wait_ge(S("mem_scores"), i + 1)
                link(ve.tensor_reduce(mrow[:, 0, i, :], ps[i][:, :].rearrange(
                    "p (t m) -> p t m", t=TT), AX, ALU.max))
                ve.tensor_scalar(mrow[:, 1, i, :], mrow[:, 0, i, :], -SC_SB, None, ALU.mult).then_inc(
                    S("mem_max"), 1)
            ve.wait_ge(S("mem_probs"), MEM_HEADS)
            link(ve.reciprocal(mrow[:, 3], mrow[:, 2]))
            ve.wait_ge(S("mem_o"), MEM_HEADS)
            for t in range(TT):
                ve.tensor_tensor(o_mem[:, t, :].rearrange("p (h d) -> p h d", h=MEM_HEADS),
                                 ps[5 + t][:, :].rearrange("p (h d) -> p h d", h=MEM_HEADS),
                                 mrow[:, 3, :, t:t + 1].to_broadcast([P, MEM_HEADS, HD]),
                                 ALU.mult).then_inc(S("mem_o_copied"), 1)
            split_rest("memo", None, lo=memo_lo)
            def router_copy(q):
                for i in range(2 if q == 3 else 4):
                    ve.wait_ge(S("h_turned"), 2 * q + i // 2 + 1)
                    if q >= 2:
                        ve.wait_ge(S("logits"), q - 1)
                    ve.tensor_scalar(h_t[:, q % 2, i, :],
                                     ps[4 + i // 2][:, i % 2 * SEQ:(i % 2 + 1) * SEQ],
                                     g_t[:, 70 + 4 * q + i:71 + 4 * q + i], None,
                                     ALU.mult).then_inc(S("h_copied"), 1)

            for q in range(4):
                if q >= 1:
                    router_copy(q - 1)
                add_chunk(MEM_O + q, q * UN)
                split_w(UNIT0[MEM_O + q + 1] + RING)
            router_copy(3)
            x_sums(SS_X2, 8 * TT)

            def field(a, *dims):
                n = 1
                for d in dims:
                    n *= d
                v = rt[:, a:a + n]
                names = "abcd"[:len(dims)]
                if len(dims) > 1:
                    v = v.rearrange(f"p ({' '.join(names)}) -> p {' '.join(names)}",
                                    **{m: d for m, d in zip(names, dims)})
                return v

            def bc(v, *shape):
                return v.to_broadcast([P, *shape])

            lg = field(32, TT, 36)
            gl, el = lg[:, :, 0:GROUPS], lg[:, :, GROUPS:36]
            gm = field(104, TT, 1)
            gsum = field(106, TT, 1)
            gx, gexp = field(0, TT, GROUPS), field(8, TT, GROUPS)
            gap, r2 = field(16, TT), field(18, TT)
            ghot = field(112, TT, GROUPS)
            first_of = field(120, TT, GROUPS)
            best = field(128, TT, 1)
            prod = field(160, TT, GROUPS, PER_GROUP)
            cand = field(224, TT, PER_GROUP)
            m1, m2 = field(240, TT, 1), field(242, TT, 1)
            e1 = field(248, TT, PER_GROUP)
            hot1 = field(264, TT, PER_GROUP)
            hot2 = field(280, TT, PER_GROUP)
            den = field(296, TT)
            pick1 = field(320, TT, GROUPS, PER_GROUP)
            pick2 = field(384, TT, GROUPS, PER_GROUP)
            sel = field(512, TT, EXPERTS)
            row = field(576, TT, EXPERTS)
            tmpr = field(32, 2, TT, EXPERTS)
            base_row = field(640, TT, EXPERTS)
            cnt = field(704, 8)
            picks = field(320, 2, TT, EXPERTS)
            falling = field(720, PER_GROUP)
            row0 = field(736, EXPERTS)

            ve.wait_ge(S("rstd"), 7)
            ve.wait_ge(S("logits"), 4)
            ve.wait_ge(S("router_consts"), 2)
            for t in range(TT):
                ins = ve.scalar_tensor_tensor(out=lg[:, t, :], in0=ps[6 + t][:, 0:36],
                                              scalar=rstd[:, SS_X2 + t:SS_X2 + t + 1],
                                              in1=b_r[:, :], op0=ALU.mult, op1=ALU.add)
            link(ins)
            link(ve.tensor_reduce(gm, gl, AX, ALU.max))
            ve.tensor_tensor(gx, gl, bc(gm, TT, GROUPS), ALU.subtract).then_inc(S("logits_ready"), 1)

            def first_hot(dst, values, top, scratch_, n):
                link(ve.tensor_tensor(scratch_, values, bc(top, TT, n), ALU.is_equal))
                f = falling[:, 0:n].rearrange("p (a b) -> p a b", a=1)
                fb = bc(f, TT, n)
                link(ve.tensor_tensor(scratch_, scratch_, fb, ALU.mult))
                link(ve.tensor_reduce(best, scratch_, AX, ALU.max))
                link(ve.tensor_tensor(dst, fb, bc(best, TT, n), ALU.is_equal))

            first_hot(ghot, gl, gm, first_of, GROUPS)
            gh4 = ghot.rearrange("p t (g e) -> p t g e", e=1)
            for t in range(TT):
                ins = ve.tensor_tensor(prod[:, t], el[:, t].rearrange("p (g e) -> p g e", g=GROUPS),
                                       bc(gh4[:, t], GROUPS, PER_GROUP), ALU.mult)
            link(ins)
            link(ve.tensor_reduce(cand, prod.rearrange("p t g e -> p t e g"), AX, ALU.add))
            link(ve.tensor_reduce(m1, cand, AX, ALU.max))
            first_hot(hot1, cand, m1, e1, PER_GROUP)
            link(ve.scalar_tensor_tensor(out=cand, in0=hot1, scalar=-3.0e38, in1=cand, op0=ALU.mult,
                                         op1=ALU.add))
            link(ve.tensor_reduce(m2, cand, AX, ALU.max))
            ve.tensor_tensor(gap.rearrange("p (t a) -> p t a", a=1), m2, m1, ALU.subtract).then_inc(
                S("second_gap"), 1)
            first_hot(hot2, cand, m2, e1, PER_GROUP)
            for t in range(TT):
                for hot_n, pick in ((hot1, pick1), (hot2, pick2)):
                    hb = hot_n[:, t:t + 1, :]
                    ins = ve.tensor_tensor(pick[:, t], bc(hb, GROUPS, PER_GROUP),
                                           bc(gh4[:, t], GROUPS, PER_GROUP), ALU.mult)
            link(ins)
            p1 = pick1.rearrange("p t g e -> p t (g e)")
            p2 = pick2.rearrange("p t g e -> p t (g e)")
            ve.tensor_tensor(sel, p1, p2, ALU.add).then_inc(S("chosen"), 1)
            ve.wait_ge(S("group_exp"), 1)
            ve.wait_ge(S("second_exp"), 1)
            link(ve.tensor_reduce(gsum, gexp, AX, ALU.add))
            link(ve.tensor_scalar(den, r2, 1.0, None, ALU.add))
            link(ve.tensor_tensor(den, den, gsum.rearrange("p t a -> p (t a)"), ALU.mult))
            link(ve.reciprocal(gate_w[:, 0, :], den))
            link(ve.tensor_tensor(gate_w[:, 1, :], gate_w[:, 0, :], r2, ALU.mult))
            ve.wait_ge(S("ranked"), 1)
            rank = ps[2][:, 0:TT * EXPERTS].rearrange("p (t e) -> p t e", t=TT)
            r0 = row0.rearrange("p (a e) -> p a e", a=1)
            ve.tensor_tensor(base_row, rank, bc(r0, TT, EXPERTS), ALU.add)
            link(ve.tensor_scalar(row, rank, -(SLOTS - 1) / 2.0, 1.0 / SLOTS, ALU.add, ALU.mult))
            link(ve.tensor_scalar(row, row, magic, -magic, ALU.add, ALU.add))
            link(ve.scalar_tensor_tensor(out=row, in0=row, scalar=float(SLOTS * EXPERTS - SLOTS),
                                         in1=base_row, op0=ALU.mult, op1=ALU.add))
            flat = row.rearrange("p t e -> p (t e)").rearrange("p (a n) -> p a n", a=1)
            link(ve.tensor_tensor(tmpr.rearrange("p i t e -> p i (t e)"),
                                  picks.rearrange("p i t e -> p i (t e)"),
                                  bc(flat, 2, TT * EXPERTS), ALU.mult))
            link(ve.tensor_reduce(rel[:, :, :].rearrange("p i t -> p (i t)").rearrange(
                "p (i a) -> p i a", a=1), tmpr.rearrange("p i t e -> p (i t) e"), AX, ALU.add))

            def pick_hot(n):
                it = iota32[:, :].rearrange("p (a s) -> p a s", a=1)
                rb = rel[:, :, :].rearrange("p i t -> p (i t)").rearrange("p (i a) -> p i a", a=1)
                ve.tensor_tensor(hot_f[:, :, :, :].rearrange("p i t s -> p (i t) s"),
                                 bc(it, 2 * TT, SLOTS), bc(rb, 2 * TT, SLOTS),
                                 ALU.is_equal).then_inc(S("pick_hot"), 1)
                ve.wait_ge(S("pick_hot"), n + 1)
                ve.tensor_tensor(hot[:, :, :], hot_f[:, 0], hot_f[:, 1], ALU.add).then_inc(
                    S("hot_ready"), 1)

            def gained(n):
                ve.wait_ge(S("slots_turned"), n + 1)
                for g in range(NJ):
                    gb = g_ffn[:, 4 * g:4 * g + 4].rearrange("p (k a) -> p k a", a=1)
                    bank = ps[4][:, :].rearrange("p (j g s) -> p j g s", j=4, g=NJ)
                    ins = ve.tensor_tensor(xe[:, 4 * g:4 * g + 4, :], bank[:, :, g, :],
                                           bc(gb, 4, SLOTS), ALU.mult)
                ins.then_inc(S("xe_ready"), 1)

            def add_y(m, t):
                ve.wait_ge(S("combined"), TT * m + t + 1)
                for g in range(NJ):
                    xs = x_res[:, t, g * UN:(g + 1) * UN]
                    ins = ve.tensor_tensor(xs, ps[g][:, :], xs, ALU.add)
                ins.then_inc(S("y_added"), 1)

            def expert(n, m=None):
                if m is not None:
                    ve.wait_ge(S("bank6_turned"), n)
                for t in range(TT):
                    ve.tensor_scalar(comb_0[:, t, :], hot_f[:, 0, t, :], gate_w[:, 0, t:t + 1], None,
                                     ALU.mult).then_inc(S("comb_half"), 1)
                ve.wait_ge(S("comb_half"), TT * (n + 1))
                for t in range(TT):
                    ve.scalar_tensor_tensor(
                        out=comb[:, t], in0=bc(hot_f[:, 1, t:t + 1, :], NJ, SLOTS),
                        scalar=gate_w[:, 1, t:t + 1], in1=bc(comb_0[:, t:t + 1, :], NJ, SLOTS),
                        op0=ALU.mult, op1=ALU.add).then_inc(S("comb_ready"), 1)
                ve.wait_ge(S("gathered"), n + 1)
                ve.wait_ge(S("comb_ready"), TT * (n + 1))
                ve.tensor_scalar(rel[:, :, :], rel[:, :, :], -float(SLOTS), None,
                                 ALU.add).then_inc(S("rel_moved"), 1)
                ve.wait_ge(S("rel_moved"), n + 1)
                pick_hot(n + 1)
                if m is not None:
                    for t in range(TT):
                        add_y(m, t)
                ve.wait_ge(S("silu"), n + 1)
                if m is not None:
                    ve.wait_ge(S("bank6_turned"), n)
                ve.tensor_tensor(act[:, :], sg[:, :], ps[5][:, P:2 * P], ALU.mult).then_inc(
                    S("act_ready"), 1)
                ve.wait_ge(S("gu_used1"), n + 1)
                gained(n + 1)

            pick_hot(0)
            link(ve.tensor_reduce(cnt[:, 0:1], ps[3][:, 0:EXPERTS], AX, ALU.max))
            link(ve.tensor_scalar(cnt[:, 0:1], cnt[:, 0:1], (SLOTS - 1) / 2.0, 1.0 / SLOTS, ALU.add,
                                  ALU.mult))
            link(ve.tensor_scalar(cnt[:, 0:1], cnt[:, 0:1], magic, -magic, ALU.add, ALU.add))
            link(ve.tensor_scalar(cnt[:, 0:1], cnt[:, 0:1], float(EXPERTS), None, ALU.mult))
            ve.tensor_scalar(cnt[:, 1:2], cnt[:, 0:1], -1.0, None, ALU.add)
            link(ve.tensor_scalar(cnt[:, 2:3], cnt[:, 0:1], 0.5, -1.0, ALU.mult, ALU.add))
            ve.tensor_copy(n_iter[:, :], cnt[:, 0:3]).then_inc(S("routed"), 1)
            gained(0)
            ve.wait_ge(S("routed"), 1)
            last = ve.value_load(n_iter[0:1, 1:2], min_val=EXPERTS - 1,
                                 max_val=MAX_PASSES * EXPERTS - 1)
            expert(0)
            with ve.Fori(0, last) as m:
                expert(m + 1, m)
            def last_add(t, g):
                ve.wait_ge(S("last_combined"), NJ * t + g + 1)
                xs = x_res[:, t, g * UN:(g + 1) * UN]
                ve.tensor_tensor(xs, ps[g][:, :], xs, ALU.add).then_inc(S("last_added"), 1)

            def last_sum(t):
                ve.wait_ge(S("final_squared"), NJ * (t + 1))
                ve.tensor_reduce(sums[:, t:t + 1], chunk_ss[:, t, :], AX, ALU.add).then_inc(
                    S("final_summed"), 1)

            def final(t, f):
                ve.wait_ge(S("final_rstd"), t + 1)
                cols = slice(f * D // 2, (f + 1) * D // 2)
                ve.scalar_tensor_tensor(out=x_res[:, t, cols], in0=x_res[:, t, cols],
                                        scalar=rstd[:, t:t + 1], in1=g_fin[:, cols], op0=ALU.mult,
                                        op1=ALU.mult).then_inc(S("final"), 1)

            for g in range(NJ):
                last_add(0, g)
            last_add(1, 0)
            last_add(1, 1)
            last_sum(0)
            last_add(1, 2)
            ve.wait_ge(S("final_gain_loaded"), 16)
            final(0, 0)
            last_add(1, 3)
            final(0, 1)
            last_sum(1)
            final(1, 0)
            final(1, 1)

        @block.gpsimd
        def _(gp):
            steps = [0]

            def link(ins):
                steps[0] += 1
                ins.then_inc(S("gp_step"), 1)
                gp.wait_ge(S("gp_step"), steps[0])

            half = ROPE // 2
            for i in range(half):
                ins = gp.memset(small[:, i:i + 1], float(10000.0 ** (-2.0 * i / ROPE)))
            ins.then_inc(S("inv_freq"), 1)
            gp.memset(ident[:, :], 0.0)
            gp.memset(ones[:, :], 1.0)
            gp.memset(sb_mask[:, :], 1.0)
            link(gp.memset(mla_mask[:, :], 0.0))
            gp.affine_select(out=ident[:, :], in_=ident[:, :], compare_op=ALU.not_equal, fill=1.0, base=0,
                             pattern=[[-1, P]], channel_multiplier=1)
            gp.affine_select(out=above[:, :], in_=ones[:, :], compare_op=ALU.is_gt, fill=0.0, base=0,
                             pattern=[[-1, P]], channel_multiplier=1)
            for lo in (0, SEQ):
                gp.affine_select(out=sb_mask[:, lo:lo + P], in_=sb_mask[:, lo:lo + P],
                                 compare_op=ALU.is_gt, fill=0.0, base=0, pattern=[[1, P]],
                                 channel_multiplier=-1)
                gp.affine_select(out=mla_mask[:, lo:lo + P], in_=mla_mask[:, lo:lo + P],
                                 compare_op=ALU.is_ge, fill=-1.0e30, base=0, pattern=[[-1, P]],
                                 channel_multiplier=1)
            link(gp.iota(iota32[:, :], [[1, SLOTS]], base=0, channel_multiplier=0,
                         allow_small_or_imprecise_dtypes=True))
            gp.sem_inc(S("consts"), 1)
            gp.memset(minus_half[:, :], -0.5)

            def norms(cols, width, made, count):
                gp.wait_ge(S(made), count)
                for col in cols:
                    r = rstd[:, col:col + TT]
                    link(gp.tensor_scalar(r, sums[:, col:col + TT], 1.0 / width, EPS, ALU.mult, ALU.add))
                    ins = gp.tensor_tensor(r, r, minus_half[:, :], ALU.pow)
                ins.then_inc(S("rstd"), 1)

            norms([SS_X], D, "squared", TT)
            norms([SS_Q], Q_RANK, "squared", 2 * TT)
            norms([SS_KV], KV_RANK, "squared", 3 * TT)
            norms([SS_MEM], D, "squared", 4 * TT)
            for i in range(HEADS + 1):
                if i >= 1:
                    h = i - 1
                    gp.wait_ge(S("sb_exp"), h + 1)
                    if h >= 1:
                        gp.wait_ge(S("o_made"), h)
                    gp.tensor_tensor(sb_a[:, :], sb_b[:, h % 2], sb_mask[:, :], ALU.mult).then_inc(
                        S("sb_weights"), 1)
                if i < HEADS:
                    gp.wait_ge(S("sb_logs"), i + 1)
                    gp.tensor_tensor(sb_m[:, :], sb_m[:, :], sb_mask[:, :], ALU.mult).then_inc(
                        S("sb_masked"), 1)
            norms([SS_A, SS_B], HEADS * HD, "sums_made", 1)
            norms([SS_X1], D, "sums_made", 2)
            gp.wait_ge(S("turned"), bank0[MEM_Q] + 2)
            gp.dma_start(w_r[:, :, 0:GROUPS], w_group[0].rearrange("(k p) g -> p k g", p=P)).then_inc(
                S("router_loaded"), 16)
            gp.dma_start(w_r[:, :, GROUPS:36], w_expert_router[0].rearrange("(k p) g -> p k g", p=P)
                         ).then_inc(S("router_loaded"), 16)
            gp.dma_start(b_r[:, 0:GROUPS], b_group[0:1, :].to_broadcast([P, GROUPS])).then_inc(
                S("router_loaded"), 16)
            gp.dma_start(b_r[:, GROUPS:36], b_expert[0:1, :].to_broadcast([P, EXPERTS])).then_inc(
                S("router_loaded"), 16)
            gp.iota(rt[:, 720:720 + PER_GROUP], [[-1, PER_GROUP]], base=PER_GROUP, channel_multiplier=0,
                    allow_small_or_imprecise_dtypes=True).then_inc(S("router_consts"), 1)
            gp.iota(rt[:, 736:736 + EXPERTS], [[SLOTS, EXPERTS]], base=0, channel_multiplier=0,
                    allow_small_or_imprecise_dtypes=True).then_inc(S("router_consts"), 1)
            norms([SS_X2], D, "sums_made", 3)
            gp.wait_ge(S("rstd"), 7)
            for t in range(TT):
                gp.wait_ge(S("final_summed"), t + 1)
                link(gp.tensor_scalar(rstd[:, t:t + 1], sums[:, t:t + 1], 1.0 / D, EPS, ALU.mult,
                                      ALU.add))
                gp.tensor_tensor(rstd[:, t:t + 1], rstd[:, t:t + 1], minus_half[:, 0:1],
                                 ALU.pow).then_inc(S("final_rstd"), 1)


_INS = ["x", "mem", "positions", "norm_mix", "w_in", "norm_q_lat", "w_q_b", "norm_kv_lat", "w_kv_b",
        "norm_mla_out", "norm_sb_out", "w_out", "norm_mem_x", "norm_mem_src", "w_mem_q", "w_mem_kv",
        "w_mem_o", "norm_ffn", "w_group", "b_group", "w_expert_router", "b_expert", "w_gate", "w_up",
        "w_down", "norm_final"]


def kernel(**inputs):
    import numpy as _np
    import concourse.bacc as _bacc
    from concourse import mybir as _mybir
    from concourse.bass_utils import run_bass_kernel_spmd as _run

    nc = _bacc.Bacc("TRN2", target_bir_lowering=False, num_devices=1)
    arrays, args = {}, []
    for name in _INS:
        a = _np.ascontiguousarray(inputs[name])
        arrays[f"in_{name}"] = a
        args.append(nc.dram_tensor(f"in_{name}", a.shape, _mybir.dt.from_np(a.dtype),
                                   kind="ExternalInput").ap())
    args.append(nc.dram_tensor("out_0", (1, SEQ, D), F32, kind="ExternalOutput").ap())
    layer(nc, *args)
    r = _run(nc, [arrays], core_ids=[0])
    return r.results[0]["out_0"]
```
